# Optimizing a Trainium2 kernel written in Bass

```python
import math
import jax, jax.numpy as jnp
from jax import lax
import numpy as np

D_MODEL = 1024
BATCH = 1
SEQ = 256
DEPTH = 1

MEM_LEN = 256
DIFF_HEADS = 4
DIFF_HEAD_DIM = 64
DIFF_WIDTH = DIFF_HEADS * 2 * DIFF_HEAD_DIM
MOBA_HEADS = 8
MOBA_HEAD_DIM = 64
MOBA_WIDTH = MOBA_HEADS * MOBA_HEAD_DIM
MIX_WIDTH = DIFF_WIDTH + MOBA_WIDTH
MOBA_BLOCK = 256
MOBA_TOPK = 3
Q_BLOCK = 128
ROPE_THETA = 500000.0
ROT_DIM = 64 // 4
MEM_HEADS = 4
MEM_HEAD_DIM = D_MODEL // MEM_HEADS
N_EXPERTS = 32
TOP_K = 4
D_FF = D_MODEL
SWIGLU_ALPHA = 1.702
SWIGLU_LIMIT = 7.0
LN_EPS = 1e-5
RMS_EPS = 1e-5
DEEPNORM_ALPHA = (2.0 * DEPTH) ** 0.25
DEEPNORM_BETA = (8.0 * DEPTH) ** -0.25

kernel_name = "hybrid_diffattn_moba_memxattn_moe_deepnorm"

def layer_norm(x, g, b):
    xf = x.astype(jnp.float32)
    mu = jnp.mean(xf, axis=-1, keepdims=True)
    var = jnp.mean(jnp.square(xf - mu), axis=-1, keepdims=True)
    return ((xf - mu) * lax.rsqrt(var + LN_EPS) * g + b).astype(x.dtype)

def rms_norm(x, g):
    xf = x.astype(jnp.float32)
    return (xf * lax.rsqrt(jnp.mean(xf * xf, axis=-1, keepdims=True) + RMS_EPS) * g).astype(x.dtype)

def rope_tables(seq):
    inv_freq = ROPE_THETA ** (-jnp.arange(0, ROT_DIM, 2, dtype=jnp.float32) / ROT_DIM)
    ang = jnp.arange(seq, dtype=jnp.float32)[:, None] * inv_freq[None, :]
    return jnp.cos(ang), jnp.sin(ang)

def apply_partial_rope(x, cos, sin):
    half = cos.shape[-1]
    bshape = (cos.shape[0],) + (1,) * (x.ndim - 3) + (half,)
    c = cos.reshape(bshape).astype(x.dtype)
    s = sin.reshape(bshape).astype(x.dtype)
    x1, x2, rest = x[..., :half], x[..., half:2 * half], x[..., 2 * half:]
    return jnp.concatenate([x1 * c - x2 * s, x2 * c + x1 * s, rest], axis=-1)

def differential_attention(q, k, v, lam, lambda_init, subln_g):
    B, S = q.shape[0], q.shape[1]
    nqb = S // Q_BLOCK
    scale = DIFF_HEAD_DIM ** -0.5
    q_blocks = q.reshape(B, nqb, Q_BLOCK, DIFF_HEADS, 2, DIFF_HEAD_DIM).swapaxes(0, 1)
    kpos = jnp.arange(S)

    def one_block(args):
        qi, i = args
        qpos = i * Q_BLOCK + jnp.arange(Q_BLOCK)
        s = jnp.einsum('bqhcd,bkhcd->bhcqk', qi, k).astype(jnp.float32) * scale
        s = jnp.where(kpos[None, :] <= qpos[:, None], s, -jnp.inf)
        p = jax.nn.softmax(s, axis=-1)
        a = p[:, :, 0] - lam * p[:, :, 1]
        return jnp.einsum('bhqk,bkhe->bqhe', a.astype(v.dtype), v)

    o = lax.map(one_block, (q_blocks, jnp.arange(nqb)))
    o = o.swapaxes(0, 1).reshape(B, S, DIFF_HEADS, 2 * DIFF_HEAD_DIM)
    o = rms_norm(o, subln_g) * (1.0 - lambda_init)
    return o.reshape(B, S, DIFF_WIDTH)

def moba_attention(q, k, v):
    B, S, H, d = q.shape
    scale = d ** -0.5
    s_pad = -(-S // MOBA_BLOCK) * MOBA_BLOCK
    nb = s_pad // MOBA_BLOCK
    n_sel = min(MOBA_TOPK, nb)
    pad = ((0, 0), (0, s_pad - S), (0, 0), (0, 0))
    kb = jnp.pad(k, pad).reshape(B, nb, MOBA_BLOCK, H, d).transpose(0, 3, 1, 2, 4)
    vb = jnp.pad(v, pad).reshape(B, nb, MOBA_BLOCK, H, d).transpose(0, 3, 1, 2, 4)
    k_mean = jnp.mean(kb.astype(jnp.float32), axis=3)
    qh = q.transpose(0, 2, 1, 3)
    gate = jnp.einsum('bhsd,bhnd->bhsn', qh.astype(jnp.float32), k_mean)
    fully_past = jnp.arange(nb)[None, :] < (jnp.arange(S) // MOBA_BLOCK)[:, None]
    gate = jnp.where(fully_past, gate, -jnp.inf)
    _, sel = lax.top_k(gate, n_sel)
    n_chunks = S // Q_BLOCK

    def per_batch(args):
        q_b, kb_b, vb_b, sel_b = args

        def per_chunk(c):
            q0 = c * Q_BLOCK
            qc = lax.dynamic_slice_in_dim(q_b, q0, Q_BLOCK, axis=1)
            sc = lax.dynamic_slice_in_dim(sel_b, q0, Q_BLOCK, axis=1)
            qpos = q0 + jnp.arange(Q_BLOCK)
            own_blk = q0 // MOBA_BLOCK
            k_sel = jax.vmap(lambda kbh, sh: kbh[sh])(kb_b, sc)
            v_sel = jax.vmap(lambda vbh, sh: vbh[sh])(vb_b, sc)
            s_sel = jnp.einsum('hqd,hqnld->hqnl', qc, k_sel).astype(jnp.float32) * scale
            slot_valid = jnp.arange(n_sel) < own_blk
            s_sel = jnp.where(slot_valid[None, None, :, None], s_sel, -jnp.inf)
            k_own = lax.dynamic_index_in_dim(kb_b, own_blk, axis=1, keepdims=False)
            v_own = lax.dynamic_index_in_dim(vb_b, own_blk, axis=1, keepdims=False)
            s_own = jnp.einsum('hqd,hld->hql', qc, k_own).astype(jnp.float32) * scale
            kpos_own = own_blk * MOBA_BLOCK + jnp.arange(MOBA_BLOCK)
            s_own = jnp.where(kpos_own[None, None, :] <= qpos[None, :, None], s_own, -jnp.inf)
            s_all = jnp.concatenate([s_sel.reshape(H, Q_BLOCK, n_sel * MOBA_BLOCK), s_own], axis=-1)
            p = jax.nn.softmax(s_all, axis=-1).astype(v_b_dtype)
            p_sel = p[..., :n_sel * MOBA_BLOCK].reshape(H, Q_BLOCK, n_sel, MOBA_BLOCK)
            p_own = p[..., n_sel * MOBA_BLOCK:]
            return (jnp.einsum('hqnl,hqnld->hqd', p_sel, v_sel)
                    + jnp.einsum('hql,hld->hqd', p_own, v_own))

        o = lax.map(per_chunk, jnp.arange(n_chunks))
        return o.transpose(1, 0, 2, 3).reshape(H, S, d)

    v_b_dtype = v.dtype
    o = lax.map(per_batch, (qh, kb, vb, sel))
    return o.transpose(0, 2, 1, 3).reshape(B, S, MOBA_WIDTH)

def hybrid_mixer(h, w_in, lq1, lk1, lq2, lk2, subln_g, w_out, lambda_init, cos, sin):
    B, S, _ = h.shape
    proj = h @ w_in
    cuts = [DIFF_WIDTH, 2 * DIFF_WIDTH, 3 * DIFF_WIDTH,
            3 * DIFF_WIDTH + MOBA_WIDTH, 3 * DIFF_WIDTH + 2 * MOBA_WIDTH]
    dq, dk, dv, mq, mk, mv = jnp.split(proj, cuts, axis=-1)
    dq = apply_partial_rope(dq.reshape(B, S, DIFF_HEADS, 2, DIFF_HEAD_DIM), cos, sin)
    dk = apply_partial_rope(dk.reshape(B, S, DIFF_HEADS, 2, DIFF_HEAD_DIM), cos, sin)
    dv = dv.reshape(B, S, DIFF_HEADS, 2 * DIFF_HEAD_DIM)
    lam = (jnp.exp(jnp.sum(lq1.astype(jnp.float32) * lk1.astype(jnp.float32)))
           - jnp.exp(jnp.sum(lq2.astype(jnp.float32) * lk2.astype(jnp.float32))) + lambda_init)
    out_a = differential_attention(dq, dk, dv, lam, lambda_init, subln_g)
    mq = apply_partial_rope(mq.reshape(B, S, MOBA_HEADS, MOBA_HEAD_DIM), cos, sin)
    mk = apply_partial_rope(mk.reshape(B, S, MOBA_HEADS, MOBA_HEAD_DIM), cos, sin)
    mv = mv.reshape(B, S, MOBA_HEADS, MOBA_HEAD_DIM)
    out_b = moba_attention(mq, mk, mv)
    return jnp.concatenate([out_a, out_b], axis=-1) @ w_out

def memory_cross_attention(h, mem_n, w_q, w_kv, w_o):
    B, S, D = h.shape
    M = mem_n.shape[1]
    q = (h @ w_q).reshape(B, S, MEM_HEADS, MEM_HEAD_DIM)
    k, v = jnp.split(mem_n @ w_kv, 2, axis=-1)
    k = k.reshape(B, M, MEM_HEADS, MEM_HEAD_DIM)
    v = v.reshape(B, M, MEM_HEADS, MEM_HEAD_DIM)
    s = jnp.einsum('bshd,bmhd->bhsm', q, k).astype(jnp.float32) * (MEM_HEAD_DIM ** -0.5)
    p = jax.nn.softmax(s, axis=-1).astype(v.dtype)
    o = jnp.einsum('bhsm,bmhd->bshd', p, v).reshape(B, S, D)
    return o @ w_o

def clamped_swiglu(hidden):
    glu, lin = hidden[..., ::2], hidden[..., 1::2]
    glu = jnp.minimum(glu, SWIGLU_LIMIT)
    lin = jnp.clip(lin, -SWIGLU_LIMIT, SWIGLU_LIMIT)
    return glu * jax.nn.sigmoid(SWIGLU_ALPHA * glu) * (lin + 1.0)

def moe_ffn(h, w_router, b_router, w_mlp1, b_mlp1, w_mlp2, b_mlp2):
    B, S, D = h.shape
    xt = h.reshape(B * S, D)
    logits = (xt @ w_router + b_router).astype(jnp.float32)
    top_val, top_idx = lax.top_k(logits, TOP_K)
    top_w = jax.nn.softmax(top_val, axis=-1)
    combine = jnp.einsum('tk,tke->te', top_w,
                         jax.nn.one_hot(top_idx, N_EXPERTS, dtype=jnp.float32)).astype(h.dtype)
    y = jnp.zeros_like(xt)
    for e in range(N_EXPERTS):
        hid = clamped_swiglu(xt @ w_mlp1[e] + b_mlp1[e])
        y = y + combine[:, e:e + 1] * (hid @ w_mlp2[e] + b_mlp2[e])
    return y.reshape(B, S, D)

def setup_inputs(seed: int = 0) -> dict:
    key = jax.random.key(seed)
    ks = jax.random.split(key, 30)
    f32 = jnp.float32
    L, D = DEPTH, D_MODEL

    def nrm(k, shape, scale):
        return jax.random.normal(k, shape, f32) * scale

    x = nrm(ks[0], (BATCH, SEQ, D), 1.0)
    mem = nrm(ks[1], (BATCH, MEM_LEN, D), 1.0)
    w_in = jnp.concatenate([
        nrm(ks[2], (L, D, 2 * DIFF_WIDTH), D ** -0.5),
        nrm(ks[3], (L, D, DIFF_WIDTH), D ** -0.5 * DEEPNORM_BETA),
        nrm(ks[4], (L, D, 2 * MOBA_WIDTH), D ** -0.5),
        nrm(ks[5], (L, D, MOBA_WIDTH), D ** -0.5 * DEEPNORM_BETA)], axis=-1)
    diff_lambda_q1 = nrm(ks[6], (L, DIFF_HEAD_DIM), 0.1)
    diff_lambda_k1 = nrm(ks[7], (L, DIFF_HEAD_DIM), 0.1)
    diff_lambda_q2 = nrm(ks[8], (L, DIFF_HEAD_DIM), 0.1)
    diff_lambda_k2 = nrm(ks[9], (L, DIFF_HEAD_DIM), 0.1)
    diff_subln_g = 1.0 + nrm(ks[10], (L, 2 * DIFF_HEAD_DIM), 0.05)
    w_mix_out = nrm(ks[11], (L, MIX_WIDTH, D), MIX_WIDTH ** -0.5 * DEEPNORM_BETA)
    ln1_g = 1.0 + nrm(ks[12], (L, D), 0.05)
    ln1_b = nrm(ks[13], (L, D), 0.02)
    mem_ln_g = 1.0 + nrm(ks[14], (D,), 0.05)
    mem_ln_b = nrm(ks[15], (D,), 0.02)
    w_mem_q = nrm(ks[16], (L, D, D), D ** -0.5)
    w_mem_kv = jnp.concatenate([nrm(ks[17], (L, D, D), D ** -0.5),
                                nrm(ks[18], (L, D, D), D ** -0.5 * DEEPNORM_BETA)], axis=-1)
    w_mem_o = nrm(ks[19], (L, D, D), D ** -0.5 * DEEPNORM_BETA)
    ln2_g = 1.0 + nrm(ks[20], (L, D), 0.05)
    ln2_b = nrm(ks[21], (L, D), 0.02)
    w_router = nrm(ks[22], (L, D, N_EXPERTS), D ** -0.5)
    b_router = nrm(ks[23], (L, N_EXPERTS), 0.01)
    w_mlp1 = nrm(ks[24], (L, N_EXPERTS, D, 2 * D_FF), D ** -0.5)
    b_mlp1 = nrm(ks[25], (L, N_EXPERTS, 2 * D_FF), 0.01)
    w_mlp2 = nrm(ks[26], (L, N_EXPERTS, D_FF, D), D_FF ** -0.5 * DEEPNORM_BETA)
    b_mlp2 = nrm(ks[27], (L, N_EXPERTS, D), 0.01)
    ln3_g = 1.0 + nrm(ks[28], (L, D), 0.05)
    ln3_b = nrm(ks[29], (L, D), 0.02)
    return {"x": x, "mem": mem, "w_in": w_in,
            "diff_lambda_q1": diff_lambda_q1, "diff_lambda_k1": diff_lambda_k1,
            "diff_lambda_q2": diff_lambda_q2, "diff_lambda_k2": diff_lambda_k2,
            "diff_subln_g": diff_subln_g, "w_mix_out": w_mix_out, "ln1_g": ln1_g, "ln1_b": ln1_b,
            "mem_ln_g": mem_ln_g, "mem_ln_b": mem_ln_b, "w_mem_q": w_mem_q, "w_mem_kv": w_mem_kv,
            "w_mem_o": w_mem_o, "ln2_g": ln2_g, "ln2_b": ln2_b, "w_router": w_router,
            "b_router": b_router, "w_mlp1": w_mlp1, "b_mlp1": b_mlp1, "w_mlp2": w_mlp2,
            "b_mlp2": b_mlp2, "ln3_g": ln3_g, "ln3_b": ln3_b}

def reference(x, mem, w_in, diff_lambda_q1, diff_lambda_k1, diff_lambda_q2, diff_lambda_k2,
              diff_subln_g, w_mix_out, ln1_g, ln1_b, mem_ln_g, mem_ln_b, w_mem_q, w_mem_kv,
              w_mem_o, ln2_g, ln2_b, w_router, b_router, w_mlp1, b_mlp1, w_mlp2, b_mlp2,
              ln3_g, ln3_b):
    S = x.shape[1]
    cos, sin = rope_tables(S)
    mem_n = layer_norm(mem, mem_ln_g, mem_ln_b)
    h = x
    for l in range(DEPTH):
        lambda_init = 0.8 - 0.6 * math.exp(-0.3 * l)
        mix = hybrid_mixer(h, w_in[l], diff_lambda_q1[l], diff_lambda_k1[l], diff_lambda_q2[l],
                           diff_lambda_k2[l], diff_subln_g[l], w_mix_out[l], lambda_init, cos, sin)
        h = layer_norm(DEEPNORM_ALPHA * h + mix, ln1_g[l], ln1_b[l])
        xatt = memory_cross_attention(h, mem_n, w_mem_q[l], w_mem_kv[l], w_mem_o[l])
        h = layer_norm(DEEPNORM_ALPHA * h + xatt, ln2_g[l], ln2_b[l])
        ffn = moe_ffn(h, w_router[l], b_router[l], w_mlp1[l], b_mlp1[l], w_mlp2[l], b_mlp2[l])
        h = layer_norm(DEEPNORM_ALPHA * h + ffn, ln3_g[l], ln3_b[l])
    return h


_drawn_inputs = setup_inputs


def setup_inputs(seed=0):
    import zlib

    import numpy as np

    out = dict(_drawn_inputs(seed))
    spreads = {}
    factors = {'diff_lambda_q1': 4.148,
     'diff_lambda_k2': 8.0,
     'mem_ln_g': 8.0,
     'mem_ln_b': 4.79,
     'b_router': 3.45,
     'b_mlp1': 8.0,
     'b_mlp2': 8.0,
     'ln3_b': 2.931}
    for name, (base, spread) in spreads.items():
        noise = np.random.default_rng([zlib.crc32(name.encode()), seed]).standard_normal(out[name].shape)
        drawn = base * np.exp(spread * noise) if base else spread * noise
        out[name] = __import__('jax').numpy.asarray(drawn.astype(out[name].dtype))
    for name, factor in factors.items():
        out[name] = (out[name] * factor).astype(out[name].dtype)
    return out
```

```python
from contextlib import ExitStack
import math

import numpy as np

import concourse.bass as bass
from concourse import mybir

F32 = mybir.dt.float32
BF16 = mybir.dt.bfloat16
I32 = mybir.dt.int32
ALU = mybir.AluOpType
ACT = mybir.ActivationFunctionType
AX = mybir.AxisListType
ds = bass.ds

P = 128
D = 1024
S = 256
NT = S // P
KC = D // P
HD = 64
MAPS = 16
GROUP = 4
SEG = 3 * P
SCALE = HD ** -0.5
MEM_HEADS = 4
MEM_SCALE = (D // MEM_HEADS) ** -0.5
ROT = 8
E = 32
TOPK = 4
SLOTS = 64
FF = 1024
LIMIT = 7.0
SW_ALPHA = 1.702
EPS = 1e-5
ALPHA = 2.0 ** 0.25
LAMBDA_INIT = 0.2
BIG = 1e30

NSLOT = 12
PRE = 6

C_ID, C_MASK, C_TRI, C_IOTA, C_HOT, C_COS, C_SIN = 0, 128, 512, 640, 768, 801, 817
C_END = 833

BLOCKS = [("in", b) for b in range(6)] + [("kv", 0), ("kv", 1), ("out", 0), ("out", 1), ("kv", 2),
                                          ("q", 0), ("q", 1), ("kv", 3), ("o", 0), ("o", 1)]


def shape_constants():
    c = np.zeros((P, C_END), np.float32)
    row, col = np.arange(P)[:, None], np.arange(P)[None, :]
    c[:, C_ID:C_ID + P] = row == col
    causal = np.where(col <= row, 0.0, -BIG)
    c[:, C_MASK:C_MASK + P] = causal
    c[:, C_MASK + 2 * P:C_MASK + 3 * P] = causal
    c[:, C_TRI:C_TRI + P] = row < col
    c[:, C_IOTA:C_IOTA + P] = np.arange(P) % SLOTS
    c[:, C_HOT:C_HOT + E + 1] = (row % E) == (np.arange(E + 1) % E)
    inv = (np.float32(500000.0) ** (-np.arange(0, 2 * ROT, 2, dtype=np.float32) / np.float32(2 * ROT))).astype(np.float32)
    ang = np.arange(S, dtype=np.float32)[:, None] * inv[None, :]
    for t in range(NT):
        c[:, C_COS + ROT * t:C_COS + ROT * (t + 1)] = np.cos(ang[P * t:P * (t + 1)])
        c[:, C_SIN + ROT * t:C_SIN + ROT * (t + 1)] = np.sin(ang[P * t:P * (t + 1)])
    return c


def plan_banks():
    jobs = [("xT", t, q) for t in range(NT) for q in range(2)]
    jobs += [(k, t) for k in ("dq", "dk", "dv") for t in range(NT)]
    jobs += [("memT", t, q) for t in range(NT) for q in range(2)]
    jobs += [(k, t) for k in ("Tdq", "Tdk") for t in range(NT)]
    jobs += [("S", m) for m in range(8)]
    jobs += [(k, t) for k in ("mq", "mk") for t in range(NT)]
    jobs += [("TA", 0), ("TA", 1), ("PV", 0), ("TA", 2), ("PV", 1), ("TA", 3), ("PV", 2), ("PV", 3)]
    jobs += [("mv", t) for t in range(NT)]
    jobs += [(k, t) for k in ("Tmq", "Tmk") for t in range(NT)]
    jobs += [("S", m) for m in range(8, 16)]
    jobs += [("kmT", cb, j) for cb in range(2) for j in range(2)]
    jobs += [("TA", 4)]
    for m in range(4, 12):
        jobs += ([("TA", m + 1)] if m < 11 else []) + [("PV", m)]
    jobs += [("oT", t, q) for t in range(NT) for q in range(2)]
    jobs += [("mix", cb, t) for cb in range(2) for t in range(NT)]
    jobs += [("vm", 0, t) for t in range(NT)]
    jobs += [("h1T", t, q) for t in range(NT) for q in range(2)]
    jobs += [("qmT", cb, j) for cb in range(2) for j in range(2)]
    jobs += [("MS", h) for h in range(MEM_HEADS)]
    jobs += [("vm", 1, t) for t in range(NT)]
    jobs += [("TP", 0)]
    for h in range(MEM_HEADS):
        jobs += ([("TP", h + 1)] if h < 3 else []) + [("PM", h)]
    jobs += [("mo", cb, t) for cb in range(2) for t in range(NT)]
    plan, used = {}, [0] * 8
    for n, name in enumerate(jobs):
        plan[name] = (n % 8, used[n % 8])
        used[n % 8] += 1
    late = [("h2T", t, q) for t in range(NT) for q in range(2)] + [("lgT",), ("lg",), ("rank",)]
    for n, name in enumerate(late):
        plan[name] = (n % 4, used[n % 4])
        used[n % 4] += 1
    for b, (t, g) in enumerate((t, g) for t in range(NT) for g in range(2)):
        plan[("Y", t, g)] = (4 + b, used[4 + b])
    return plan, used


def decoder_layer(nc, a):
    plan, bank_jobs = plan_banks()
    w_dram = {"in": a["w_in"][0], "kv": a["w_mem_kv"][0], "out": a["w_mix_out"][0],
              "q": a["w_mem_q"][0], "o": a["w_mem_o"][0]}

    with ExitStack() as ctx:
        def sb(name, shape, dt=F32):
            return ctx.enter_context(nc.sbuf_tensor(name, shape, dt))

        def sem(name):
            return ctx.enter_context(nc.semaphore(name))

        banks = [ctx.enter_context(nc.psum_tensor(f"bank{i}", [P, 512], F32)) for i in range(8)]

        ring = sb("ring", [P, NSLOT, 2048])
        qk_raw = ring[:, 6:8, :].rearrange("p s n -> p (s n)").rearrange("p (t k n) -> p t k n", t=NT, k=4)
        qz = ring[:, 8:10, :].rearrange("p s n -> p (s n)").rearrange("p (m n) -> p m n", m=MAPS)

        def slot3(k):
            return ring[:, k, :].rearrange("p (c n) -> p c n", c=KC)

        kT, h1T = slot3(10), slot3(10)
        xT, oT = slot3(11), slot3(11)
        qmT = slot3(8)
        pm = ring[:, 9, :].rearrange("p (h t n) -> p h t n", h=MEM_HEADS, t=NT)
        pmT = ring[:, 6, :].rearrange("p (h t n) -> p h t n", h=MEM_HEADS, t=NT)
        omT = slot3(7)

        h = sb("h", [P, NT, D])
        mem_o = sb("mem_o", [P, NT, D])
        mem_t = sb("mem_t", [P, KC, S])
        v = sb("v", [P, NT, D])
        gb_a = sb("gb_a", [P, 2, D])
        late = sb("late", [P, 4096])
        vm = sb("vm", [P, NT, D])
        scores = sb("scores", [P, 2, GROUP, SEG])
        aT = sb("aT", [P, GROUP, SEG])
        gb_b = late[:, 0:2 * D].rearrange("p (a n) -> p a n", a=2)
        kmT = late[:, 2 * D:4 * D].rearrange("p (c n) -> p c n", c=KC)
        bias_f = late[0:96, 0:3 * D]
        h_parts = scores[:, :, :, :].rearrange("p a b c -> p (a b c)").bitcast(BF16).rearrange(
            "p (t j n) -> p t j n", t=NT, j=3)
        hidden = v[:, :, :].rearrange("p t n -> p (t n)").rearrange("p (a n) -> p a n", a=4)
        glu, sig, lin, hidT = (hidden[:, i, :] for i in range(4))

        bias_parts = sb("bias_parts", [96, 3 * D], BF16)
        x_e = sb("x_e", [P, KC, SLOTS])
        y_e = sb("y_e", [P, 512])
        back = sb("back", [P, 2, S])
        pick_w = sb("pick_w", [P, NT, P])
        pick = sb("pick", [P, NT, SLOTS], BF16)
        hot = sb("hot", [96, SLOTS], BF16)
        ones96 = sb("ones96", [96, SLOTS])
        const = sb("const", [P, C_END])
        tri_b = sb("tri_b", [P, P], BF16)
        ones_b = sb("ones_b", [P, P], BF16)
        diag = sb("diag", [P, P])
        w_router = sb("w_router", [P, KC, E])
        b_router = sb("b_router", [E, 1])
        sub_g = sb("sub_g", [P, P])
        lam_in = sb("lam_in", [P, 4, HD])
        lam = sb("lam", [P, 8])
        rope_tmp = sb("rope_tmp", [P, 4, NT, 8, ROT])
        stats = sb("stats", [P, 8, 2, 6])
        mv_ln = sb("mv_ln", [P, 8, 2])
        ln_s = sb("ln_s", [P, 8, 3])
        half = sb("half", [P, 8])
        top_max = sb("top_max", [P, 4, 2, GROUP])
        sums = sb("sums", [P, 4, 2, GROUP])
        recips = sb("recips", [P, 4, 2, GROUP])
        rms = sb("rms", [P, 3, 8])
        mem_s = sb("mem_s", [P, 4, MEM_HEADS, 2])
        lgT = sb("lgT", [E, S])
        lg = sb("lg", [P, NT, E])
        best = sb("best", [P, NT, 8])
        route = sb("route", [P, 4, NT, E])
        mask_b = sb("mask_b", [P, NT, E], BF16)
        small = sb("small", [P, 16])
        sweeps_i = sb("sweeps_i", [P, 1], I32)
        pos = sb("pos", [P, NT, E + 1])
        wt = sb("wt", [P, NT, E + 1])
        square = sb("square", [P, P])

        ident = const[:, C_ID:C_ID + P]
        mask = const[:, C_MASK:C_MASK + SEG]
        iota = const[:, C_IOTA:C_IOTA + P]

        filled = [sem(f"bank_filled{i}") for i in range(8)]
        drained = [sem(f"bank_drained{i}") for i in range(8)]
        x_in = [sem(f"x_in{t}") for t in range(NT)]
        mem_in = [sem(f"mem_in{t}") for t in range(NT)]
        const_in, gb_a_in, gb_b_in = sem("const_in"), sem("gb_a_in"), sem("gb_b_in")
        small_in, bias_in, router_in = sem("small_in"), sem("bias_in"), sem("router_in")
        unit_in = [sem(f"unit_in{i}") for i in range(PRE)]
        first_half_used = sem("first_half_used")
        qz_zeroed, bias_split = sem("qz_zeroed"), sem("bias_split")
        pool_step, dve_step = sem("pool_step"), sem("dve_step")
        var_ready, rstd_ready, shift_ready = sem("var_ready"), sem("rstd_ready"), sem("shift_ready")
        normed, ln_ready = sem("normed"), sem("ln_ready")
        lam_sums, lam_exp = sem("lam_sums"), sem("lam_exp")
        roped, max_ready, exp_ready, mixed = sem("roped"), sem("max_ready"), sem("exp_ready"), sem("mixed")
        squared, rms_var, rms_rstd = sem("squared"), sem("rms_var"), sem("rms_rstd")
        o_ready = sem("o_ready")
        mem_max, pm_ready = sem("mem_max"), sem("pm_ready")
        best_ready, route_exp, mask_ready = sem("best_ready"), sem("route_exp"), sem("mask_ready")
        part_ready, rest_ready, prepared = sem("part_ready"), sem("rest_ready"), sem("prepared")
        sweeps_ready = sem("sweeps_ready")
        chunk_in = [sem(f"chunk_in{i}") for i in range(NSLOT)]
        chunks_used = sem("chunks_used")
        hot_ready, hot_used = sem("hot_ready"), sem("hot_used")
        pick_ready, pick_w_ready = sem("pick_ready"), sem("pick_w_ready")
        gathered, x_e_ready = sem("gathered"), sem("x_e_ready")
        up_done, up_read = sem("up_done"), sem("up_read")
        glu_ready, sig_ready, act_ready, hid_ready = sem("glu_ready"), sem("sig_ready"), sem("act_ready"), sem("hid_ready")
        turned, back_ready, scattered = sem("turned"), sem("back_ready"), sem("scattered")
        hid_turned, hidT_ready = sem("hid_turned"), sem("hidT_ready")
        down_done, y_ready = sem("down_done"), sem("y_ready")
        pos_moved, all_added = sem("pos_moved"), sem("all_added")
        out_written = sem("out_written")

        def bank_for(pe, *name):
            b, n = plan[name]
            if n:
                pe.wait_ge(drained[b], n)
            return banks[b]

        def filled_by(*name):
            return filled[plan[name][0]]

        def drained_by(*name):
            return drained[plan[name][0]]

        def wait_filled(eng, *name):
            b, n = plan[name]
            eng.wait_ge(filled[b], n + 1)
            return banks[b]

        def wait_drained(eng, *name):
            b, n = plan[name]
            eng.wait_ge(drained[b], n + 1)

        def unit(u):
            return ring[:, u % PRE, :].rearrange("p (c n) -> p c n", c=4)

        last_job = [("dq", 1), ("dk", 1), ("dv", 1), ("mq", 1), ("mk", 1), ("mv", 1), ("kmT", 0, 1), ("kmT", 1, 1),
                    ("mix", 0, 1), ("mix", 1, 1), ("vm", 0, 1), ("qmT", 0, 1), ("qmT", 1, 1), ("vm", 1, 1),
                    ("mo", 0, 1), ("mo", 1, 1)]

        def wait_unit_used(eng, u):
            if u % 2 == 0:
                eng.wait_ge(first_half_used, u // 2 + 1)
            else:
                wait_filled(eng, *last_job[u // 2])

        def expert_src(e, k):
            if k < KC:
                return a["w_mlp1"][0, ds(e, 1), P * k:P * (k + 1), :].rearrange("a p n -> p (a n)")
            r = 2 * P * (k - KC)
            return a["w_mlp2"][0, ds(e, 1), r:r + 2 * P, :].rearrange("a (c p) n -> p (a c) n", c=2)

        def expert_dst(k):
            if k < KC:
                return ring[:, k, :]
            return ring[:, k, :].rearrange("p (c n) -> p c n", c=2)

        block = ctx.enter_context(nc.Block())

        @block.sync
        def _(sp):
            for t in range(NT):
                sp.dma_start(h[:, t, :], a["x"][0, P * t:P * (t + 1), :]).then_inc(x_in[t], 16)
                if t == 0:
                    sp.dma_start(const[:, :], a["const"]).then_inc(const_in, 16)
            for u in range(2 * len(BLOCKS)):
                tensor, cb = BLOCKS[u // 2]
                if u >= PRE:
                    wait_unit_used(sp, u - PRE)
                src = w_dram[tensor][512 * (u % 2):512 * (u % 2 + 1), 512 * cb:512 * (cb + 1)]
                sp.dma_start(unit(u), src.rearrange("(c p) n -> p c n", c=4)).then_inc(unit_in[u % PRE], 16)
            n = 2 * len(BLOCKS)
            last_reader = {11: ("mix", 1, 1), 10: ("qmT", 1, 1), 8: ("MS", 3), 9: ("TP", 3), 6: ("PM", 3), 7: ("mo", 1, 1)}
            for k in (11, 10, 8, 9, 2, 3, 6, 4, 5, 0, 1, 7):
                if k >= PRE:
                    wait_filled(sp, *last_reader[k])
                else:
                    wait_unit_used(sp, max(u for u in range(n) if u % PRE == k))
                sp.dma_start(expert_dst(k), expert_src(0, k)).then_inc(chunk_in[k], 16)

            def load_expert(e, before):
                used = 0
                for k in range(NSLOT):
                    if k == KC - 1:
                        sp.wait_ge(up_done, before)
                    elif k == NSLOT - 1:
                        sp.wait_ge(down_done, before)
                    else:
                        used += 1
                        sp.wait_ge(chunks_used, before * 10 + (used - 10))
                    sp.dma_start(expert_dst(k), expert_src(e, k)).then_inc(chunk_in[k], 16)

            with sp.Fori(1, E) as e:
                load_expert(e, e)
            sp.wait_ge(sweeps_ready, 1)
            sweeps = sp.value_load(sweeps_i[0:1, 0:1], min_val=1, max_val=S // SLOTS)
            with sp.If(sweeps > 1):
                with sp.Fori(1, sweeps) as s:
                    with sp.Fori(0, E) as e:
                        load_expert(e, s * E + e)
            for t in range(NT):
                sp.wait_ge(ln_ready, 7 + t)
                sp.dma_start(a["out"][0, P * t:P * (t + 1), :], h[:, t, :]).then_inc(out_written, 16)
            sp.wait_ge(out_written, 16 * NT)

        @block.gpsimd
        def _(pool):
            steps = [0]

            def step(ins):
                steps[0] += 1
                ins.then_inc(pool_step, 1)
                pool.wait_ge(pool_step, steps[0])

            def row(ap):
                return ap.broadcast_to([P, ap.shape[1]])

            for t in range(NT):
                pool.dma_start(mem_o[:, t, :], a["mem"][0, P * t:P * (t + 1), :]).then_inc(mem_in[t], 16)
            pool.dma_start(gb_a[:, 0, :], row(a["mem_ln_g"].rearrange("(a n) -> a n", a=1))).then_inc(gb_a_in, 16)
            pool.dma_start(gb_a[:, 1, :], row(a["mem_ln_b"].rearrange("(a n) -> a n", a=1))).then_inc(gb_a_in, 16)
            step(pool.memset(half[:, :], -0.5))
            pool.memset(qz, 0.0).then_inc(qz_zeroed, 1)
            for i, name in enumerate(("diff_lambda_q1", "diff_lambda_q2", "diff_lambda_k1", "diff_lambda_k2")):
                pool.dma_start(lam_in[:, i, :], row(a[name])).then_inc(small_in, 16)
            pool.dma_start(sub_g[:, :], row(a["diff_subln_g"])).then_inc(small_in, 16)
            for i in range(3):
                pool.dma_start(bias_f[E * i:E * (i + 1), 0:2 * FF], a["b_mlp1"][0]).then_inc(bias_in, 16)
                pool.dma_start(bias_f[E * i:E * (i + 1), 2 * FF:3 * FF], a["b_mlp2"][0]).then_inc(bias_in, 16)
            pool.dma_start(w_router[:, :, :], a["w_router"][0].rearrange("(c p) e -> p c e", c=KC)).then_inc(router_in, 16)
            pool.dma_start(b_router[:, :], a["b_router"].rearrange("a e -> e a")).then_inc(router_in, 16)

            def inverse_root(n):
                pool.wait_ge(var_ready, n + 1)
                pool.tensor_tensor(ln_s[:, n, 1:2], ln_s[:, n, 0:1], half[:, 0:1], ALU.pow).then_inc(rstd_ready, 1)

            for n in range(2):
                inverse_root(n)
            pool.wait_ge(bias_in, 16 * 6)
            step(pool.tensor_copy(bias_parts[:, :], bias_f))
            for i in (1, 2):
                lo = E * i
                while lo < 96:
                    step(pool.tensor_tensor(bias_f[lo:lo + E], bias_f[lo:lo + E], bias_parts[lo:lo + E, :], ALU.subtract))
                    step(pool.tensor_copy(bias_parts[lo:lo + E, :], bias_f[lo:lo + E]))
                    lo += E
            pool.memset(ones96[:, :], 1.0).then_inc(bias_split, 1)
            pool.wait_ge(bias_split, 1)
            pool.dma_start(gb_b[:, 0, :], row(a["ln1_g"])).then_inc(gb_b_in, 16)
            pool.dma_start(gb_b[:, 1, :], row(a["ln1_b"])).then_inc(gb_b_in, 16)
            pool.wait_ge(ln_ready, 2)
            pool.dma_start(gb_a[:, 0, :], row(a["ln2_g"])).then_inc(gb_a_in, 16)
            pool.dma_start(gb_a[:, 1, :], row(a["ln2_b"])).then_inc(gb_a_in, 16)
            pool.wait_ge(rms_var, 1)
            pool.tensor_tensor(rms[:, 2, :], rms[:, 1, :], half[:, :], ALU.pow).then_inc(rms_rstd, 1)
            for n in range(2, 4):
                inverse_root(n)
            pool.wait_ge(ln_ready, 4)
            pool.dma_start(gb_b[:, 0, :], row(a["ln3_g"])).then_inc(gb_b_in, 16)
            pool.dma_start(gb_b[:, 1, :], row(a["ln3_b"])).then_inc(gb_b_in, 16)
            for n in range(4, 8):
                inverse_root(n)

        @block.tensor
        def _(pe):
            def wait_unit(u):
                pe.wait_ge(unit_in[u % PRE], 16 * (u // PRE + 1))

            def turn_rows(name, src):
                for t in range(NT):
                    for q in range(2):
                        if name == "xT" and q == 0:
                            pe.wait_ge(x_in[t], 16)
                        b = bank_for(pe, name, t, q)
                        for j in range(4):
                            c = 4 * q + j
                            last = pe.transpose(b[:, P * j:P * (j + 1)], src[:, t, P * c:P * (c + 1)], ident)
                        last.then_inc(filled_by(name, t, q), 1)

            def project_rows(blk, left, *names):
                b = [bank_for(pe, *names[t]) for t in range(NT)]
                for c in range(KC):
                    if c % 4 == 0:
                        wait_unit(2 * blk + c // 4)
                    for t in range(NT):
                        mm = pe.matmul(b[t][:, :], left[:, c, P * t:P * (t + 1)], unit(2 * blk + c // 4)[:, c % 4, :],
                                       start=(c == 0), stop=(c == KC - 1))
                        if c == KC - 1:
                            mm.then_inc(filled_by(*names[t]), 1)
                    if c == 3:
                        mm.then_inc(first_half_used, 1)

            def project_cols(blk, right, name, cb):
                for h_ in range(2):
                    wait_unit(2 * blk + h_)
                for pair in range(2):
                    b = bank_for(pe, name, cb, pair)
                    for i in range(2):
                        j = 2 * pair + i
                        for c in range(KC):
                            mm = pe.matmul(b[:, S * i:S * (i + 1)], unit(2 * blk + c // 4)[:, c % 4, P * j:P * (j + 1)],
                                           right[:, c, :], start=(c == 0), stop=(c == KC - 1))
                            if j == 3 and c == 3:
                                mm.then_inc(first_half_used, 1)
                    mm.then_inc(filled_by(name, cb, pair), 1)

            def turn_heads(kind, index):
                pe.wait_ge(roped, index + 1)
                for t in range(NT):
                    b = bank_for(pe, "T" + kind, t)
                    for j in range(4):
                        last = pe.transpose(b[:, P * j:P * (j + 1)], qk_raw[:, t, index, P * j:P * (j + 1)], ident)
                    last.then_inc(filled_by("T" + kind, t), 1)

            def score(m):
                b = bank_for(pe, "S", m)
                pe.matmul(b[:, 0:P], qz[:, m, 0:P], kT[:, m // 2, 0:P], start=True, stop=True)
                pe.matmul(b[:, P:SEG], qz[:, m, P:S], kT[:, m // 2, :], start=True, stop=True)\
                    .then_inc(filled_by("S", m), 1)

            def probs_at(j):
                return (j // 2, 2 * (j % 2)) if j < 4 else (2 + (j - 4) // 4, (j - 4) % 4)

            def turn_probs(j):
                g, i = probs_at(j)
                if j < 4:
                    pe.wait_ge(mixed, g + 1)
                else:
                    pe.wait_ge(exp_ready, g + 1)
                b = bank_for(pe, "TA", j)
                for n in range(3):
                    last = pe.transpose(b[:, P * n:P * (n + 1)], scores[:, g % 2, i, P * n:P * (n + 1)], ident)
                last.then_inc(filled_by("TA", j), 1)

            def weigh(j):
                wait_drained(pe, "TA", j)
                b = bank_for(pe, "PV", j)
                col = P * j if j < 4 else 512 + P * ((j - 4) // 2)
                at = aT[:, j % GROUP, :]
                pe.matmul(b[:, 0:P], at[:, 0:P], v[:, 0, col:col + P], start=True, stop=True)
                pe.matmul(b[:, P:2 * P], at[:, P:2 * P], v[:, 0, col:col + P], start=True, stop=False)
                pe.matmul(b[:, P:2 * P], at[:, 2 * P:3 * P], v[:, 1, col:col + P], start=False, stop=True)\
                    .then_inc(filled_by("PV", j), 1)

            pe.wait_ge(const_in, 16)
            turn_rows("xT", h)
            for t in range(NT):
                for q in range(2):
                    wait_drained(pe, "xT", t, q)
            for i, kind in enumerate(("dq", "dk", "dv")):
                project_rows(i, xT, (kind, 0), (kind, 1))
            pe.wait_ge(ln_ready, 2)
            turn_rows("memT", mem_o)
            turn_heads("dq", 0)
            turn_heads("dk", 1)
            for k in ("Tdq", "Tdk"):
                for t in range(NT):
                    wait_drained(pe, k, t)
            for m in range(8):
                score(m)
            project_rows(3, xT, ("mq", 0), ("mq", 1))
            project_rows(4, xT, ("mk", 0), ("mk", 1))
            for t in range(NT):
                wait_drained(pe, "dv", t)
            turn_probs(0)
            for j in range(4):
                if j < 3:
                    turn_probs(j + 1)
                weigh(j)
            project_rows(5, xT, ("mv", 0), ("mv", 1))
            turn_heads("mq", 2)
            turn_heads("mk", 3)
            for k in ("Tmq", "Tmk"):
                for t in range(NT):
                    wait_drained(pe, k, t)
            for m in range(8, 16):
                score(m)
            for t in range(NT):
                for q in range(2):
                    wait_drained(pe, "memT", t, q)
            project_cols(6, mem_t, "kmT", 0)
            project_cols(7, mem_t, "kmT", 1)
            for t in range(NT):
                wait_drained(pe, "mv", t)
            turn_probs(4)
            for j in range(4, 12):
                if j < 11:
                    turn_probs(j + 1)
                weigh(j)
            pe.wait_ge(o_ready, 1)
            turn_rows("oT", mem_o)
            for t in range(NT):
                for q in range(2):
                    wait_drained(pe, "oT", t, q)
            project_rows(8, oT, ("mix", 0, 0), ("mix", 0, 1))
            project_rows(9, oT, ("mix", 1, 0), ("mix", 1, 1))
            project_rows(10, mem_t, ("vm", 0, 0), ("vm", 0, 1))
            pe.wait_ge(ln_ready, 4)
            turn_rows("h1T", h)
            for t in range(NT):
                for q in range(2):
                    wait_drained(pe, "h1T", t, q)
            project_cols(11, h1T, "qmT", 0)
            project_cols(12, h1T, "qmT", 1)
            for cb in range(2):
                for j in range(2):
                    wait_drained(pe, "kmT", cb, j)
                    wait_drained(pe, "qmT", cb, j)
            for hd in range(MEM_HEADS):
                b = bank_for(pe, "MS", hd)
                for t in range(NT):
                    for i in range(2):
                        mm = pe.matmul(b[:, S * t:S * (t + 1)], qmT[:, 2 * hd + i, P * t:P * (t + 1)],
                                       kmT[:, 2 * hd + i, :], start=(i == 0), stop=(i == 1))
                mm.then_inc(filled_by("MS", hd), 1)
            project_rows(13, mem_t, ("vm", 1, 0), ("vm", 1, 1))

            def turn_mem_probs(hd):
                pe.wait_ge(pm_ready, hd + 1)
                b = bank_for(pe, "TP", hd)
                for mt in range(2):
                    for t in range(NT):
                        n = 2 * mt + t
                        last = pe.transpose(b[:, P * n:P * (n + 1)], pm[:, hd, t, P * mt:P * (mt + 1)], ident)
                last.then_inc(filled_by("TP", hd), 1)

            for cb in range(2):
                for t in range(NT):
                    wait_drained(pe, "vm", cb, t)
            turn_mem_probs(0)
            for hd in range(MEM_HEADS):
                if hd < 3:
                    turn_mem_probs(hd + 1)
                wait_drained(pe, "TP", hd)
                b = bank_for(pe, "PM", hd)
                for i in range(2):
                    c = 2 * hd + i
                    for mt in range(2):
                        mm = pe.matmul(b[:, S * i:S * (i + 1)], vm[:, mt, P * c:P * (c + 1)], pmT[:, hd, mt, :],
                                       start=(mt == 0), stop=(mt == 1))
                mm.then_inc(filled_by("PM", hd), 1)
            for hd in range(MEM_HEADS):
                wait_drained(pe, "PM", hd)
            project_rows(14, omT, ("mo", 0, 0), ("mo", 0, 1))
            project_rows(15, omT, ("mo", 1, 0), ("mo", 1, 1))

            pe.wait_ge(ln_ready, 6)
            turn_rows("h2T", h)
            pe.wait_ge(router_in, 32)
            for t in range(NT):
                for q in range(2):
                    wait_drained(pe, "h2T", t, q)
            b = bank_for(pe, "lgT")
            for c in range(KC):
                mm = pe.matmul(b[0:E, 0:S], w_router[:, c, :], mem_t[:, c, :], start=(c == 0), stop=(c == KC - 1))
            mm.then_inc(filled_by("lgT"), 1)
            pe.wait_ge(prepared, 1)
            for t in range(NT):
                for g in range(2):
                    b = bank_for(pe, "Y", t, g)
                    pe.matmul(b[:, :], diag[:, :], h[:, t, 512 * g:512 * (g + 1)], start=True, stop=False)
            wait_drained(pe, "lgT")
            b = bank_for(pe, "lg")
            for t in range(NT):
                mm = pe.transpose(b[:, E * t:E * (t + 1)], lgT[:, P * t:P * (t + 1)], const[0:E, C_ID:C_ID + E])
            mm.then_inc(filled_by("lg"), 1)
            pe.wait_ge(mask_ready, 1)
            b = bank_for(pe, "rank")
            pe.matmul(b[:, 0:E], tri_b[:, :], mask_b[:, 0, :], start=True, stop=True)
            pe.matmul(b[:, E:2 * E], ones_b[:, :], mask_b[:, 0, :], start=True, stop=False)
            pe.matmul(b[:, E:2 * E], tri_b[:, :], mask_b[:, 1, :], start=False, stop=True)
            pe.matmul(b[:, 2 * E:3 * E], ones_b[:, :], mask_b[:, 0, :], start=True, stop=False)
            pe.matmul(b[:, 2 * E:3 * E], ones_b[:, :], mask_b[:, 1, :], start=False, stop=True)\
                .then_inc(filled_by("rank"), 1)

            up, ty, xg = banks[0:2], banks[2], banks[3]
            acc = [[banks[4 + 2 * t + g] for g in range(2)] for t in range(NT)]
            for i in range(4):
                pe.wait_ge(drained[i], bank_jobs[i])

            def gather():
                for c in range(KC):
                    for n in range(6):
                        t, part = n // 3, n % 3
                        mm = pe.matmul(xg[:, SLOTS * c:SLOTS * (c + 1)], h_parts[:, t, part, P * c:P * (c + 1)],
                                       pick[:, t, :], start=(n == 0), stop=(n == 5))
                mm.then_inc(gathered, 1)

            def scatter(last):
                for t in range(NT):
                    for g in range(2):
                        mm = pe.matmul(acc[t][g][:, :], back[:, g, P * t:P * (t + 1)], y_e[:, :],
                                       start=False, stop=last)
                mm.then_inc(all_added if last else scattered, 1)

            pe.wait_ge(part_ready, 6)
            pe.wait_ge(pick_ready, 1)
            gather()
            pe.wait_ge(sweeps_ready, 1)
            sweeps = pe.value_load(sweeps_i[0:1, 0:1], min_val=1, max_val=S // SLOTS)
            with pe.Fori(0, sweeps) as s:
                with pe.Fori(0, E) as e:
                    now = pe.snap(s * E + e + 1)
                    nxt = pe.snap(now + 1)
                    landed = pe.snap(now * 16)
                    pe.wait_ge(hot_ready, now)
                    pe.wait_ge(up_read, now)
                    for n in range(2):
                        for g in range(2):
                            col = 1024 * g + 512 * n
                            pe.matmul(up[n][64 * g:64 * g + SLOTS, :], hot[:, :], bias_parts[:, col:col + 512],
                                      start=True, stop=False)
                    pe.wait_ge(x_e_ready, now)
                    for k in range(KC):
                        pe.wait_ge(chunk_in[k], landed)
                        for n in range(2):
                            for g in range(2):
                                col = 1024 * g + 512 * n
                                mm = pe.matmul(up[n][64 * g:64 * g + SLOTS, :], x_e[:, k, :],
                                               ring[:, k, col:col + 512], start=False, stop=(k == KC - 1))
                        mm.then_inc(chunks_used if k < KC - 1 else up_done, 1)
                    pe.wait_ge(pick_w_ready, now)
                    pe.wait_ge(y_ready, now)
                    for t in range(NT):
                        mm = pe.transpose(ty[:, P * t:P * (t + 1)], pick_w[:, t, :], ident)
                    mm.then_inc(turned, 1)
                    pe.wait_ge(back_ready, now)
                    scatter(False)
                    pe.wait_ge(pick_ready, nxt)
                    gather()
                    pe.wait_ge(hid_ready, now)
                    pe.wait_ge(back_ready, nxt)
                    for q in range(4):
                        mm = pe.transpose(ty[:, P * q:P * (q + 1)], glu[:, P * q:P * (q + 1)], ident)
                    mm.then_inc(hid_turned, 1)
                    pe.wait_ge(hidT_ready, now)
                    for g in range(2):
                        mm = pe.matmul(ty[64 * g:64 * g + SLOTS, :], hot[:, :],
                                       bias_parts[:, 2 * FF + 512 * g:2 * FF + 512 * (g + 1)], start=True, stop=False)
                    mm.then_inc(hot_used, 1)
                    for u in range(4):
                        pe.wait_ge(chunk_in[KC + u], landed)
                        for i in range(2):
                            c = 2 * u + i
                            for g in range(2):
                                mm = pe.matmul(ty[64 * g:64 * g + SLOTS, :],
                                               hidT[:, P * (c % 4) + 64 * (c // 4):P * (c % 4) + 64 * (c // 4) + SLOTS],
                                               ring[:, KC + u, D * i + 512 * g:D * i + 512 * (g + 1)],
                                               start=False, stop=(c == KC - 1))
                        mm.then_inc(chunks_used if u < 3 else down_done, 1)
            served = pe.snap(sweeps * E + 1)
            pe.wait_ge(y_ready, served)
            pe.wait_ge(back_ready, served)
            scatter(True)

        @block.scalar
        def _(act):
            def copy_rows(name, dst, tiles):
                for t, q in tiles:
                    b = wait_filled(act, name, t, q)
                    act.activation(dst[:, 4 * q:4 * q + 4, P * t:P * (t + 1)],
                                   b[:, :].rearrange("p (c n) -> p c n", c=4), ACT.Copy).then_inc(drained_by(name, t, q), 1)

            def copy_to(dst, *name):
                b = wait_filled(act, *name)
                act.activation(dst, b[:, 0:512], ACT.Copy).then_inc(drained_by(*name), 1)

            def copy_heads(kind, base):
                for t in range(NT):
                    b = wait_filled(act, "T" + kind, t)
                    src = b[:, :].rearrange("p (j n) -> p j n", j=4)
                    if kind[1] == "q":
                        to = qz[:, 2 * base:2 * base + 8, P * t:P * (t + 1)].rearrange("p (j c) n -> p j c n", c=2)
                        act.activation(to[0:HD, :, 0, :], src[0:HD], ACT.Copy)
                        act.activation(to[HD:P, :, 1, :], src[HD:P], ACT.Copy).then_inc(drained_by("T" + kind, t), 1)
                    else:
                        act.activation(kT[:, base:base + 4, P * t:P * (t + 1)], src, ACT.Copy)\
                            .then_inc(drained_by("T" + kind, t), 1)

            def normalise(n, src):
                act.wait_ge(shift_ready, n + 1)
                for i, part in enumerate(src):
                    w = D // len(src)
                    dst = (mem_o if n < 2 else h)[:, n % 2, w * i:w * (i + 1)]
                    last = act.activation(dst, part, ACT.Identity, bias=ln_s[:, n, 2:3], scale=ln_s[:, n, 1:2])
                last.then_inc(normed, 1)

            def exps(g):
                act.wait_ge(max_ready, g + 1)
                for t in range(NT):
                    for i in range(GROUP):
                        at = scores[:, g % 2, i, 0:P] if t == 0 else scores[:, g % 2, i, P:SEG]
                        last = act.activation(at, at, ACT.Exp, bias=top_max[:, g, t, i:i + 1], scale=SCALE,
                                              accum_out=sums[:, g, t, i:i + 1])
                last.then_inc(exp_ready, 1)

            def copy_probs(j):
                b = wait_filled(act, "TA", j)
                if j >= GROUP:
                    wait_filled(act, "PV", j - GROUP)
                act.activation(aT[:, j % GROUP, :], b[:, 0:SEG], ACT.Copy).then_inc(drained_by("TA", j), 1)

            copy_rows("xT", xT, [(0, 1), (1, 1)])
            for i, kind in enumerate(("dq", "dk")):
                for t in range(NT):
                    copy_to(qk_raw[:, t, i, :], kind, t)
            for n in range(2):
                normalise(n, [mem_o[:, n, :]])
            act.wait_ge(lam_sums, 1)
            act.activation(lam[:, 2:4], lam[:, 0:2], ACT.Exp).then_inc(lam_exp, 1)
            for t in range(NT):
                copy_to(v[:, t, 0:512], "dv", t)
            copy_rows("memT", mem_t, [(0, 0), (0, 1), (1, 0), (1, 1)])
            act.wait_ge(qz_zeroed, 1)
            copy_heads("dq", 0)
            copy_heads("dk", 0)
            exps(0)
            exps(1)
            for i, kind in enumerate(("mq", "mk")):
                for t in range(NT):
                    copy_to(qk_raw[:, t, 2 + i, :], kind, t)
            for j in range(4):
                copy_probs(j)
            for t in range(NT):
                copy_to(v[:, t, 512:1024], "mv", t)
            for j in range(4):
                wait_drained(act, "PV", j)
                for t in range(NT):
                    if j or t:
                        act.wait_ge(squared, 2 * j + t)
                    act.activation(square[:, :], mem_o[:, t, P * j:P * (j + 1)], ACT.Square,
                                   accum_out=rms[:, 0, 4 * t + j:4 * t + j + 1]).then_inc(squared, 1)
            copy_heads("mq", 4)
            copy_heads("mk", 4)
            exps(2)
            exps(3)
            act.wait_ge(bias_split, 1)
            for cb in range(2):
                for j in range(2):
                    copy_to(kmT[:, 4 * cb + 2 * j:4 * cb + 2 * j + 2, :].rearrange("p c n -> p (c n)"), "kmT", cb, j)
            for j in range(4, 12):
                copy_probs(j)
            copy_rows("oT", oT, [(0, 0), (0, 1), (1, 0), (1, 1)])
            for n in range(2, 4):
                normalise(n, [h[:, n - 2, :]])
            for t in range(NT):
                copy_to(vm[:, t, 0:512], "vm", 0, t)
            copy_rows("h1T", h1T, [(0, 1), (1, 1)])
            for cb in range(2):
                for j in range(2):
                    copy_to(qmT[:, 4 * cb + 2 * j:4 * cb + 2 * j + 2, :].rearrange("p c n -> p (c n)"), "qmT", cb, j)
            for hd in range(MEM_HEADS):
                b = wait_filled(act, "MS", hd)
                act.wait_ge(mem_max, hd + 1)
                for t in range(NT):
                    last = act.activation(pm[:, hd, t, :], b[:, S * t:S * (t + 1)], ACT.Exp,
                                          bias=mem_s[:, 1, hd, t:t + 1], scale=MEM_SCALE,
                                          accum_out=mem_s[:, 2, hd, t:t + 1])
                last.then_inc(drained_by("MS", hd), 1)
            for t in range(NT):
                copy_to(vm[:, t, 512:1024], "vm", 1, t)
            for hd in range(MEM_HEADS):
                copy_to(pmT[:, hd, :, :].rearrange("p t n -> p (t n)"), "TP", hd)
            for n in range(4, 6):
                normalise(n, [h[:, n - 4, :]])
            copy_rows("h2T", mem_t, [(0, 1), (1, 1)])
            act.wait_ge(ln_ready, 6)
            for part in range(3):
                for t in range(NT):
                    if part:
                        act.wait_ge(rest_ready, 2 * (part - 1) + t + 1)
                    src = h if part == 0 else mem_o
                    act.activation(h_parts[:, t, part, :], src[:, t, :], ACT.Copy).then_inc(part_ready, 1)
                if part == 0:
                    act.wait_ge(best_ready, 1)
                    for t in range(NT):
                        last = act.activation(route[:, 2, t, :], lg[:, t, :], ACT.Exp, bias=small[:, t:t + 1], scale=1.0)
                    last.then_inc(route_exp, 1)

            def take_tokens():
                act.activation(x_e[:, :, :], banks[3][:, :].rearrange("p (c n) -> p c n", c=KC), ACT.Copy)\
                    .then_inc(x_e_ready, 1)

            act.wait_ge(gathered, 1)
            take_tokens()
            act.wait_ge(sweeps_ready, 1)
            sweeps = act.value_load(sweeps_i[0:1, 0:1], min_val=1, max_val=S // SLOTS)
            with act.Fori(0, sweeps) as s:
                with act.Fori(0, E) as e:
                    now = act.snap(s * E + e + 1)
                    nxt = act.snap(now + 1)
                    act.wait_ge(glu_ready, now)
                    act.activation(sig, glu, ACT.Sigmoid, scale=SW_ALPHA).then_inc(sig_ready, 1)
                    act.wait_ge(gathered, nxt)
                    take_tokens()
                    act.wait_ge(hid_turned, now)
                    act.activation(hidT, banks[2][:, :], ACT.Copy).then_inc(hidT_ready, 1)
                    act.wait_ge(down_done, now)
                    act.activation(y_e[:, :], banks[2][:, :], ACT.Copy).then_inc(y_ready, 1)
            act.wait_ge(all_added, 1)
            for n in range(6, 8):
                t = n - 6
                normalise(n, [banks[4 + 2 * t + g][:, :] for g in range(2)])

        @block.vector
        def _(dve):
            steps = [0]

            def step(ins):
                steps[0] += 1
                ins.then_inc(dve_step, 1)
                dve.wait_ge(dve_step, steps[0])

            def copy_rows(name, dst, tiles):
                for t, q in tiles:
                    b = wait_filled(dve, name, t, q)
                    dve.tensor_copy(dst[:, 4 * q:4 * q + 4, P * t:P * (t + 1)],
                                    b[:, :].rearrange("p (c n) -> p c n", c=4)).then_inc(drained_by(name, t, q), 1)

            def variance(n, halves):
                for i in range(2):
                    last = dve.bn_stats(stats[:, n, i, :], halves[i])
                step(last)
                step(dve.bn_aggr(mv_ln[:, n, :], stats[:, n, :, :].rearrange("p a b -> p (a b)")))
                dve.tensor_scalar(ln_s[:, n, 0:1], mv_ln[:, n, 1:2], EPS, None, ALU.add).then_inc(var_ready, 1)

            def shift(n):
                dve.wait_ge(rstd_ready, n + 1)
                dve.tensor_scalar(ln_s[:, n, 2:3], mv_ln[:, n, 0:1], ln_s[:, n, 1:2], -1.0, ALU.mult, ALU.mult)\
                    .then_inc(shift_ready, 1)

            def gain(n, gb):
                x = (mem_o if n < 2 else h)[:, n % 2, :]
                dve.wait_ge(normed, n + 1)
                step(dve.tensor_tensor(x, x, gb[:, 0, :], ALU.mult))
                dve.tensor_tensor(x, x, gb[:, 1, :], ALU.add).then_inc(ln_ready, 1)

            def residual_norm(n, name, gb, gb_in, gb_count):
                for cb in range(2):
                    for t in range(NT):
                        b = wait_filled(dve, name, cb, t)
                        x = h[:, t, 512 * cb:512 * (cb + 1)]
                        dve.scalar_tensor_tensor(out=x, in0=x, scalar=ALPHA, in1=b[:, :], op0=ALU.mult, op1=ALU.add)\
                            .then_inc(drained_by(name, cb, t), 1)
                for t in range(NT):
                    wait_drained(dve, name, 1, t)
                    variance(n + t, [h[:, t, 0:512], h[:, t, 512:1024]])
                for t in range(NT):
                    shift(n + t)
                dve.wait_ge(gb_in, gb_count)
                for t in range(NT):
                    gain(n + t, gb)

            def rope(index, kinds):
                for t in range(NT):
                    wait_drained(dve, kinds, t)
                x = qk_raw[:, :, index, :].rearrange("p t (h d) -> p t h d", h=8)
                x1, x2 = x[:, :, :, 0:ROT], x[:, :, :, ROT:2 * ROT]
                cos = const[:, C_COS:C_COS + 2 * ROT].rearrange("p (t a r) -> p t a r", t=NT, a=1).broadcast_to([P, NT, 8, ROT])
                sin = const[:, C_SIN:C_SIN + 2 * ROT].rearrange("p (t a r) -> p t a r", t=NT, a=1).broadcast_to([P, NT, 8, ROT])
                dve.tensor_tensor(rope_tmp[:, 0], x1, cos, ALU.mult)
                dve.tensor_tensor(rope_tmp[:, 1], x2, sin, ALU.mult)
                dve.tensor_tensor(rope_tmp[:, 2], x2, cos, ALU.mult)
                step(dve.tensor_tensor(rope_tmp[:, 3], x1, sin, ALU.mult))
                dve.tensor_tensor(x1, rope_tmp[:, 0], rope_tmp[:, 1], ALU.subtract)
                dve.tensor_tensor(x2, rope_tmp[:, 2], rope_tmp[:, 3], ALU.add).then_inc(roped, 1)
                dve.wait_ge(roped, index + 1)

            def mask_group(g):
                if g >= 2:
                    wait_filled(dve, "TA", 2 * (g - 2) + 1)
                for i in range(GROUP):
                    m = GROUP * g + i
                    b = wait_filled(dve, "S", m)
                    dve.tensor_tensor(scores[:, g % 2, i, :], b[:, 0:SEG], mask, ALU.add).then_inc(drained_by("S", m), 1)
                wait_drained(dve, "S", GROUP * g + GROUP - 1)
                dve.tensor_reduce(top_max[:, g, 0, :], scores[:, g % 2, :, 0:P], AX.X, ALU.max)
                step(dve.tensor_reduce(top_max[:, g, 1, :], scores[:, g % 2, :, P:SEG], AX.X, ALU.max))
                dve.tensor_scalar(top_max[:, g], top_max[:, g], -SCALE, None, ALU.mult).then_inc(max_ready, 1)

            def invert(g):
                dve.wait_ge(exp_ready, g + 1)
                step(dve.reciprocal(recips[:, g], sums[:, g]))

            def mix_group(g):
                invert(g)
                r1 = recips[:, g].rearrange("p t (j c) -> p t j c", c=2)[:, :, :, 1]
                step(dve.tensor_scalar(r1, r1, lam[:, 4:5], None, ALU.mult))
                parts = [(i, t, slice(0, P) if t == 0 else slice(P, SEG)) for i in (0, 2) for t in range(NT)]
                for i, t, at in parts:
                    p1 = scores[:, g % 2, i + 1, at]
                    last = dve.tensor_scalar(p1, p1, recips[:, g, t, i + 1:i + 2], None, ALU.mult)
                step(last)
                for i, t, at in parts:
                    p0 = scores[:, g % 2, i, at]
                    last = dve.scalar_tensor_tensor(out=p0, in0=p0, scalar=recips[:, g, t, i:i + 1],
                                                    in1=scores[:, g % 2, i + 1, at], op0=ALU.mult, op1=ALU.add)
                last.then_inc(mixed, 1)

            copy_rows("xT", xT, [(0, 0), (1, 0)])
            for t in range(NT):
                dve.wait_ge(mem_in[t], 16)
                variance(t, [mem_o[:, t, 0:512], mem_o[:, t, 512:1024]])
            for t in range(NT):
                shift(t)
            dve.wait_ge(small_in, 16 * 5)
            step(dve.tensor_tensor(lam_in[:, 0:2, :], lam_in[:, 0:2, :], lam_in[:, 2:4, :], ALU.mult))
            dve.tensor_reduce(lam[:, 0:2], lam_in[:, 0:2, :], AX.X, ALU.add).then_inc(lam_sums, 1)
            dve.tensor_scalar(sub_g[:, :], sub_g[:, :], 1.0 - LAMBDA_INIT, None, ALU.mult)
            dve.wait_ge(const_in, 16)
            dve.tensor_copy(tri_b[:, :], const[:, C_TRI:C_TRI + P])
            dve.memset(ones_b[:, :], 1.0)
            dve.tensor_scalar(diag[:, :], ident, ALPHA, None, ALU.mult).then_inc(prepared, 1)
            dve.wait_ge(gb_a_in, 32)
            for t in range(NT):
                gain(t, gb_a)
            dve.wait_ge(lam_exp, 1)
            step(dve.tensor_scalar(lam[:, 4:5], lam[:, 3:4], lam[:, 2:3], LAMBDA_INIT, ALU.subtract, ALU.subtract))
            rope(0, "dq")
            rope(1, "dk")
            dve.wait_ge(prepared, 1)
            mask_group(0)
            mask_group(1)
            mix_group(0)
            mix_group(1)
            rope(2, "mq")
            rope(3, "mk")
            for t in range(NT):
                for q in range(2):
                    wait_filled(dve, "memT", t, q)
            for j in range(4):
                b = wait_filled(dve, "PV", j)
                dve.tensor_copy(mem_o[:, :, P * j:P * (j + 1)], b[:, 0:2 * P].rearrange("p (t n) -> p t n", t=NT))\
                    .then_inc(drained_by("PV", j), 1)
            dve.wait_ge(squared, 8)
            dve.tensor_scalar(rms[:, 1, :], rms[:, 0, :], 1.0 / P, EPS, ALU.mult, ALU.add).then_inc(rms_var, 1)
            dve.wait_ge(rms_rstd, 1)
            for t in range(NT):
                for j in range(4):
                    o = mem_o[:, t, P * j:P * (j + 1)]
                    dve.scalar_tensor_tensor(out=o, in0=o, scalar=rms[:, 2, 4 * t + j:4 * t + j + 1], in1=sub_g[:, :],
                                             op0=ALU.mult, op1=ALU.mult)
            mask_group(2)
            mask_group(3)
            invert(2)
            invert(3)
            for j in range(8):
                b = wait_filled(dve, "PV", 4 + j)
                for t in range(NT):
                    off = P * t + HD * (j % 2)
                    last = dve.tensor_scalar(mem_o[:, t, 512 + HD * j:512 + HD * (j + 1)], b[:, off:off + HD],
                                             recips[:, 2 + j // 4, t, j % 4:j % 4 + 1], None, ALU.mult)
                last.then_inc(drained_by("PV", 4 + j), 1)
            wait_drained(dve, "PV", 11)
            dve.memset(small[:, 8:16], 0.0).then_inc(o_ready, 1)
            residual_norm(2, "mix", gb_b, gb_b_in, 32)
            copy_rows("h1T", h1T, [(0, 0), (1, 0)])
            for hd in range(MEM_HEADS):
                b = wait_filled(dve, "MS", hd)
                step(dve.tensor_reduce(mem_s[:, 0, hd, :], b[:, :].rearrange("p (t n) -> p t n", t=NT), AX.X, ALU.max))
                dve.tensor_scalar(mem_s[:, 1, hd, :], mem_s[:, 0, hd, :], -MEM_SCALE, None, ALU.mult).then_inc(mem_max, 1)
            for hd in range(MEM_HEADS):
                wait_drained(dve, "MS", hd)
                step(dve.reciprocal(mem_s[:, 3, hd, :], mem_s[:, 2, hd, :]))
                for t in range(NT):
                    last = dve.tensor_scalar(pm[:, hd, t, :], pm[:, hd, t, :], mem_s[:, 3, hd, t:t + 1], None, ALU.mult)
                last.then_inc(pm_ready, 1)
            for hd in range(MEM_HEADS):
                b = wait_filled(dve, "PM", hd)
                dve.tensor_copy(omT[:, 2 * hd:2 * hd + 2, :], b[:, :].rearrange("p (c n) -> p c n", c=2))\
                    .then_inc(drained_by("PM", hd), 1)
            residual_norm(4, "mo", gb_a, gb_a_in, 64)
            copy_rows("h2T", mem_t, [(0, 0), (1, 0)])

            def rest(part):
                for t in range(NT):
                    dve.wait_ge(part_ready, 2 * part + t + 1)
                    src = h if part == 0 else mem_o
                    dve.tensor_tensor(mem_o[:, t, :], src[:, t, :], h_parts[:, t, part, :], ALU.subtract)\
                        .then_inc(rest_ready, 1)

            b = wait_filled(dve, "lgT")
            dve.wait_ge(router_in, 32)
            dve.tensor_scalar(lgT[:, :], b[0:E, 0:S], b_router[:, 0:1], None, ALU.add).then_inc(drained_by("lgT"), 1)
            b = wait_filled(dve, "lg")
            dve.tensor_copy(lg[:, :, :], b[:, 0:2 * E].rearrange("p (t e) -> p t e", t=NT)).then_inc(drained_by("lg"), 1)
            wait_drained(dve, "lg")
            for t in range(NT):
                last = dve.max(best[:, t, :], lg[:, t, :])
            step(last)
            dve.tensor_scalar(small[:, 0:2], best[:, :, 0], -1.0, None, ALU.mult).then_inc(best_ready, 1)
            step(dve.memset(best[:, :, TOPK:8], 3e38))
            for t in range(NT):
                last = dve.match_replace(route[:, 0, t, :], best[:, t, :], lg[:, t, :], -BIG)
            step(last)
            step(dve.tensor_tensor(route[:, 1], route[:, 0], lg[:, :, :], ALU.not_equal))
            dve.tensor_copy(mask_b[:, :, :], route[:, 1]).then_inc(mask_ready, 1)
            rest(0)
            dve.wait_ge(route_exp, 1)
            step(dve.tensor_tensor(route[:, 2], route[:, 2], route[:, 1], ALU.mult))
            step(dve.tensor_reduce(small[:, 2:4], route[:, 2], AX.X, ALU.add))
            step(dve.reciprocal(small[:, 4:6], small[:, 2:4]))
            for t in range(NT):
                last = dve.tensor_scalar(wt[:, t, 0:E], route[:, 2, t, :], small[:, 4 + t:5 + t], None, ALU.mult)
            step(last)
            step(dve.tensor_copy(wt[:, :, E:E + 1], wt[:, :, 0:1]))
            rest(1)
            b = wait_filled(dve, "rank")
            step(dve.scalar_tensor_tensor(out=route[:, 3], in0=b[:, 0:2 * E].rearrange("p (t e) -> p t e", t=NT), scalar=1.0,
                                          in1=route[:, 1], op0=ALU.add, op1=ALU.mult))
            step(dve.tensor_scalar(pos[:, :, 0:E], route[:, 3], -1.0, None, ALU.add))
            step(dve.tensor_scalar(pos[:, :, E:E + 1], pos[:, :, 0:1], -float(SLOTS), None, ALU.add))
            dve.tensor_reduce(small[:, 6:7], b[:, 2 * E:3 * E], AX.X, ALU.max).then_inc(drained_by("rank"), 1)
            wait_drained(dve, "rank")
            step(dve.tensor_scalar(small[:, 8:9], small[:, 6:7], float(SLOTS), 1.0, ALU.is_gt, ALU.add))
            for i in (2, 3):
                step(dve.tensor_scalar(small[:, 7 + i:8 + i], small[:, 6:7], float(SLOTS * i), small[:, 6 + i:7 + i],
                                       ALU.is_gt, ALU.add))
            dve.tensor_copy(sweeps_i[:, :], small[:, 10:11]).then_inc(sweeps_ready, 1)

            def choose(e):
                for t in range(NT):
                    last = dve.tensor_scalar(pick[:, t, :], iota[:, 0:SLOTS], pos[:, t, ds(e, 1)], None, ALU.is_equal)
                last.then_inc(pick_ready, 1)

            def choose_weighted(e):
                for t in range(NT):
                    last = dve.tensor_scalar(pick_w[:, t, :], iota, pos[:, t, ds(e, 1)], wt[:, t, ds(e, 1)],
                                             ALU.is_equal, ALU.mult)
                last.then_inc(pick_w_ready, 1)

            def mark(e):
                dve.tensor_scalar(hot[:, :], ones96[:, :], const[0:96, ds(C_HOT + e, 1)], None, ALU.mult).then_inc(hot_ready, 1)

            dve.memset(y_e[:, :], 0.0).then_inc(y_ready, 1)
            dve.memset(back[:, :, :], 0.0).then_inc(back_ready, 1)
            choose(0)
            dve.wait_ge(bias_split, 1)
            mark(0)
            choose_weighted(0)
            dve.memset(small[:, 12:13], 0.0).then_inc(up_read, 1)
            dve.wait_ge(sweeps_ready, 1)
            sweeps = dve.value_load(sweeps_i[0:1, 0:1], min_val=1, max_val=S // SLOTS)
            with dve.Fori(0, sweeps) as s:
                with dve.Fori(0, E) as e:
                    now = dve.snap(s * E + e + 1)
                    nxt = dve.snap(now + 1)
                    dve.wait_ge(gathered, now)
                    choose(e + 1)
                    dve.wait_ge(up_done, now)
                    for n in range(2):
                        hid = banks[n][:, :].rearrange("p (j c) -> p j c", c=2)
                        last = dve.tensor_scalar(glu[:, S * n:S * (n + 1)], hid[:, :, 0], LIMIT, None, ALU.min)
                    last.then_inc(glu_ready, 1)
                    for n in range(2):
                        hid = banks[n][:, :].rearrange("p (j c) -> p j c", c=2)
                        last = dve.tensor_scalar(lin[:, S * n:S * (n + 1)], hid[:, :, 1], LIMIT, -LIMIT, ALU.min, ALU.max)
                    last.then_inc(up_read, 1)
                    dve.wait_ge(up_read, nxt)
                    dve.scalar_tensor_tensor(out=lin, in0=lin, scalar=1.0, in1=glu, op0=ALU.add, op1=ALU.mult)\
                        .then_inc(act_ready, 1)
                    dve.wait_ge(act_ready, now)
                    dve.wait_ge(sig_ready, now)
                    dve.tensor_tensor(glu, lin, sig, ALU.mult).then_inc(hid_ready, 1)
                    dve.wait_ge(turned, now)
                    dve.wait_ge(scattered, now)
                    for g in range(2):
                        last = dve.tensor_copy(back[64 * g:64 * g + SLOTS, g, :], banks[2][64 * g:64 * g + SLOTS, 0:S])
                    last.then_inc(back_ready, 1)
                    choose_weighted(e + 1)
                    dve.wait_ge(hot_used, now)
                    mark(e + 1)
                dve.wait_ge(pick_w_ready, s * E + E + 1)
                dve.tensor_scalar(pos[:, :, :], pos[:, :, :], -float(SLOTS), None, ALU.add).then_inc(pos_moved, 1)
                dve.wait_ge(pos_moved, s + 1)
            dve.wait_ge(all_added, 1)
            for t in range(NT):
                variance(6 + t, [banks[4 + 2 * t + g][:, :] for g in range(2)])
            for t in range(NT):
                shift(6 + t)
            dve.wait_ge(gb_b_in, 64)
            for t in range(NT):
                gain(6 + t, gb_b)


_INS = ["x", "mem", "w_in", "diff_lambda_q1", "diff_lambda_k1", "diff_lambda_q2", "diff_lambda_k2", "diff_subln_g",
        "w_mix_out", "ln1_g", "ln1_b", "mem_ln_g", "mem_ln_b", "w_mem_q", "w_mem_kv", "w_mem_o", "ln2_g", "ln2_b",
        "w_router", "b_router", "w_mlp1", "b_mlp1", "w_mlp2", "b_mlp2", "ln3_g", "ln3_b"]


def kernel(**inputs):
    import concourse.bacc as _bacc
    from concourse.bass_utils import run_bass_kernel_spmd as _run

    nc = _bacc.Bacc("TRN2", target_bir_lowering=False, num_devices=1)
    arrays, args = {}, {}
    for name in _INS:
        x = np.ascontiguousarray(inputs[name])
        arrays[f"in_{name}"] = x
        args[name] = nc.dram_tensor(f"in_{name}", x.shape, mybir.dt.from_np(x.dtype), kind="ExternalInput").ap()
    c = shape_constants()
    arrays["in_const"] = c
    args["const"] = nc.dram_tensor("in_const", c.shape, F32, kind="ExternalInput").ap()
    args["out"] = nc.dram_tensor("out", (1, S, D), F32, kind="ExternalOutput").ap()
    decoder_layer(nc, args)
    return _run(nc, [arrays], core_ids=[0]).results[0]["out"]
```

```python
from contextlib import ExitStack
import math

import numpy as np

import concourse.bass as bass
from concourse import mybir

F32 = mybir.dt.float32
F32R = mybir.dt.float32r
BF16 = mybir.dt.bfloat16
I32 = mybir.dt.int32
ALU = mybir.AluOpType
ACT = mybir.ActivationFunctionType
AX = mybir.AxisListType
ds = bass.ds

P = 128
D = 1024
S = 256
NT = S // P
KC = D // P
HD = 64
MAPS = 16
GROUP = 4
SEG = 3 * P
SCALE = HD ** -0.5
MEM_HEADS = 4
MEM_SCALE = (D // MEM_HEADS) ** -0.5
ROT = 8
E = 32
TOPK = 4
SLOTS = 64
FF = 1024
LIMIT = 7.0
SW_ALPHA = 1.702
EPS = 1e-5
ALPHA = 2.0 ** 0.25
LAMBDA_INIT = 0.2
BIG = 1e30

PIECES = 12
NSLOT = 20
PEELED = 4
STEADY = PIECES * PEELED % NSLOT
LAG = PEELED - PIECES * PEELED // NSLOT - 1
assert STEADY + PIECES == NSLOT
PLACE = [12, 16, 8, 9, 14, 17, 10, 11, 13, 15, 7, 5, 6, 4, 0, 1, 2, 3, 18, 19]

UNITS = 4
RAW = 6
SPLIT = 5

EARLY_UNIT = 35

BY_TILE = [(t, q) for t in range(NT) for q in range(2)]
BY_HALF = [(t, q) for q in range(2) for t in range(NT)]

C_ID, C_MASK, C_TRI, C_IOTA, C_HOT, C_COS, C_SIN = 0, 128, 512, 640, 768, 801, 817
C_END = 833

BLOCKS = [("in", b) for b in range(6)] + [("kv", 0), ("kv", 1), ("out", 0), ("out", 1), ("kv", 2),
                                          ("q", 0), ("q", 1), ("kv", 3), ("o", 0), ("o", 1)]


def shape_constants():
    c = np.zeros((P, C_END), np.float32)
    row, col = np.arange(P)[:, None], np.arange(P)[None, :]
    c[:, C_ID:C_ID + P] = row == col
    causal = np.where(col <= row, 0.0, -BIG)
    c[:, C_MASK:C_MASK + P] = causal
    c[:, C_MASK + 2 * P:C_MASK + 3 * P] = causal
    c[:, C_TRI:C_TRI + P] = row < col
    c[:, C_IOTA:C_IOTA + P] = np.arange(P) % SLOTS
    c[:, C_HOT:C_HOT + E + 1] = (row % E) == (np.arange(E + 1) % E)
    inv = (np.float32(500000.0) ** (-np.arange(0, 2 * ROT, 2, dtype=np.float32) / np.float32(2 * ROT))).astype(np.float32)
    ang = np.arange(S, dtype=np.float32)[:, None] * inv[None, :]
    for t in range(NT):
        c[:, C_COS + ROT * t:C_COS + ROT * (t + 1)] = np.cos(ang[P * t:P * (t + 1)])
        c[:, C_SIN + ROT * t:C_SIN + ROT * (t + 1)] = np.sin(ang[P * t:P * (t + 1)])
    return c


def plan_banks():
    jobs = [("xT", t, q) for q in range(2) for t in range(NT)]
    jobs += [(k, t) for k in ("dq", "dk", "dv") for t in range(NT)]
    jobs += [(k, t) for k in ("Tdq", "Tdk") for t in range(NT)]
    jobs += [("memT", t, q) for t in range(NT) for q in range(2)]
    jobs += [("S", m) for m in range(8)]
    jobs += [(k, t) for k in ("mq", "mk") for t in range(NT)]
    jobs += [("TA", 0), ("TA", 1), ("PV", 0), ("TA", 2), ("PV", 1), ("TA", 3), ("PV", 2), ("PV", 3)]
    jobs += [("mv", t) for t in range(NT)]
    jobs += [(k, t) for k in ("Tmq", "Tmk") for t in range(NT)]
    jobs += [("kmT", 0, j) for j in range(4)]
    jobs += [("S", m) for m in range(8, 16)]
    jobs += [("kmT", 1, j) for j in range(4)]
    jobs += [("TA", 4), ("oT", 0, 0), ("oT", 1, 0)]
    for m in range(4, 12):
        jobs += ([("TA", m + 1)] if m < 11 else []) + [("PV", m)]
    jobs += [("oT", 0, 1), ("oT", 1, 1)]
    jobs += [("mix", cb, t) for cb in range(2) for t in range(NT)]
    jobs += [("vm", 0, t) for t in range(NT)]
    jobs += [("h1T", t, q) for t in range(NT) for q in range(2)]
    jobs += [("qmT", cb, j) for cb in range(2) for j in range(4)]
    jobs += [("MS", h) for h in range(MEM_HEADS)]
    jobs += [("vm", 1, t) for t in range(NT)]
    jobs += [("TP", 0)]
    for h in range(MEM_HEADS):
        jobs += ([("TP", h + 1)] if h < 3 else []) + [("PM", h)]
    jobs += [("mo", cb, t) for cb in range(2) for t in range(NT)]
    plan, used = {}, [0] * 8
    for n, name in enumerate(jobs):
        plan[name] = (n % 8, used[n % 8])
        used[n % 8] += 1
    late = [("h2T", 0, 0), ("h2T", 0, 1), ("lgT", 0), ("h2T", 1, 0), ("h2T", 1, 1), ("lgT", 1), ("lg",), ("rank",)]
    for n, name in enumerate(late):
        plan[name] = (n % 4, used[n % 4])
        used[n % 4] += 1
    for b, (t, g) in enumerate((t, g) for t in range(NT) for g in range(2)):
        plan[("Y", t, g)] = (4 + b, used[4 + b])
    return plan, used


def decoder_layer(nc, a):
    plan, bank_jobs = plan_banks()
    w_dram = {"in": a["w_in"][0], "kv": a["w_mem_kv"][0], "out": a["w_mix_out"][0],
              "q": a["w_mem_q"][0], "o": a["w_mem_o"][0]}

    with ExitStack() as ctx:
        def sb(name, shape, dt=F32):
            return ctx.enter_context(nc.sbuf_tensor(name, shape, dt))

        def sem(name):
            return ctx.enter_context(nc.semaphore(name))

        banks = [ctx.enter_context(nc.psum_tensor(f"bank{i}", [P, 512], F32)) for i in range(8)]

        ring = sb("ring", [P, NSLOT, 2048])
        ring_at = nc.sbuf_base - (NSLOT) * 8192

        def at_place(name, shape, dt, place):
            return nc.alloc_sbuf_tensor_at(name, shape, dt, offset=ring_at + int(8192 * place))

        w_split = at_place("w_split", [P, SPLIT, 2, 2, 512], F32R, 0)
        w_raw = at_place("w_raw", [P, RAW, 2, 512], F32, 5)
        left = at_place("left", [P, 2, KC, S], F32R, 8)
        left_m = at_place("left_m", [P, 2, KC, S], F32R, 10)
        qk_raw = at_place("qk_raw", [P, NT, 2, 512], F32, 12)
        qz = at_place("qz", [P, 8, S], F32, 13)
        pmT = at_place("pmT", [P, MEM_HEADS, NT, S], F32, 13)
        qmT = at_place("qmT", [P, KC, S], F32, 17)
        kmT = at_place("kmT", [P, KC, S], F32, 14)
        vm = at_place("vm", [P, NT, D], F32, 15)
        bias_f = at_place("bias_f", [96, 3 * D], F32, 14)
        kT = at_place("kT", [P, 4, S], F32, 16)
        mem_o = at_place("mem_o", [P, NT, D], F32, 17)
        gb = at_place("gb", [P, 2, D], F32, 18)
        h = at_place("h", [P, NT, D], F32, 19)

        v = sb("v", [P, NT, D])
        v_flat = v[:, :, :].rearrange("p t n -> p (t n)")
        pm = v_flat.rearrange("p (h t n) -> p h t n", h=MEM_HEADS, t=NT)
        h2T = v_flat.rearrange("p (c n) -> p c n", c=KC)
        work = sb("work", [P, 2 * GROUP * SEG + 1536])
        left_o = nc.alloc_sbuf_tensor_at("left_o", [P, 2, KC, S], F32R, offset=nc.sbuf_base - 4 * (2 * GROUP * SEG + 1536))
        scores = work[:, 0:2 * GROUP * SEG].rearrange("p (a b c) -> p a b c", a=2, b=GROUP)
        h_parts = work[:, 0:2 * GROUP * SEG].bitcast(BF16).rearrange(
            "p (t j n) -> p t j n", t=NT, j=3)
        hidden = v_flat.rearrange("p (a n) -> p a n", a=4)
        glu, sig, lin, hidT = (hidden[:, i, :] for i in range(4))
        shared = work[:, 2 * GROUP * SEG:]
        aT = shared.rearrange("p (j n) -> p j n", j=GROUP)
        x_e = shared[:, 0:512].rearrange("p (c n) -> p c n", c=KC)
        y_e = shared[:, 512:1024]
        back = shared[:, 1024:1536].rearrange("p (g n) -> p g n", g=2)

        bias_parts = sb("bias_parts", [96, 3 * D], BF16)
        pick_w = sb("pick_w", [P, NT, P])
        pick = sb("pick", [P, NT, SLOTS], BF16)
        hot = sb("hot", [96, SLOTS], BF16)
        ones96 = sb("ones96", [96, SLOTS])
        const = sb("const", [P, C_END])
        tri_b = sb("tri_b", [P, P], BF16)
        ones_b = sb("ones_b", [P, P], BF16)
        diag = sb("diag", [P, P])
        w_router = sb("w_router", [P, KC, E])
        b_router = sb("b_router", [E, 1])
        sub_g = sb("sub_g", [P, P])
        lam_in = sb("lam_in", [P, 4, HD])
        lam = sb("lam", [P, 8])
        rope_tmp = sb("rope_tmp", [P, 4, NT, 8, ROT])
        stats = sb("stats", [P, 8, 2, 6])
        mv_ln = sb("mv_ln", [P, 8, 2])
        ln_s = sb("ln_s", [P, 8, 2])
        half = sb("half", [P, 8])
        top_max = sb("top_max", [P, 4, 2, GROUP])
        sums = sb("sums", [P, 4, 2, GROUP])
        recips = sb("recips", [P, 4, 2, GROUP])
        rms = sb("rms", [P, 3, 8])
        mem_s = sb("mem_s", [P, 4, MEM_HEADS, 2])
        lgT = sb("lgT", [E, S])
        lg = sb("lg", [P, NT, E])
        best = sb("best", [P, NT, 8])
        route = sb("route", [P, 4, NT, E])
        mask_b = sb("mask_b", [P, NT, E], BF16)
        small = sb("small", [P, 16])
        sweeps_i = sb("sweeps_i", [P, 1], I32)
        pos = sb("pos", [P, NT, E + 1])
        wt = sb("wt", [P, NT, E + 1])
        square = sb("square", [P, P])

        ident = const[:, C_ID:C_ID + P]
        mask = const[:, C_MASK:C_MASK + SEG]
        iota = const[:, C_IOTA:C_IOTA + P]

        filled = [sem(f"bank_filled{i}") for i in range(8)]
        drained = [sem(f"bank_drained{i}") for i in range(8)]
        x_in = [sem(f"x_in{q}") for q in range(2)]
        mem_in = [sem(f"mem_in{t}") for t in range(NT)]
        ident_in, const_in = sem("ident_in"), sem("const_in")
        gb_in, last_gb_in = sem("gb_in"), sem("last_gb_in")
        small_in, bias_in, router_in = sem("small_in"), sem("bias_in"), sem("router_in")
        unit_in = [sem(f"unit_in{i}") for i in range(RAW)]
        high_ready, low_ready = sem("high_ready"), sem("low_ready")
        unit_used = sem("unit_used")
        left_high = sem("left_high")
        qz_zeroed, bias_split = sem("qz_zeroed"), sem("bias_split")
        pool_step, dve_step = sem("pool_step"), sem("dve_step")
        var_ready, rstd_ready, ln_ready = sem("var_ready"), sem("rstd_ready"), sem("ln_ready")
        lam_sums, lam_exp = sem("lam_sums"), sem("lam_exp")
        roped, max_ready, exp_ready, mixed = sem("roped"), sem("max_ready"), sem("exp_ready"), sem("mixed")
        squared, rms_var, rms_rstd = sem("squared"), sem("rms_var"), sem("rms_rstd")
        o_ready = sem("o_ready")
        mem_max, pm_ready = sem("mem_max"), sem("pm_ready")
        best_ready, route_exp, mask_ready = sem("best_ready"), sem("route_exp"), sem("mask_ready")
        part_ready, rest_ready, prepared = sem("part_ready"), sem("rest_ready"), sem("prepared")
        sweeps_ready = sem("sweeps_ready")
        piece_in = [sem(f"piece_in{i}") for i in range(NSLOT)]
        pieces_used = sem("pieces_used")
        hot_ready, hot_used = sem("hot_ready"), sem("hot_used")
        pick_ready, pick_w_ready = sem("pick_ready"), sem("pick_w_ready")
        gathered, x_e_ready = sem("gathered"), sem("x_e_ready")
        up_done, up_read = sem("up_done"), sem("up_read")
        glu_ready, sig_ready, act_ready, hid_ready = sem("glu_ready"), sem("sig_ready"), sem("act_ready"), sem("hid_ready")
        turned, back_ready, scattered = sem("turned"), sem("back_ready"), sem("scattered")
        hid_turned, hidT_ready = sem("hid_turned"), sem("hidT_ready")
        down_done, y_ready = sem("down_done"), sem("y_ready")
        pos_moved, all_added = sem("pos_moved"), sem("all_added")
        out_written = sem("out_written")

        def bank_for(pe, *name):
            b, n = plan[name]
            if n:
                pe.wait_ge(drained[b], n)
            return banks[b]

        def filled_by(*name):
            return filled[plan[name][0]]

        def drained_by(*name):
            return drained[plan[name][0]]

        def wait_filled(eng, *name):
            b, n = plan[name]
            eng.wait_ge(filled[b], n + 1)
            return banks[b]

        def wait_drained(eng, *name):
            b, n = plan[name]
            eng.wait_ge(drained[b], n + 1)

        last_job = [("dq", 1), ("dk", 1), ("dv", 1), ("mq", 1), ("mk", 1), ("mv", 1), ("kmT", 0, 3), ("kmT", 1, 3),
                    ("mix", 0, 1), ("mix", 1, 1), ("vm", 0, 1), ("qmT", 0, 3), ("qmT", 1, 3), ("vm", 1, 1),
                    ("mo", 0, 1), ("mo", 1, 1)]

        def wait_unit_used(eng, u):
            blk, q = u // UNITS, u % UNITS
            if q < UNITS - 1:
                eng.wait_ge(unit_used, (UNITS - 1) * blk + q + 1)
            else:
                wait_filled(eng, *last_job[blk])

        def expert_src(e, k):
            if k < KC:
                return a["w_mlp1"][0, ds(e, 1), P * k:P * (k + 1), :].rearrange("a p n -> p (a n)")
            r = 2 * P * (k - KC)
            return a["w_mlp2"][0, ds(e, 1), r:r + 2 * P, :].rearrange("a (c p) n -> p (a c) n", c=2)

        def slot(k):
            return ring[:, PLACE[k], :]

        block = ctx.enter_context(nc.Block())

        @block.sync
        def _(sp):
            sp.dma_start(const[:, C_ID:C_ID + P], a["const"][:, C_ID:C_ID + P]).then_inc(ident_in, 16)
            for q in range(2):
                for t in range(NT):
                    sp.dma_start(h[:, t, 512 * q:512 * (q + 1)], a["x"][0, P * t:P * (t + 1), 512 * q:512 * (q + 1)])\
                        .then_inc(x_in[q], 16)
            def free_place(place):
                if place < SPLIT:
                    last = UNITS * len(BLOCKS) - 1
                    wait_unit_used(sp, last - (last - place) % SPLIT)
                elif place < 8:
                    last = UNITS * len(BLOCKS)
                    sp.wait_ge(low_ready, last - (last - 2 - 2 * (place - SPLIT)) % RAW)
                elif place < 10:
                    wait_filled(sp, "qmT", 1, 3)
                elif place < 12:
                    wait_filled(sp, "vm", 1, 1)
                elif place == 12:
                    wait_filled(sp, "Tmk", 1)
                elif place == 13 or place == 15:
                    wait_filled(sp, "PM", 3)
                elif place == 14 or place == 17:
                    wait_filled(sp, "MS", 3)
                elif place == 16:
                    wait_filled(sp, "S", 15)
                elif place == 18:
                    sp.wait_ge(ln_ready, 12)
                else:
                    sp.wait_ge(part_ready, 6)
                    wait_filled(sp, "rank")

            def load(e, k, at):
                dst = slot(at) if k < KC else slot(at).rearrange("p (c n) -> p c n", c=2)
                sp.dma_start(dst, expert_src(e, k)).then_inc(piece_in[at], 16)

            def wait_piece_used(before, k):
                if k == KC - 1:
                    sp.wait_ge(up_done, before + 1)
                elif k == PIECES - 1:
                    sp.wait_ge(down_done, before + 1)
                else:
                    sp.wait_ge(pieces_used, before * (PIECES - 2) + (k + 1 if k < KC else k))

            def prefetch(slots):
                for at in slots:
                    free_place(PLACE[at])
                    load(at // PIECES, at % PIECES, at)

            for u in range(UNITS * len(BLOCKS)):
                tensor, cb = BLOCKS[u // UNITS]
                if u >= RAW:
                    sp.wait_ge(low_ready, u - RAW + 1)
                q = u % UNITS
                src = w_dram[tensor][256 * q:256 * (q + 1), 512 * cb:512 * (cb + 1)]
                sp.dma_start(w_raw[:, u % RAW, :, :], src.rearrange("(c p) n -> p c n", c=2)).then_inc(unit_in[u % RAW], 16)
                if u == RAW - 1:
                    sp.dma_start(const[:, C_ID + P:C_END], a["const"][:, C_ID + P:C_END]).then_inc(const_in, 16)
                if u == EARLY_UNIT:
                    prefetch(range(2))
            prefetch(range(2, NSLOT))

            for n in range(NSLOT, PIECES * (PEELED + 1)):
                wait_piece_used((n - NSLOT) // PIECES, (n - NSLOT) % PIECES)
                load(n // PIECES, n % PIECES, n % NSLOT)

            def load_expert(e, before):
                for k in range(PIECES):
                    wait_piece_used(before, k)
                    load(e, k, STEADY + k)

            with sp.Fori(PEELED + 1, E) as e:
                load_expert(e, sp.snap(e - 1))
            sp.wait_ge(sweeps_ready, 1)
            sweeps = sp.value_load(sweeps_i[0:1, 0:1], min_val=1, max_val=S // SLOTS)
            with sp.If(sweeps > 1):
                with sp.Fori(1, sweeps) as s:
                    with sp.Fori(0, E) as e:
                        load_expert(e, sp.snap(s * E + e - 1))
            sp.wait_ge(down_done, sp.snap(sweeps * E))
            for i, name in enumerate(("ln3_g", "ln3_b")):
                sp.dma_start(gb[:, i, :], a[name].broadcast_to([P, D])).then_inc(last_gb_in, 16)
            for t in range(NT):
                for q in range(2):
                    sp.wait_ge(ln_ready, 12 + 2 * t + q + 1)
                    sp.dma_start(a["out"][0, P * t:P * (t + 1), 512 * q:512 * (q + 1)], h[:, t, 512 * q:512 * (q + 1)])\
                        .then_inc(out_written, 16)
            sp.wait_ge(out_written, 16 * 2 * NT)

        @block.gpsimd
        def _(pool):
            steps = [0]

            def step(ins):
                steps[0] += 1
                ins.then_inc(pool_step, 1)
                pool.wait_ge(pool_step, steps[0])

            def row(ap):
                return ap.broadcast_to([P, ap.shape[1]])

            for t in range(NT):
                pool.dma_start(mem_o[:, t, :], a["mem"][0, P * t:P * (t + 1), :]).then_inc(mem_in[t], 16)

            def load_gains(gain, bias):
                pool.dma_start(gb[:, 0, :], row(gain)).then_inc(gb_in, 16)
                pool.dma_start(gb[:, 1, :], row(bias)).then_inc(gb_in, 16)

            load_gains(a["mem_ln_g"].rearrange("(a n) -> a n", a=1), a["mem_ln_b"].rearrange("(a n) -> a n", a=1))
            step(pool.memset(half[:, :], -0.5))
            pool.memset(qz[:, :, :], 0.0).then_inc(qz_zeroed, 1)
            for i, name in enumerate(("diff_lambda_q1", "diff_lambda_q2", "diff_lambda_k1", "diff_lambda_k2")):
                pool.dma_start(lam_in[:, i, :], row(a[name])).then_inc(small_in, 16)
            pool.dma_start(sub_g[:, :], row(a["diff_subln_g"])).then_inc(small_in, 16)
            for i in range(3):
                pool.dma_start(bias_f[E * i:E * (i + 1), 0:2 * FF], a["b_mlp1"][0]).then_inc(bias_in, 16)
                pool.dma_start(bias_f[E * i:E * (i + 1), 2 * FF:3 * FF], a["b_mlp2"][0]).then_inc(bias_in, 16)
            pool.dma_start(w_router[:, :, :], a["w_router"][0].rearrange("(c p) e -> p c e", c=KC)).then_inc(router_in, 16)
            pool.dma_start(b_router[:, :], a["b_router"].rearrange("a e -> e a")).then_inc(router_in, 16)

            def inverse_root(n):
                pool.wait_ge(var_ready, n + 1)
                pool.tensor_tensor(ln_s[:, n, 1:2], ln_s[:, n, 0:1], half[:, 0:1], ALU.pow).then_inc(rstd_ready, 1)

            for n in range(2):
                inverse_root(n)
            pool.wait_ge(bias_in, 16 * 6)
            step(pool.tensor_copy(bias_parts[:, :], bias_f[:, :]))
            for i in (1, 2):
                lo = E * i
                while lo < 96:
                    step(pool.tensor_tensor(bias_f[lo:lo + E, :], bias_f[lo:lo + E, :], bias_parts[lo:lo + E, :], ALU.subtract))
                    step(pool.tensor_copy(bias_parts[lo:lo + E, :], bias_f[lo:lo + E, :]))
                    lo += E
            pool.memset(ones96[:, :], 1.0).then_inc(bias_split, 1)
            pool.wait_ge(ln_ready, 4)
            load_gains(a["ln1_g"], a["ln1_b"])
            pool.wait_ge(rms_var, 1)
            pool.tensor_tensor(rms[:, 2, :], rms[:, 1, :], half[:, :], ALU.pow).then_inc(rms_rstd, 1)
            for n in range(2, 4):
                inverse_root(n)
            pool.wait_ge(ln_ready, 8)
            load_gains(a["ln2_g"], a["ln2_b"])
            for n in range(4, 8):
                inverse_root(n)

        @block.tensor
        def _(pe):
            def turn_rows(name, src, t, q):
                b = bank_for(pe, name, t, q)
                for j in range(4):
                    c = 4 * q + j
                    last = pe.transpose(b[:, P * j:P * (j + 1)], src[:, t, P * c:P * (c + 1)], ident)
                last.then_inc(filled_by(name, t, q), 1)

            def turned_rows(name):
                def before(c):
                    if c % 4 == 0:
                        for t in range(NT):
                            wait_drained(pe, name, t, c // 4)
                return before

            def three_passes(out, stationary, moving, start, stop):
                pe.matmul(out, stationary[0], moving[0], start=start, stop=False)
                pe.matmul(out, stationary[1], moving[0], start=False, stop=False)
                return pe.matmul(out, stationary[0], moving[1], start=False, stop=stop)

            def weights(u, c, cols):
                return [w_split[:, u % SPLIT, part, c % 2, cols] for part in range(2)]

            def project_rows(blk, act_, names, before=None, by_tile=False):
                b = [bank_for(pe, *names[t]) for t in range(NT)]
                for tiles in ([[0], [1]] if by_tile else [[0, 1]]):
                    for c in range(KC):
                        u = UNITS * blk + c // 2
                        if tiles[0] == 0:
                            if c % 2 == 0:
                                pe.wait_ge(low_ready, u + 1)
                            if before:
                                before(c)
                        for t in tiles:
                            mm = three_passes(b[t][:, :], [act_[:, part, c, P * t:P * (t + 1)] for part in range(2)],
                                              weights(u, c, slice(0, 512)), c == 0, c == KC - 1)
                            if c == KC - 1:
                                mm.then_inc(filled_by(*names[t]), 1)
                        if c % 2 and c < KC - 1 and tiles[-1] == NT - 1:
                            mm.then_inc(unit_used, 1)

            def project_cols(blk, act_, name, cb, before=None):
                b = [bank_for(pe, name, cb, j) for j in range(4)]
                for c in range(KC):
                    u = UNITS * blk + c // 2
                    if c % 2 == 0:
                        pe.wait_ge(low_ready, u + 1)
                    if before:
                        before(c)
                    for j in range(4):
                        mm = three_passes(b[j][:, 0:S], weights(u, c, slice(P * j, P * (j + 1))),
                                          [act_[:, part, c, :] for part in range(2)], c == 0, c == KC - 1)
                        if c == KC - 1:
                            mm.then_inc(filled_by(name, cb, j), 1)
                    if c % 2 and c < KC - 1:
                        mm.then_inc(unit_used, 1)

            def turn_heads(kind, index):
                pe.wait_ge(roped, index + 1)
                for t in range(NT):
                    b = bank_for(pe, "T" + kind, t)
                    for j in range(4):
                        last = pe.transpose(b[:, P * j:P * (j + 1)], qk_raw[:, t, index % 2, P * j:P * (j + 1)], ident)
                    last.then_inc(filled_by("T" + kind, t), 1)

            def score(m):
                b = bank_for(pe, "S", m)
                pe.matmul(b[:, 0:P], qz[:, m % 8, 0:P], kT[:, m % 8 // 2, 0:P], start=True, stop=True)
                pe.matmul(b[:, P:SEG], qz[:, m % 8, P:S], kT[:, m % 8 // 2, :], start=True, stop=True)\
                    .then_inc(filled_by("S", m), 1)

            def probs_at(j):
                return (j // 2, 2 * (j % 2)) if j < 4 else (2 + (j - 4) // 4, (j - 4) % 4)

            def turn_probs(j):
                g, i = probs_at(j)
                if j < 4:
                    pe.wait_ge(mixed, g + 1)
                else:
                    pe.wait_ge(exp_ready, g + 1)
                b = bank_for(pe, "TA", j)
                for n in range(3):
                    last = pe.transpose(b[:, P * n:P * (n + 1)], scores[:, g % 2, i, P * n:P * (n + 1)], ident)
                last.then_inc(filled_by("TA", j), 1)

            def weigh(j):
                wait_drained(pe, "TA", j)
                b = bank_for(pe, "PV", j)
                col = P * j if j < 4 else 512 + P * ((j - 4) // 2)
                at = aT[:, j % GROUP, :]
                pe.matmul(b[:, 0:P], at[:, 0:P], v[:, 0, col:col + P], start=True, stop=True)
                pe.matmul(b[:, P:2 * P], at[:, P:2 * P], v[:, 0, col:col + P], start=True, stop=False)
                pe.matmul(b[:, P:2 * P], at[:, 2 * P:3 * P], v[:, 1, col:col + P], start=False, stop=True)\
                    .then_inc(filled_by("PV", j), 1)

            pe.wait_ge(ident_in, 16)
            for q in range(2):
                pe.wait_ge(x_in[q], 16 * NT)
                for t in range(NT):
                    turn_rows("xT", h, t, q)
            for i, kind in enumerate(("dq", "dk", "dv")):
                project_rows(i, left, ((kind, 0), (kind, 1)), turned_rows("xT") if i == 0 else None)
            turn_heads("dq", 0)
            turn_heads("dk", 1)
            pe.wait_ge(ln_ready, 4)
            for t in range(NT):
                for q in range(2):
                    turn_rows("memT", mem_o, t, q)
            for k in ("Tdq", "Tdk"):
                for t in range(NT):
                    wait_drained(pe, k, t)
            for m in range(8):
                score(m)
            project_rows(3, left, (("mq", 0), ("mq", 1)))
            project_rows(4, left, (("mk", 0), ("mk", 1)))
            for t in range(NT):
                wait_drained(pe, "dv", t)
            turn_probs(0)
            for j in range(4):
                if j < 3:
                    turn_probs(j + 1)
                weigh(j)
            project_rows(5, left, (("mv", 0), ("mv", 1)))
            turn_heads("mq", 2)
            turn_heads("mk", 3)
            project_cols(6, left_m, "kmT", 0, turned_rows("memT"))
            for k in ("Tmq", "Tmk"):
                for t in range(NT):
                    wait_drained(pe, k, t)
            for m in range(8, 16):
                score(m)
            project_cols(7, left_m, "kmT", 1)
            for t in range(NT):
                wait_drained(pe, "mv", t)
            turn_probs(4)
            pe.wait_ge(o_ready, 1)
            for t in range(NT):
                turn_rows("oT", mem_o, t, 0)
            for j in range(4, 12):
                if j < 11:
                    turn_probs(j + 1)
                weigh(j)
            pe.wait_ge(o_ready, 2)
            for t in range(NT):
                turn_rows("oT", mem_o, t, 1)
            project_rows(8, left, (("mix", 0, 0), ("mix", 0, 1)), turned_rows("oT"))
            project_rows(9, left, (("mix", 1, 0), ("mix", 1, 1)), by_tile=True)
            project_rows(10, left_m, (("vm", 0, 0), ("vm", 0, 1)))
            for t in range(NT):
                for q in range(2):
                    pe.wait_ge(ln_ready, 4 + 2 * t + q + 1)
                    turn_rows("h1T", h, t, q)
            project_cols(11, left, "qmT", 0, turned_rows("h1T"))
            project_cols(12, left, "qmT", 1)
            for cb in range(2):
                for j in range(4):
                    wait_drained(pe, "kmT", cb, j)
                    wait_drained(pe, "qmT", cb, j)
            for hd in range(MEM_HEADS):
                b = bank_for(pe, "MS", hd)
                for t in range(NT):
                    for i in range(2):
                        mm = pe.matmul(b[:, S * t:S * (t + 1)], qmT[:, 2 * hd + i, P * t:P * (t + 1)],
                                       kmT[:, 2 * hd + i, :], start=(i == 0), stop=(i == 1))
                mm.then_inc(filled_by("MS", hd), 1)
            project_rows(13, left_m, (("vm", 1, 0), ("vm", 1, 1)))

            def turn_mem_probs(hd):
                pe.wait_ge(pm_ready, hd + 1)
                b = bank_for(pe, "TP", hd)
                for mt in range(2):
                    for t in range(NT):
                        n = 2 * mt + t
                        last = pe.transpose(b[:, P * n:P * (n + 1)], pm[:, hd, t, P * mt:P * (mt + 1)], ident)
                last.then_inc(filled_by("TP", hd), 1)

            for cb in range(2):
                for t in range(NT):
                    wait_drained(pe, "vm", cb, t)
            turn_mem_probs(0)
            for hd in range(MEM_HEADS):
                if hd < 3:
                    turn_mem_probs(hd + 1)
                wait_drained(pe, "TP", hd)
                b = bank_for(pe, "PM", hd)
                for i in range(2):
                    c = 2 * hd + i
                    for mt in range(2):
                        mm = pe.matmul(b[:, S * i:S * (i + 1)], vm[:, mt, P * c:P * (c + 1)], pmT[:, hd, mt, :],
                                       start=(mt == 0), stop=(mt == 1))
                mm.then_inc(filled_by("PM", hd), 1)
            def mem_outputs(c):
                if c % 2 == 0:
                    wait_drained(pe, "PM", c // 2)
            project_rows(14, left_o, (("mo", 0, 0), ("mo", 0, 1)), mem_outputs)
            project_rows(15, left_o, (("mo", 1, 0), ("mo", 1, 1)), by_tile=True)

            pe.wait_ge(router_in, 32)

            def route(t):
                for q in range(2):
                    pe.wait_ge(ln_ready, 8 + 2 * t + q + 1)
                    turn_rows("h2T", h, t, q)
                for q in range(2):
                    wait_drained(pe, "h2T", t, q)
                b = bank_for(pe, "lgT", t)
                for c in range(KC):
                    mm = pe.matmul(b[0:E, 0:P], w_router[:, c, :], h2T[:, c, P * t:P * (t + 1)],
                                   start=(c == 0), stop=(c == KC - 1))
                mm.then_inc(filled_by("lgT", t), 1)

            def start_sum(t):
                for g in range(2):
                    b = bank_for(pe, "Y", t, g)
                    pe.matmul(b[:, :], diag[:, :], h[:, t, 512 * g:512 * (g + 1)], start=True, stop=False)

            pe.wait_ge(prepared, 1)
            route(0)
            start_sum(0)
            route(1)
            b = bank_for(pe, "lg")
            for t in range(NT):
                wait_drained(pe, "lgT", t)
                mm = pe.transpose(b[:, E * t:E * (t + 1)], lgT[:, P * t:P * (t + 1)], const[0:E, C_ID:C_ID + E])
            mm.then_inc(filled_by("lg"), 1)
            start_sum(1)
            pe.wait_ge(mask_ready, 1)
            b = bank_for(pe, "rank")
            pe.matmul(b[:, 0:E], tri_b[:, :], mask_b[:, 0, :], start=True, stop=True)
            pe.matmul(b[:, E:2 * E], ones_b[:, :], mask_b[:, 0, :], start=True, stop=False)
            pe.matmul(b[:, E:2 * E], tri_b[:, :], mask_b[:, 1, :], start=False, stop=True)
            pe.matmul(b[:, 2 * E:3 * E], ones_b[:, :], mask_b[:, 0, :], start=True, stop=False)
            pe.matmul(b[:, 2 * E:3 * E], ones_b[:, :], mask_b[:, 1, :], start=False, stop=True)\
                .then_inc(filled_by("rank"), 1)

            up, ty, xg = banks[0:2], banks[2], banks[3]
            acc = [[banks[4 + 2 * t + g] for g in range(2)] for t in range(NT)]
            for i in range(4):
                pe.wait_ge(drained[i], bank_jobs[i])

            def gather():
                for c in range(KC):
                    for n in range(6):
                        t, part = n // 3, n % 3
                        mm = pe.matmul(xg[:, SLOTS * c:SLOTS * (c + 1)], h_parts[:, t, part, P * c:P * (c + 1)],
                                       pick[:, t, :], start=(n == 0), stop=(n == 5))
                mm.then_inc(gathered, 1)

            def scatter(last):
                for t in range(NT):
                    for g in range(2):
                        mm = pe.matmul(acc[t][g][:, :], back[:, g, P * t:P * (t + 1)], y_e[:, :],
                                       start=False, stop=last)
                        if last:
                            mm.then_inc(all_added, 1)
                if not last:
                    mm.then_inc(scattered, 1)

            pe.wait_ge(part_ready, 6)
            pe.wait_ge(pick_ready, 1)
            gather()

            def exchange(now, nxt):
                pe.wait_ge(pick_w_ready, now)
                pe.wait_ge(y_ready, now)
                for t in range(NT):
                    mm = pe.transpose(ty[:, P * t:P * (t + 1)], pick_w[:, t, :], ident)
                mm.then_inc(turned, 1)
                pe.wait_ge(back_ready, now)
                scatter(False)
                pe.wait_ge(pick_ready, nxt)
                gather()

            def serve(now, nxt, piece, scatter_early=False):
                pe.wait_ge(hot_ready, now)
                pe.wait_ge(up_read, now)
                for n in range(2):
                    for g in range(2):
                        col = 1024 * g + 512 * n
                        pe.matmul(up[n][64 * g:64 * g + SLOTS, :], hot[:, :], bias_parts[:, col:col + 512],
                                  start=True, stop=False)
                pe.wait_ge(x_e_ready, now)
                for k in range(KC):
                    at = piece(k)
                    for n in range(2):
                        for g in range(2):
                            col = 1024 * g + 512 * n
                            mm = pe.matmul(up[n][64 * g:64 * g + SLOTS, :], x_e[:, k, :],
                                           slot(at)[:, col:col + 512], start=False, stop=(k == KC - 1))
                    mm.then_inc(pieces_used if k < KC - 1 else up_done, 1)
                    if k == 0 and scatter_early:
                        exchange(now, nxt)
                if not scatter_early:
                    exchange(now, nxt)
                pe.wait_ge(hid_ready, now)
                pe.wait_ge(back_ready, nxt)
                for q in range(4):
                    mm = pe.transpose(ty[:, P * q:P * (q + 1)], glu[:, P * q:P * (q + 1)], ident)
                mm.then_inc(hid_turned, 1)
                pe.wait_ge(hidT_ready, now)
                for g in range(2):
                    mm = pe.matmul(ty[64 * g:64 * g + SLOTS, :], hot[:, :],
                                   bias_parts[:, 2 * FF + 512 * g:2 * FF + 512 * (g + 1)], start=True, stop=False)
                mm.then_inc(hot_used, 1)
                for u in range(4):
                    at = piece(KC + u)
                    for i in range(2):
                        c = 2 * u + i
                        for g in range(2):
                            mm = pe.matmul(ty[64 * g:64 * g + SLOTS, :],
                                           hidT[:, P * (c % 4) + 64 * (c // 4):P * (c % 4) + 64 * (c // 4) + SLOTS],
                                           slot(at)[:, D * i + 512 * g:D * i + 512 * (g + 1)],
                                           start=False, stop=(c == KC - 1))
                    mm.then_inc(pieces_used if u < 3 else down_done, 1)

            def early_piece(e):
                def piece(k):
                    n = PIECES * e + k
                    pe.wait_ge(piece_in[n % NSLOT], 16 * (n // NSLOT + 1))
                    return n % NSLOT
                return piece

            def steady_piece(loads):
                def piece(k):
                    pe.wait_ge(piece_in[STEADY + k], loads)
                    return STEADY + k
                return piece

            for e in range(PEELED):
                serve(e + 1, e + 2, early_piece(e))
            with pe.Fori(PEELED, E - 1) as e:
                serve(pe.snap(e + 1), pe.snap(e + 2), steady_piece(pe.snap((e - LAG) * 16)))
            serve(E, E + 1, steady_piece((E - 1 - LAG) * 16), scatter_early=True)
            pe.wait_ge(sweeps_ready, 1)
            sweeps = pe.value_load(sweeps_i[0:1, 0:1], min_val=1, max_val=S // SLOTS)
            with pe.If(sweeps > 1):
                with pe.Fori(1, sweeps) as s:
                    with pe.Fori(0, E) as e:
                        now = pe.snap(s * E + e + 1)
                        serve(now, pe.snap(now + 1), steady_piece(pe.snap((now - 1 - LAG) * 16)))
            served = pe.snap(sweeps * E + 1)
            pe.wait_ge(y_ready, served)
            pe.wait_ge(back_ready, served)
            scatter(True)

        @block.scalar
        def _(act):
            def copy_rows(name, dst, tiles):
                for t, q in tiles:
                    b = wait_filled(act, name, t, q)
                    act.activation(dst[:, 4 * q:4 * q + 4, P * t:P * (t + 1)],
                                   b[:, :].rearrange("p (c n) -> p c n", c=4), ACT.Copy).then_inc(drained_by(name, t, q), 1)

            units = [0]

            def split(count):
                for _ in range(count):
                    u = units[0]
                    units[0] += 1
                    act.wait_ge(unit_in[u % RAW], 16 * (u // RAW + 1))
                    if u >= SPLIT:
                        wait_unit_used(act, u - SPLIT)
                    act.activation(w_split[:, u % SPLIT, 0], w_raw[:, u % RAW], ACT.Copy).then_inc(high_ready, 1)

            def split_rows(name, dst, tiles):
                for t, q in tiles:
                    b = wait_filled(act, name, t, q)
                    act.activation(dst[:, 0, 4 * q:4 * q + 4, P * t:P * (t + 1)],
                                   b[:, :].rearrange("p (c n) -> p c n", c=4), ACT.Copy).then_inc(left_high, 1)

            def copy_to(dst, *name):
                b = wait_filled(act, *name)
                act.activation(dst, b[:, 0:512], ACT.Copy).then_inc(drained_by(*name), 1)

            def copy_heads(kind):
                for t in range(NT):
                    b = wait_filled(act, "T" + kind, t)
                    src = b[:, :].rearrange("p (j n) -> p j n", j=4)
                    if kind[1] == "q":
                        to = qz[:, :, P * t:P * (t + 1)].rearrange("p (j c) n -> p j c n", c=2)
                        act.activation(to[0:HD, :, 0, :], src[0:HD], ACT.Copy)
                        act.activation(to[HD:P, :, 1, :], src[HD:P], ACT.Copy).then_inc(drained_by("T" + kind, t), 1)
                    else:
                        act.activation(kT[:, :, P * t:P * (t + 1)], src, ACT.Copy)\
                            .then_inc(drained_by("T" + kind, t), 1)

            def exps(g):
                act.wait_ge(max_ready, g + 1)
                for t in range(NT):
                    for i in range(GROUP):
                        at = scores[:, g % 2, i, 0:P] if t == 0 else scores[:, g % 2, i, P:SEG]
                        last = act.activation(at, at, ACT.Exp, bias=top_max[:, g, t, i:i + 1], scale=SCALE,
                                              accum_out=sums[:, g, t, i:i + 1])
                last.then_inc(exp_ready, 1)

            def copy_probs(j):
                b = wait_filled(act, "TA", j)
                if j >= GROUP:
                    wait_filled(act, "PV", j - GROUP)
                act.activation(aT[:, j % GROUP, :], b[:, 0:SEG], ACT.Copy).then_inc(drained_by("TA", j), 1)

            def copy_raw(index, kind):
                for t in range(NT):
                    copy_to(qk_raw[:, t, index, :], kind, t)

            def copy_cols(name, cb, dst):
                for j in range(4):
                    b = wait_filled(act, name, cb, j)
                    act.activation(dst[:, 4 * cb + j, :], b[:, 0:S], ACT.Copy).then_inc(drained_by(name, cb, j), 1)

            def split_pair(hd):
                b = wait_filled(act, "PM", hd)
                act.activation(left_o[:, 0, 2 * hd:2 * hd + 2, :], b[:, :].rearrange("p (c n) -> p c n", c=2), ACT.Copy)\
                    .then_inc(left_high, 1)

            split_rows("xT", left, BY_HALF)
            split(8)
            copy_raw(0, "dq")
            split(4)
            copy_raw(1, "dk")
            act.wait_ge(lam_sums, 1)
            act.activation(lam[:, 2:4], lam[:, 0:2], ACT.Exp).then_inc(lam_exp, 1)
            split(4)
            for t in range(NT):
                copy_to(v[:, t, 0:512], "dv", t)
            act.wait_ge(qz_zeroed, 1)
            copy_heads("dq")
            copy_heads("dk")
            split_rows("memT", left_m, BY_TILE)
            exps(0)
            split(2)
            exps(1)
            split(2)
            copy_raw(0, "mq")
            split(4)
            copy_raw(1, "mk")
            for j in range(4):
                copy_probs(j)
            split(4)
            for j in range(4):
                wait_drained(act, "PV", j)
                for t in range(NT):
                    if j or t:
                        act.wait_ge(squared, 2 * j + t)
                    act.activation(square[:, :], mem_o[:, t, P * j:P * (j + 1)], ACT.Square,
                                   accum_out=rms[:, 0, 4 * t + j:4 * t + j + 1]).then_inc(squared, 1)
            for t in range(NT):
                copy_to(v[:, t, 512:1024], "mv", t)
            copy_heads("mq")
            copy_heads("mk")
            split(4)
            act.wait_ge(bias_split, 1)
            copy_cols("kmT", 0, kmT)
            exps(2)
            exps(3)
            copy_probs(4)
            split_rows("oT", left, BY_HALF[0:NT])
            copy_cols("kmT", 1, kmT)
            split(4)
            for j in range(5, 12):
                copy_probs(j)
            split_rows("oT", left, BY_HALF[NT:])
            split(12)
            for t in range(NT):
                copy_to(vm[:, t, 0:512], "vm", 0, t)
            split_rows("h1T", left, BY_TILE)
            split(4)
            copy_cols("qmT", 0, qmT)
            split(4)
            copy_cols("qmT", 1, qmT)
            for hd in range(MEM_HEADS):
                b = wait_filled(act, "MS", hd)
                act.wait_ge(mem_max, hd + 1)
                for t in range(NT):
                    last = act.activation(pm[:, hd, t, :], b[:, S * t:S * (t + 1)], ACT.Exp,
                                          bias=mem_s[:, 1, hd, t:t + 1], scale=MEM_SCALE,
                                          accum_out=mem_s[:, 2, hd, t:t + 1])
                last.then_inc(drained_by("MS", hd), 1)
            split(4)
            for t in range(NT):
                copy_to(vm[:, t, 512:1024], "vm", 1, t)
            for hd in range(MEM_HEADS):
                copy_to(pmT[:, hd, :, :].rearrange("p t n -> p (t n)"), "TP", hd)
                if hd:
                    split_pair(hd - 1)
            split_pair(MEM_HEADS - 1)
            split(4)
            assert units[0] == UNITS * len(BLOCKS)
            copy_rows("h2T", h2T, [(0, 0), (0, 1)])
            act.wait_ge(router_in, 32)

            def logits(t):
                b = wait_filled(act, "lgT", t)
                act.activation(lgT[:, P * t:P * (t + 1)], b[0:E, 0:P], ACT.Identity, bias=b_router[:, 0:1], scale=1.0)\
                    .then_inc(drained_by("lgT", t), 1)

            def h_part(part, t):
                if part:
                    act.wait_ge(rest_ready, 2 * (part - 1) + t + 1)
                else:
                    act.wait_ge(ln_ready, 8 + 2 * (t + 1))
                    wait_filled(act, "mo", 1, 1)
                src = (v if part else h)[:, t, :]
                act.activation(h_parts[:, t, part, :], src, ACT.Copy).then_inc(part_ready, 1)

            logits(0)
            h_part(0, 0)
            copy_rows("h2T", h2T, [(1, 0)])
            h_part(0, 1)
            logits(1)
            h_part(1, 0)
            h_part(1, 1)
            act.wait_ge(best_ready, 1)
            for t in range(NT):
                last = act.activation(route[:, 2, t, :], lg[:, t, :], ACT.Exp, bias=small[:, t:t + 1], scale=1.0)
            last.then_inc(route_exp, 1)
            h_part(2, 0)
            h_part(2, 1)

            def take_tokens():
                act.activation(x_e[:, :, :], banks[3][:, :].rearrange("p (c n) -> p c n", c=KC), ACT.Copy)\
                    .then_inc(x_e_ready, 1)

            act.wait_ge(gathered, 1)
            take_tokens()
            act.wait_ge(sweeps_ready, 1)
            sweeps = act.value_load(sweeps_i[0:1, 0:1], min_val=1, max_val=S // SLOTS)
            with act.Fori(0, sweeps) as s:
                with act.Fori(0, E) as e:
                    now = act.snap(s * E + e + 1)
                    nxt = act.snap(now + 1)
                    act.wait_ge(glu_ready, now)
                    act.activation(sig, glu, ACT.Sigmoid, scale=SW_ALPHA).then_inc(sig_ready, 1)
                    act.wait_ge(gathered, nxt)
                    take_tokens()
                    act.wait_ge(hid_turned, now)
                    act.activation(hidT, banks[2][:, :], ACT.Copy).then_inc(hidT_ready, 1)
                    act.wait_ge(down_done, now)
                    act.activation(y_e[:, :], banks[2][:, :], ACT.Copy).then_inc(y_ready, 1)

        @block.vector
        def _(dve):
            steps = [0]

            def step(ins):
                steps[0] += 1
                ins.then_inc(dve_step, 1)
                dve.wait_ge(dve_step, steps[0])

            def copy_rows(name, dst, tiles):
                for t, q in tiles:
                    b = wait_filled(dve, name, t, q)
                    dve.tensor_copy(dst[:, 4 * q:4 * q + 4, P * t:P * (t + 1)],
                                    b[:, :].rearrange("p (c n) -> p c n", c=4)).then_inc(drained_by(name, t, q), 1)

            units, turns = [0], [0]

            def split(count):
                for _ in range(count):
                    u = units[0]
                    units[0] += 1
                    dve.wait_ge(high_ready, u + 1)
                    dve.tensor_tensor(w_split[:, u % SPLIT, 1], w_raw[:, u % RAW], w_split[:, u % SPLIT, 0].bitcast(F32),
                                      ALU.subtract).then_inc(low_ready, 1)

            def low_part(dst, src, high, *name):
                turns[0] += 1
                dve.wait_ge(left_high, turns[0])
                dve.tensor_tensor(dst, src, high.bitcast(F32), ALU.subtract).then_inc(drained_by(*name), 1)

            def split_rows(name, dst, tiles):
                for t, q in tiles:
                    b = wait_filled(dve, name, t, q)
                    at = (slice(4 * q, 4 * q + 4), slice(P * t, P * (t + 1)))
                    low_part(dst[:, 1, at[0], at[1]], b[:, :].rearrange("p (c n) -> p c n", c=4),
                             dst[:, 0, at[0], at[1]], name, t, q)

            def half_stats(n, q, src):
                return dve.bn_stats(stats[:, n, q, :], src)

            def variance(n):
                step(dve.bn_aggr(mv_ln[:, n, :], stats[:, n, :, :].rearrange("p a b -> p (a b)")))
                dve.tensor_scalar(ln_s[:, n, 0:1], mv_ln[:, n, 1:2], EPS, None, ALU.add).then_inc(var_ready, 1)

            def apply_norm(n, x, src):
                halves = [slice(0, 512), slice(512, D)]
                for q in range(2):
                    last = dve.scalar_tensor_tensor(out=x[:, halves[q]], in0=src[q], scalar=mv_ln[:, n, 0:1],
                                                    in1=gb[:, 0, halves[q]], op0=ALU.subtract, op1=ALU.mult)
                step(last)
                dve.wait_ge(rstd_ready, n + 1)
                for q in range(2):
                    dve.scalar_tensor_tensor(out=x[:, halves[q]], in0=x[:, halves[q]], scalar=ln_s[:, n, 1:2],
                                             in1=gb[:, 1, halves[q]], op0=ALU.mult, op1=ALU.add).then_inc(ln_ready, 1)

            def residual(name, cb, t):
                b = wait_filled(dve, name, cb, t)
                x = h[:, t, 512 * cb:512 * (cb + 1)]
                dve.scalar_tensor_tensor(out=x, in0=x, scalar=ALPHA, in1=b[:, :], op0=ALU.mult, op1=ALU.add)\
                    .then_inc(drained_by(name, cb, t), 1)

            def first_halves(n, name):
                for t in range(NT):
                    residual(name, 0, t)
                for t in range(NT):
                    wait_drained(dve, name, 0, t)
                    half_stats(n + t, 0, h[:, t, 0:512])

            def finish(n, name, t, gb_count):
                residual(name, 1, t)
                wait_drained(dve, name, 1, t)
                step(half_stats(n + t, 1, h[:, t, 512:1024]))
                variance(n + t)
                dve.wait_ge(gb_in, gb_count)
                apply_norm(n + t, h[:, t, :], [h[:, t, 0:512], h[:, t, 512:1024]])

            def rope(index, kinds):
                for t in range(NT):
                    wait_drained(dve, kinds, t)
                x = qk_raw[:, :, index % 2, :].rearrange("p t (h d) -> p t h d", h=8)
                x1, x2 = x[:, :, :, 0:ROT], x[:, :, :, ROT:2 * ROT]
                cos = const[:, C_COS:C_COS + 2 * ROT].rearrange("p (t a r) -> p t a r", t=NT, a=1).broadcast_to([P, NT, 8, ROT])
                sin = const[:, C_SIN:C_SIN + 2 * ROT].rearrange("p (t a r) -> p t a r", t=NT, a=1).broadcast_to([P, NT, 8, ROT])
                dve.tensor_tensor(rope_tmp[:, 0], x1, cos, ALU.mult)
                dve.tensor_tensor(rope_tmp[:, 1], x2, sin, ALU.mult)
                dve.tensor_tensor(rope_tmp[:, 2], x2, cos, ALU.mult)
                step(dve.tensor_tensor(rope_tmp[:, 3], x1, sin, ALU.mult))
                dve.tensor_tensor(x1, rope_tmp[:, 0], rope_tmp[:, 1], ALU.subtract)
                dve.tensor_tensor(x2, rope_tmp[:, 2], rope_tmp[:, 3], ALU.add).then_inc(roped, 1)
                dve.wait_ge(roped, index + 1)

            def mask_group(g):
                if g >= 2:
                    wait_filled(dve, "TA", 2 * (g - 2) + 1)
                for i in range(GROUP):
                    m = GROUP * g + i
                    b = wait_filled(dve, "S", m)
                    dve.tensor_tensor(scores[:, g % 2, i, :], b[:, 0:SEG], mask, ALU.add).then_inc(drained_by("S", m), 1)
                wait_drained(dve, "S", GROUP * g + GROUP - 1)
                dve.tensor_reduce(top_max[:, g, 0, :], scores[:, g % 2, :, 0:P], AX.X, ALU.max)
                step(dve.tensor_reduce(top_max[:, g, 1, :], scores[:, g % 2, :, P:SEG], AX.X, ALU.max))
                dve.tensor_scalar(top_max[:, g], top_max[:, g], -SCALE, None, ALU.mult).then_inc(max_ready, 1)

            def invert(g):
                dve.wait_ge(exp_ready, g + 1)
                step(dve.reciprocal(recips[:, g], sums[:, g]))

            def mix_group(g):
                invert(g)
                r1 = recips[:, g].rearrange("p t (j c) -> p t j c", c=2)[:, :, :, 1]
                step(dve.tensor_scalar(r1, r1, lam[:, 4:5], None, ALU.mult))
                parts = [(i, t, slice(0, P) if t == 0 else slice(P, SEG)) for i in (0, 2) for t in range(NT)]
                for i, t, at in parts:
                    p1 = scores[:, g % 2, i + 1, at]
                    last = dve.tensor_scalar(p1, p1, recips[:, g, t, i + 1:i + 2], None, ALU.mult)
                step(last)
                for i, t, at in parts:
                    p0 = scores[:, g % 2, i, at]
                    last = dve.scalar_tensor_tensor(out=p0, in0=p0, scalar=recips[:, g, t, i:i + 1],
                                                    in1=scores[:, g % 2, i + 1, at], op0=ALU.mult, op1=ALU.add)
                last.then_inc(mixed, 1)

            split_rows("xT", left, BY_HALF)
            split(5)
            for t in range(NT):
                dve.wait_ge(mem_in[t], 16)
                for q in range(2):
                    last = half_stats(t, q, mem_o[:, t, 512 * q:512 * (q + 1)])
                step(last)
                variance(t)
            split(3)
            dve.wait_ge(small_in, 16 * 5)
            step(dve.tensor_tensor(lam_in[:, 0:2, :], lam_in[:, 0:2, :], lam_in[:, 2:4, :], ALU.mult))
            dve.tensor_reduce(lam[:, 0:2], lam_in[:, 0:2, :], AX.X, ALU.add).then_inc(lam_sums, 1)
            dve.tensor_scalar(sub_g[:, :], sub_g[:, :], 1.0 - LAMBDA_INIT, None, ALU.mult)
            dve.wait_ge(const_in, 16)
            dve.tensor_copy(tri_b[:, :], const[:, C_TRI:C_TRI + P])
            dve.memset(ones_b[:, :], 1.0)
            dve.tensor_scalar(diag[:, :], ident, ALPHA, None, ALU.mult).then_inc(prepared, 1)
            split(4)
            rope(0, "dq")
            dve.wait_ge(gb_in, 32)
            for t in range(NT):
                apply_norm(t, mem_o[:, t, :], [mem_o[:, t, 0:512], mem_o[:, t, 512:1024]])
            dve.wait_ge(lam_exp, 1)
            step(dve.tensor_scalar(lam[:, 4:5], lam[:, 3:4], lam[:, 2:3], LAMBDA_INIT, ALU.subtract, ALU.subtract))
            split(4)
            rope(1, "dk")
            dve.wait_ge(prepared, 1)
            split_rows("memT", left_m, BY_TILE)
            mask_group(0)
            split(2)
            mask_group(1)
            split(2)
            mix_group(0)
            mix_group(1)
            rope(2, "mq")
            split(4)
            rope(3, "mk")
            for j in range(4):
                b = wait_filled(dve, "PV", j)
                dve.tensor_copy(mem_o[:, :, P * j:P * (j + 1)], b[:, 0:2 * P].rearrange("p (t n) -> p t n", t=NT))\
                    .then_inc(drained_by("PV", j), 1)
            split(4)
            dve.wait_ge(squared, 8)
            dve.tensor_scalar(rms[:, 1, :], rms[:, 0, :], 1.0 / P, EPS, ALU.mult, ALU.add).then_inc(rms_var, 1)
            dve.wait_ge(rms_rstd, 1)
            for t in range(NT):
                for j in range(4):
                    o = mem_o[:, t, P * j:P * (j + 1)]
                    last = dve.scalar_tensor_tensor(out=o, in0=o, scalar=rms[:, 2, 4 * t + j:4 * t + j + 1], in1=sub_g[:, :],
                                                    op0=ALU.mult, op1=ALU.mult)
            last.then_inc(o_ready, 1)
            split(4)
            mask_group(2)
            mask_group(3)
            split_rows("oT", left, BY_HALF[0:NT])
            split(4)
            invert(2)
            invert(3)
            for j in range(8):
                b = wait_filled(dve, "PV", 4 + j)
                for t in range(NT):
                    off = P * t + HD * (j % 2)
                    last = dve.tensor_scalar(mem_o[:, t, 512 + HD * j:512 + HD * (j + 1)], b[:, off:off + HD],
                                             recips[:, 2 + j // 4, t, j % 4:j % 4 + 1], None, ALU.mult)
                last.then_inc(drained_by("PV", 4 + j), 1)
            wait_drained(dve, "PV", 11)
            dve.memset(small[:, 8:16], 0.0).then_inc(o_ready, 1)
            split_rows("oT", left, BY_HALF[NT:])
            split(4)
            first_halves(2, "mix")
            split(1)
            finish(2, "mix", 0, 64)
            split(3)
            finish(2, "mix", 1, 64)
            split(1)
            split_rows("h1T", left, BY_TILE)
            dve.memset(back[:, :, :], 0.0).then_inc(back_ready, 1)
            split(11)
            for hd in range(MEM_HEADS):
                b = wait_filled(dve, "MS", hd)
                step(dve.tensor_reduce(mem_s[:, 0, hd, :], b[:, :].rearrange("p (t n) -> p t n", t=NT), AX.X, ALU.max))
                dve.tensor_scalar(mem_s[:, 1, hd, :], mem_s[:, 0, hd, :], -MEM_SCALE, None, ALU.mult).then_inc(mem_max, 1)
            for hd in range(MEM_HEADS):
                wait_drained(dve, "MS", hd)
                step(dve.reciprocal(mem_s[:, 3, hd, :], mem_s[:, 2, hd, :]))
                for t in range(NT):
                    last = dve.tensor_scalar(pm[:, hd, t, :], pm[:, hd, t, :], mem_s[:, 3, hd, t:t + 1], None, ALU.mult)
                last.then_inc(pm_ready, 1)
            split(4)
            for hd in range(MEM_HEADS):
                b = wait_filled(dve, "PM", hd)
                low_part(left_o[:, 1, 2 * hd:2 * hd + 2, :], b[:, :].rearrange("p (c n) -> p c n", c=2),
                         left_o[:, 0, 2 * hd:2 * hd + 2, :], "PM", hd)
            split(4)
            first_halves(4, "mo")
            for t in range(NT):
                finish(4, "mo", t, 96)
            copy_rows("h2T", h2T, [(1, 1)])
            dve.memset(y_e[:, :], 0.0).then_inc(y_ready, 1)

            def rest(part, t):
                dve.wait_ge(part_ready, 2 * part + t + 1)
                src = h if part == 0 else v
                dve.tensor_tensor(v[:, t, :], src[:, t, :], h_parts[:, t, part, :], ALU.subtract)\
                    .then_inc(rest_ready, 1)

            wait_filled(dve, "lgT", 1)
            for t in range(NT):
                rest(0, t)
            b = wait_filled(dve, "lg")
            dve.tensor_copy(lg[:, :, :], b[:, 0:2 * E].rearrange("p (t e) -> p t e", t=NT)).then_inc(drained_by("lg"), 1)
            wait_drained(dve, "lg")
            for t in range(NT):
                last = dve.max(best[:, t, :], lg[:, t, :])
            step(last)
            dve.tensor_scalar(small[:, 0:2], best[:, :, 0], -1.0, None, ALU.mult).then_inc(best_ready, 1)
            step(dve.memset(best[:, :, TOPK:8], 3e38))
            for t in range(NT):
                last = dve.match_replace(route[:, 0, t, :], best[:, t, :], lg[:, t, :], -BIG)
            step(last)
            step(dve.tensor_tensor(route[:, 1], route[:, 0], lg[:, :, :], ALU.not_equal))
            dve.tensor_copy(mask_b[:, :, :], route[:, 1]).then_inc(mask_ready, 1)
            rest(1, 0)
            rest(1, 1)
            dve.wait_ge(route_exp, 1)
            step(dve.tensor_tensor(route[:, 2], route[:, 2], route[:, 1], ALU.mult))
            step(dve.tensor_reduce(small[:, 2:4], route[:, 2], AX.X, ALU.add))
            step(dve.reciprocal(small[:, 4:6], small[:, 2:4]))
            for t in range(NT):
                last = dve.tensor_scalar(wt[:, t, 0:E], route[:, 2, t, :], small[:, 4 + t:5 + t], None, ALU.mult)
            step(last)
            step(dve.tensor_copy(wt[:, :, E:E + 1], wt[:, :, 0:1]))
            b = wait_filled(dve, "rank")
            step(dve.scalar_tensor_tensor(out=route[:, 3], in0=b[:, 0:2 * E].rearrange("p (t e) -> p t e", t=NT), scalar=1.0,
                                          in1=route[:, 1], op0=ALU.add, op1=ALU.mult))
            step(dve.tensor_scalar(pos[:, :, 0:E], route[:, 3], -1.0, None, ALU.add))
            step(dve.tensor_scalar(pos[:, :, E:E + 1], pos[:, :, 0:1], -float(SLOTS), None, ALU.add))
            dve.tensor_reduce(small[:, 6:7], b[:, 2 * E:3 * E], AX.X, ALU.max).then_inc(drained_by("rank"), 1)
            wait_drained(dve, "rank")
            step(dve.tensor_scalar(small[:, 8:9], small[:, 6:7], float(SLOTS), 1.0, ALU.is_gt, ALU.add))
            for i in (2, 3):
                step(dve.tensor_scalar(small[:, 7 + i:8 + i], small[:, 6:7], float(SLOTS * i), small[:, 6 + i:7 + i],
                                       ALU.is_gt, ALU.add))
            dve.tensor_copy(sweeps_i[:, :], small[:, 10:11]).then_inc(sweeps_ready, 1)

            def choose(e):
                for t in range(NT):
                    last = dve.tensor_scalar(pick[:, t, :], iota[:, 0:SLOTS], pos[:, t, ds(e, 1)], None, ALU.is_equal)
                last.then_inc(pick_ready, 1)

            def choose_weighted(e):
                for t in range(NT):
                    last = dve.tensor_scalar(pick_w[:, t, :], iota, pos[:, t, ds(e, 1)], wt[:, t, ds(e, 1)],
                                             ALU.is_equal, ALU.mult)
                last.then_inc(pick_w_ready, 1)

            def mark(e):
                dve.tensor_scalar(hot[:, :], ones96[:, :], const[0:96, ds(C_HOT + e, 1)], None, ALU.mult).then_inc(hot_ready, 1)

            choose(0)
            dve.wait_ge(bias_split, 1)
            mark(0)
            choose_weighted(0)
            dve.memset(small[:, 12:13], 0.0).then_inc(up_read, 1)
            dve.wait_ge(sweeps_ready, 1)
            sweeps = dve.value_load(sweeps_i[0:1, 0:1], min_val=1, max_val=S // SLOTS)
            with dve.Fori(0, sweeps) as s:
                with dve.Fori(0, E) as e:
                    now = dve.snap(s * E + e + 1)
                    nxt = dve.snap(now + 1)
                    dve.wait_ge(gathered, now)
                    choose(e + 1)
                    dve.wait_ge(up_done, now)
                    for n in range(2):
                        hid = banks[n][:, :].rearrange("p (j c) -> p j c", c=2)
                        last = dve.tensor_scalar(glu[:, S * n:S * (n + 1)], hid[:, :, 0], LIMIT, None, ALU.min)
                    last.then_inc(glu_ready, 1)
                    for n in range(2):
                        hid = banks[n][:, :].rearrange("p (j c) -> p j c", c=2)
                        last = dve.tensor_scalar(lin[:, S * n:S * (n + 1)], hid[:, :, 1], LIMIT, -LIMIT, ALU.min, ALU.max)
                    last.then_inc(up_read, 1)
                    dve.wait_ge(up_read, nxt)
                    dve.scalar_tensor_tensor(out=lin, in0=lin, scalar=1.0, in1=glu, op0=ALU.add, op1=ALU.mult)\
                        .then_inc(act_ready, 1)
                    dve.wait_ge(act_ready, now)
                    dve.wait_ge(sig_ready, now)
                    dve.tensor_tensor(glu, lin, sig, ALU.mult).then_inc(hid_ready, 1)
                    dve.wait_ge(turned, now)
                    dve.wait_ge(scattered, now)
                    for g in range(2):
                        last = dve.tensor_copy(back[64 * g:64 * g + SLOTS, g, :], banks[2][64 * g:64 * g + SLOTS, 0:S])
                    last.then_inc(back_ready, 1)
                    choose_weighted(e + 1)
                    dve.wait_ge(hot_used, now)
                    mark(e + 1)
                dve.wait_ge(pick_w_ready, s * E + E + 1)
                dve.tensor_scalar(pos[:, :, :], pos[:, :, :], -float(SLOTS), None, ALU.add).then_inc(pos_moved, 1)
                dve.wait_ge(pos_moved, s + 1)
            for t in range(NT):
                for q in range(2):
                    dve.wait_ge(all_added, 2 * t + q + 1)
                    last = half_stats(6 + t, q, banks[4 + 2 * t + q][:, :])
                step(last)
                variance(6 + t)
                dve.wait_ge(last_gb_in, 32)
                apply_norm(6 + t, h[:, t, :], [banks[4 + 2 * t + q][:, :] for q in range(2)])


_INS = ["x", "mem", "w_in", "diff_lambda_q1", "diff_lambda_k1", "diff_lambda_q2", "diff_lambda_k2", "diff_subln_g",
        "w_mix_out", "ln1_g", "ln1_b", "mem_ln_g", "mem_ln_b", "w_mem_q", "w_mem_kv", "w_mem_o", "ln2_g", "ln2_b",
        "w_router", "b_router", "w_mlp1", "b_mlp1", "w_mlp2", "b_mlp2", "ln3_g", "ln3_b"]


def kernel(**inputs):
    import concourse.bacc as _bacc
    from concourse.bass_utils import run_bass_kernel_spmd as _run

    nc = _bacc.Bacc("TRN2", target_bir_lowering=False, num_devices=1)
    arrays, args = {}, {}
    for name in _INS:
        x = np.ascontiguousarray(inputs[name])
        arrays[f"in_{name}"] = x
        args[name] = nc.dram_tensor(f"in_{name}", x.shape, mybir.dt.from_np(x.dtype), kind="ExternalInput").ap()
    c = shape_constants()
    arrays["in_const"] = c
    args["const"] = nc.dram_tensor("in_const", c.shape, F32, kind="ExternalInput").ap()
    args["out"] = nc.dram_tensor("out", (1, S, D), F32, kind="ExternalOutput").ap()
    decoder_layer(nc, args)
    return _run(nc, [arrays], core_ids=[0]).results[0]["out"]
```

```python
from contextlib import ExitStack
import math

import numpy as np

import concourse.bass as bass
from concourse import mybir

F32 = mybir.dt.float32
F32R = mybir.dt.float32r
BF16 = mybir.dt.bfloat16
I32 = mybir.dt.int32
ALU = mybir.AluOpType
ACT = mybir.ActivationFunctionType
AX = mybir.AxisListType
ds = bass.ds

P = 128
D = 1024
S = 256
NT = S // P
KC = D // P
HD = 64
MAPS = 16
GROUP = 4
SEG = 3 * P
SCALE = HD ** -0.5
MEM_HEADS = 4
MEM_SCALE = (D // MEM_HEADS) ** -0.5
ROT = 8
E = 32
TOPK = 4
SLOTS = 64
FF = 1024
LIMIT = 7.0
SW_ALPHA = 1.702
EPS = 1e-5
ALPHA = 2.0 ** 0.25
LAMBDA_INIT = 0.2
BIG = 1e30

PIECES = 12
NSLOT = 20
PEELED = 4
STEADY = PIECES * PEELED % NSLOT
LAG = PEELED - PIECES * PEELED // NSLOT - 1
assert STEADY + PIECES == NSLOT
PLACE = [12, 14, 13, 16, 17, 10, 11, 8, 9, 7, 15, 5, 6, 4, 0, 1, 2, 3, 18, 19]
EARLY = {35: 4, 43: 1, 58: 2}

UNITS = 4
RAW = 6
SPLIT = 5

BY_TILE = [(t, q) for t in range(NT) for q in range(2)]
BY_HALF = [(t, q) for q in range(2) for t in range(NT)]

C_ID, C_MASK, C_TRI, C_IOTA, C_HOT, C_COS, C_SIN = 0, 128, 512, 640, 768, 801, 817
C_END = 833

BLOCKS = [("in", b) for b in range(6)] + [("kv", 2), ("kv", 3), ("out", 0), ("out", 1), ("kv", 0), ("kv", 1),
                                          ("q", 0), ("q", 1), ("o", 0), ("o", 1)]


def shape_constants():
    c = np.zeros((P, C_END), np.float32)
    row, col = np.arange(P)[:, None], np.arange(P)[None, :]
    c[:, C_ID:C_ID + P] = row == col
    causal = np.where(col <= row, 0.0, -BIG)
    c[:, C_MASK:C_MASK + P] = causal
    c[:, C_MASK + 2 * P:C_MASK + 3 * P] = causal
    c[:, C_TRI:C_TRI + P] = row < col
    c[:, C_IOTA:C_IOTA + P] = np.arange(P) % SLOTS
    c[:, C_HOT:C_HOT + E + 1] = (row % E) == (np.arange(E + 1) % E)
    inv = (np.float32(500000.0) ** (-np.arange(0, 2 * ROT, 2, dtype=np.float32) / np.float32(2 * ROT))).astype(np.float32)
    ang = np.arange(S, dtype=np.float32)[:, None] * inv[None, :]
    for t in range(NT):
        c[:, C_COS + ROT * t:C_COS + ROT * (t + 1)] = np.cos(ang[P * t:P * (t + 1)])
        c[:, C_SIN + ROT * t:C_SIN + ROT * (t + 1)] = np.sin(ang[P * t:P * (t + 1)])
    return c


def plan_banks():
    jobs = [("xT", t, 0) for t in range(NT)] + [("dq", t) for t in range(NT)] + [("xT", t, 1) for t in range(NT)]
    jobs += [(k, t) for k in ("dk", "dv") for t in range(NT)]
    jobs += [(k, t) for k in ("Tdq", "Tdk") for t in range(NT)]
    jobs += [("memT", t, q) for t in range(NT) for q in range(2)]
    jobs += [("S", m) for m in range(8)]
    jobs += [(k, t) for k in ("mq", "mk", "mv") for t in range(NT)]
    jobs += [("TA", 0), ("TA", 1), ("PV", 0), ("TA", 2), ("PV", 1), ("TA", 3), ("PV", 2), ("PV", 3)]
    jobs += [(k, t) for k in ("Tmq", "Tmk") for t in range(NT)]
    jobs += [("vm", 0, t) for t in range(NT)]
    jobs += [("S", m) for m in range(8, 16)]
    jobs += [("vm", 1, t) for t in range(NT)]
    jobs += [("TA", 4), ("oT", 0, 0), ("oT", 1, 0)]
    for m in range(4, 12):
        jobs += ([("TA", m + 1)] if m < 11 else []) + [("PV", m)]
    jobs += [("oT", 0, 1), ("oT", 1, 1)]
    jobs += [("mix", cb, t) for cb in range(2) for t in range(NT)]
    jobs += [("kmT", 0, j) for j in range(4)]
    jobs += [("h1T", t, q) for t in range(NT) for q in range(2)]
    jobs += [("kmT", 1, j) for j in range(4)]
    jobs += [("qmT", 0, j) for j in range(4)] + [("MS", 0), ("MS", 1)]
    jobs += [("qmT", 1, j) for j in range(4)] + [("TP", 0), ("TP", 1), ("MS", 2), ("MS", 3)]
    jobs += [("PM", 0), ("TP", 2), ("PM", 1), ("TP", 3), ("PM", 2), ("PM", 3)]
    jobs += [("mo", cb, t) for cb in range(2) for t in range(NT)]
    plan, used = {}, [0] * 8
    for n, name in enumerate(jobs):
        plan[name] = (n % 8, used[n % 8])
        used[n % 8] += 1
    late = [("h2T", 0, 0), ("h2T", 0, 1), ("lgT", 0), ("h2T", 1, 0), ("h2T", 1, 1), ("lgT", 1), ("lg",), ("rank",)]
    for n, name in enumerate(late):
        plan[name] = (n % 4, used[n % 4])
        used[n % 4] += 1
    for b, (t, g) in enumerate((t, g) for t in range(NT) for g in range(2)):
        plan[("Y", t, g)] = (4 + b, used[4 + b])
    return plan, used


def decoder_layer(nc, a):
    plan, bank_jobs = plan_banks()
    w_dram = {"in": a["w_in"][0], "kv": a["w_mem_kv"][0], "out": a["w_mix_out"][0],
              "q": a["w_mem_q"][0], "o": a["w_mem_o"][0]}

    with ExitStack() as ctx:
        def sb(name, shape, dt=F32):
            return ctx.enter_context(nc.sbuf_tensor(name, shape, dt))

        def sem(name):
            return ctx.enter_context(nc.semaphore(name))

        banks = [ctx.enter_context(nc.psum_tensor(f"bank{i}", [P, 512], F32)) for i in range(8)]

        ring = sb("ring", [P, NSLOT, 2048])
        ring_at = nc.sbuf_base - (NSLOT) * 8192

        def at_place(name, shape, dt, place):
            return nc.alloc_sbuf_tensor_at(name, shape, dt, offset=ring_at + int(8192 * place))

        w_split = at_place("w_split", [P, SPLIT, 2, 2, 512], F32R, 0)
        w_raw = at_place("w_raw", [P, RAW, 2, 512], F32, 5)
        left = at_place("left", [P, 2, KC, S], F32R, 8)
        left_m = at_place("left_m", [P, 2, KC, S], F32R, 10)
        qk_raw = at_place("qk_raw", [P, NT, 2, 512], F32, 12)
        qz = at_place("qz", [P, 8, S], F32, 13)
        vm = at_place("vm", [P, NT, D], F32, 15)
        bias_f = at_place("bias_f", [96, 3 * D], F32, 14)
        kT = at_place("kT", [P, 4, S], F32, 16)
        mem_o = at_place("mem_o", [P, NT, D], F32, 17)
        gb = at_place("gb", [P, 2, D], F32, 18)
        last_gb = at_place("last_gb", [P, 2, D], F32, PLACE[STEADY])
        h = at_place("h", [P, NT, D], F32, 19)

        v = sb("v", [P, NT, D])
        v_flat = v[:, :, :].rearrange("p t n -> p (t n)")
        pm = v_flat.rearrange("p (h t n) -> p h t n", h=MEM_HEADS, t=NT)
        h2T = v_flat.rearrange("p (c n) -> p c n", c=KC)

        work = sb("work", [P, 2 * GROUP * SEG + 1536])
        left_o = nc.alloc_sbuf_tensor_at("left_o", [P, 2, KC, S], F32R, offset=nc.sbuf_base - 4 * (2 * GROUP * SEG + 1536))
        kmT = work[:, 0:KC * S].rearrange("p (c n) -> p c n", c=KC)
        qmT = work[:, KC * S:2 * KC * S].rearrange("p (c n) -> p c n", c=KC)
        scores = work[:, 0:2 * GROUP * SEG].rearrange("p (a b c) -> p a b c", a=2, b=GROUP)
        h_parts = work[:, 0:2 * GROUP * SEG].bitcast(BF16).rearrange(
            "p (t j n) -> p t j n", t=NT, j=3)
        hidden = v_flat.rearrange("p (a n) -> p a n", a=4)
        glu, sig, lin, hidT = (hidden[:, i, :] for i in range(4))
        shared = work[:, 2 * GROUP * SEG:]
        h2_rest = [shared[:, 0:D].rearrange("p (c n) -> p c n", c=KC), h2T[:, :, 0:P]]
        aT = shared.rearrange("p (j n) -> p j n", j=GROUP)
        x_e = shared[:, 0:512].rearrange("p (c n) -> p c n", c=KC)
        y_e = shared[:, 512:1024]
        back = shared[:, 1024:1536].rearrange("p (g n) -> p g n", g=2)

        bias_parts = sb("bias_parts", [96, 3 * D], BF16)
        pick_w = sb("pick_w", [P, NT, P])
        pick = sb("pick", [P, NT, SLOTS], BF16)
        hot = sb("hot", [96, SLOTS], BF16)
        ones96 = sb("ones96", [96, SLOTS])
        const = sb("const", [P, C_END])
        tri_b = sb("tri_b", [P, P], BF16)
        ones_b = sb("ones_b", [P, P], BF16)
        diag = sb("diag", [P, P])
        w_router = sb("w_router", [P, KC, E])
        b_router = sb("b_router", [E, 1])
        sub_g = sb("sub_g", [P, P])
        lam_in = sb("lam_in", [P, 4, HD])
        lam = sb("lam", [P, 8])
        rope_tmp = sb("rope_tmp", [P, 4, NT, 8, ROT])
        stats = sb("stats", [P, 8, 2, 6])
        mv_ln = sb("mv_ln", [P, 8, 2])
        ln_s = sb("ln_s", [P, 8, 2])
        half = sb("half", [P, 8])
        top_max = sb("top_max", [P, 4, 2, GROUP])
        sums = sb("sums", [P, 4, 2, GROUP])
        recips = sb("recips", [P, 4, 2, GROUP])
        rms = sb("rms", [P, 3, 8])
        mem_s = sb("mem_s", [P, 4, MEM_HEADS, 2])
        lgT = sb("lgT", [E, S])
        lg = sb("lg", [P, NT, E])
        best = sb("best", [P, NT, 8])
        route = sb("route", [P, 4, NT, E])
        mask_b = sb("mask_b", [P, NT, E], BF16)
        small = sb("small", [P, 16])
        sweeps_i = sb("sweeps_i", [P, 1], I32)
        pos = sb("pos", [P, NT, E + 1])
        wt = sb("wt", [P, NT, E + 1])
        square = sb("square", [P, P])

        ident = const[:, C_ID:C_ID + P]
        mask = const[:, C_MASK:C_MASK + SEG]
        iota = const[:, C_IOTA:C_IOTA + P]

        filled = [sem(f"bank_filled{i}") for i in range(8)]
        drained = [sem(f"bank_drained{i}") for i in range(8)]
        x_in = [sem(f"x_in{i}") for i in range(2 * NT)]
        mem_in = [sem(f"mem_in{t}") for t in range(NT)]
        ident_in, const_in = sem("ident_in"), sem("const_in")
        gb_in, last_gb_in = sem("gb_in"), sem("last_gb_in")
        small_in, bias_in, router_in = sem("small_in"), sem("bias_in"), sem("router_in")
        unit_in = [sem(f"unit_in{i}") for i in range(RAW)]
        high_ready, low_ready = sem("high_ready"), sem("low_ready")
        unit_used = sem("unit_used")
        left_high = sem("left_high")
        qz_zeroed, bias_split = sem("qz_zeroed"), sem("bias_split")
        pool_step, dve_step = sem("pool_step"), sem("dve_step")
        var_ready, rstd_ready, ln_ready = sem("var_ready"), sem("rstd_ready"), sem("ln_ready")
        lam_sums, lam_exp = sem("lam_sums"), sem("lam_exp")
        roped, max_ready, exp_ready, mixed = sem("roped"), sem("max_ready"), sem("exp_ready"), sem("mixed")
        squared, rms_var, rms_rstd = sem("squared"), sem("rms_var"), sem("rms_rstd")
        o_ready = sem("o_ready")
        mem_max, pm_ready = sem("mem_max"), sem("pm_ready")
        best_ready, route_exp, mask_ready = sem("best_ready"), sem("route_exp"), sem("mask_ready")
        part_ready = [sem(f"part_ready{t}") for t in range(NT)]
        rest_ready = [sem(f"rest_ready{t}") for t in range(NT)]
        prepared = sem("prepared")
        sweeps_ready = sem("sweeps_ready")
        piece_in = [sem(f"piece_in{i}") for i in range(NSLOT)]
        pieces_used = sem("pieces_used")
        hot_ready, hot_used = sem("hot_ready"), sem("hot_used")
        pick_ready, pick_w_ready = sem("pick_ready"), sem("pick_w_ready")
        gathered, x_e_ready = sem("gathered"), sem("x_e_ready")
        up_done, up_read = sem("up_done"), sem("up_read")
        glu_ready, sig_ready, act_ready, hid_ready = sem("glu_ready"), sem("sig_ready"), sem("act_ready"), sem("hid_ready")
        turned, back_ready, scattered = sem("turned"), sem("back_ready"), sem("scattered")
        hid_turned, hidT_ready = sem("hid_turned"), sem("hidT_ready")
        down_done, y_ready = sem("down_done"), sem("y_ready")
        pos_moved, all_added = sem("pos_moved"), sem("all_added")
        out_written = sem("out_written")

        def bank_for(pe, *name):
            b, n = plan[name]
            if n:
                pe.wait_ge(drained[b], n)
            return banks[b]

        def filled_by(*name):
            return filled[plan[name][0]]

        def drained_by(*name):
            return drained[plan[name][0]]

        def wait_filled(eng, *name):
            b, n = plan[name]
            eng.wait_ge(filled[b], n + 1)
            return banks[b]

        def wait_drained(eng, *name):
            b, n = plan[name]
            eng.wait_ge(drained[b], n + 1)

        last_job = [("dq", 1), ("dk", 1), ("dv", 1), ("mq", 1), ("mk", 1), ("mv", 1), ("vm", 0, 1), ("vm", 1, 1),
                    ("mix", 0, 1), ("mix", 1, 1), ("kmT", 0, 3), ("kmT", 1, 3), ("qmT", 0, 3), ("qmT", 1, 3),
                    ("mo", 0, 1), ("mo", 1, 1)]

        def wait_unit_used(eng, u):
            blk, q = u // UNITS, u % UNITS
            if q < UNITS - 1:
                eng.wait_ge(unit_used, (UNITS - 1) * blk + q + 1)
            else:
                wait_filled(eng, *last_job[blk])

        def expert_src(e, k):
            if k < KC:
                return a["w_mlp1"][0, ds(e, 1), P * k:P * (k + 1), :].rearrange("a p n -> p (a n)")
            r = 2 * P * (k - KC)
            return a["w_mlp2"][0, ds(e, 1), r:r + 2 * P, :].rearrange("a (c p) n -> p (a c) n", c=2)

        def slot(k):
            return ring[:, PLACE[k], :]

        def take_part(eng, part, t):
            src = h2_rest[t] if part else h[:, t, :].rearrange("p (c n) -> p c n", c=KC)
            eng.tensor_tensor(h2_rest[t], src, h_parts[:, t, part, :].rearrange("p (c n) -> p c n", c=KC),
                              ALU.subtract).then_inc(rest_ready[t], 1)

        block = ctx.enter_context(nc.Block())

        @block.sync
        def _(sp):
            def load_unit(u):
                tensor, cb = BLOCKS[u // UNITS]
                q = u % UNITS
                src = w_dram[tensor][256 * q:256 * (q + 1), 512 * cb:512 * (cb + 1)]
                sp.dma_start(w_raw[:, u % RAW, :, :], src.rearrange("(c p) n -> p c n", c=2)).then_inc(unit_in[u % RAW], 16)

            sp.dma_start(const[:, C_ID:C_ID + P], a["const"][:, C_ID:C_ID + P]).then_inc(ident_in, 16)
            for q in range(2):
                for t in range(NT):
                    sp.dma_start(h[:, t, 512 * q:512 * (q + 1)], a["x"][0, P * t:P * (t + 1), 512 * q:512 * (q + 1)])\
                        .then_inc(x_in[2 * q + t], 16)
                load_unit(q)

            def free_place(place):
                if place < SPLIT:
                    last = UNITS * len(BLOCKS) - 1
                    wait_unit_used(sp, last - (last - place) % SPLIT)
                elif place < 8:
                    last = UNITS * len(BLOCKS)
                    sp.wait_ge(low_ready, last - (last - 2 - 2 * (place - SPLIT)) % RAW)
                elif place < 10:
                    wait_filled(sp, "qmT", 1, 3)
                elif place < 12:
                    wait_filled(sp, "kmT", 1, 3)
                elif place == 12:
                    wait_filled(sp, "Tmk", 1)
                elif place == 13 or place == 16:
                    wait_filled(sp, "S", 15)
                elif place == 14:
                    sp.wait_ge(bias_split, 1)
                elif place == 15:
                    wait_filled(sp, "PM", 3)
                elif place == 17:
                    wait_filled(sp, "oT", 1, 1)
                elif place == 18:
                    sp.wait_ge(ln_ready, 12)
                else:
                    for t in range(NT):
                        sp.wait_ge(part_ready[t], 3)
                    sp.wait_ge(gathered, 1)

            def load(e, k, at):
                dst = slot(at) if k < KC else slot(at).rearrange("p (c n) -> p c n", c=2)
                sp.dma_start(dst, expert_src(e, k)).then_inc(piece_in[at], 16)

            def wait_piece_used(before, k):
                if k == KC - 1:
                    sp.wait_ge(up_done, before + 1)
                elif k == PIECES - 1:
                    sp.wait_ge(down_done, before + 1)
                else:
                    sp.wait_ge(pieces_used, before * (PIECES - 2) + (k + 1 if k < KC else k))

            def prefetch(slots):
                for at in slots:
                    free_place(PLACE[at])
                    load(at // PIECES, at % PIECES, at)

            ahead = 0
            for u in range(2, UNITS * len(BLOCKS)):
                if u >= RAW:
                    sp.wait_ge(low_ready, u - RAW + 1)
                load_unit(u)
                if u == RAW - 1:
                    sp.dma_start(const[:, C_ID + P:C_END], a["const"][:, C_ID + P:C_END]).then_inc(const_in, 16)
                if u in EARLY:
                    prefetch(range(ahead, ahead + EARLY[u]))
                    ahead += EARLY[u]
            prefetch(range(ahead, NSLOT))

            for n in range(NSLOT, PIECES * (PEELED + 1)):
                wait_piece_used((n - NSLOT) // PIECES, (n - NSLOT) % PIECES)
                load(n // PIECES, n % PIECES, n % NSLOT)

            def load_expert(e, before):
                for k in range(PIECES):
                    wait_piece_used(before, k)
                    load(e, k, STEADY + k)

            with sp.Fori(PEELED + 1, E) as e:
                load_expert(e, sp.snap(e - 1))
            sp.wait_ge(sweeps_ready, 1)
            sweeps = sp.value_load(sweeps_i[0:1, 0:1], min_val=1, max_val=S // SLOTS)
            with sp.If(sweeps > 1):
                with sp.Fori(1, sweeps) as s:
                    with sp.Fori(0, E) as e:
                        load_expert(e, sp.snap(s * E + e - 1))
            sp.wait_ge(up_done, sp.snap(sweeps * E))
            for i, name in enumerate(("ln3_g", "ln3_b")):
                sp.dma_start(last_gb[:, i, :], a[name].broadcast_to([P, D])).then_inc(last_gb_in, 16)
            for t in range(NT):
                for q in range(2):
                    sp.wait_ge(ln_ready, 12 + 2 * t + q + 1)
                    sp.dma_start(a["out"][0, P * t:P * (t + 1), 512 * q:512 * (q + 1)], h[:, t, 512 * q:512 * (q + 1)])\
                        .then_inc(out_written, 16)
            sp.wait_ge(out_written, 16 * 2 * NT)

        @block.gpsimd
        def _(pool):
            steps = [0]

            def step(ins):
                steps[0] += 1
                ins.then_inc(pool_step, 1)
                pool.wait_ge(pool_step, steps[0])

            def row(ap):
                return ap.broadcast_to([P, ap.shape[1]])

            step(pool.memset(half[:, :], -0.5))
            pool.memset(qz[:, :, :], 0.0).then_inc(qz_zeroed, 1)
            pool.wait_ge(unit_in[1], 16)
            for t in range(NT):
                pool.dma_start(mem_o[:, t, :], a["mem"][0, P * t:P * (t + 1), :]).then_inc(mem_in[t], 16)

            def load_gains(gain, bias):
                pool.dma_start(gb[:, 0, :], row(gain)).then_inc(gb_in, 16)
                pool.dma_start(gb[:, 1, :], row(bias)).then_inc(gb_in, 16)

            load_gains(a["mem_ln_g"].rearrange("(a n) -> a n", a=1), a["mem_ln_b"].rearrange("(a n) -> a n", a=1))
            for i, name in enumerate(("diff_lambda_q1", "diff_lambda_q2", "diff_lambda_k1", "diff_lambda_k2")):
                pool.dma_start(lam_in[:, i, :], row(a[name])).then_inc(small_in, 16)
            pool.dma_start(sub_g[:, :], row(a["diff_subln_g"])).then_inc(small_in, 16)
            for i in range(3):
                pool.dma_start(bias_f[E * i:E * (i + 1), 0:2 * FF], a["b_mlp1"][0]).then_inc(bias_in, 16)
                pool.dma_start(bias_f[E * i:E * (i + 1), 2 * FF:3 * FF], a["b_mlp2"][0]).then_inc(bias_in, 16)
            pool.dma_start(w_router[:, :, :], a["w_router"][0].rearrange("(c p) e -> p c e", c=KC)).then_inc(router_in, 16)
            pool.dma_start(b_router[:, :], a["b_router"].rearrange("a e -> e a")).then_inc(router_in, 16)

            def inverse_root(n):
                pool.wait_ge(var_ready, n + 1)
                pool.tensor_tensor(ln_s[:, n, 1:2], ln_s[:, n, 0:1], half[:, 0:1], ALU.pow).then_inc(rstd_ready, 1)

            for n in range(2):
                inverse_root(n)
            pool.wait_ge(bias_in, 16 * 6)
            step(pool.tensor_copy(bias_parts[:, :], bias_f[:, :]))
            for i in (1, 2):
                lo = E * i
                while lo < 96:
                    step(pool.tensor_tensor(bias_f[lo:lo + E, :], bias_f[lo:lo + E, :], bias_parts[lo:lo + E, :], ALU.subtract))
                    step(pool.tensor_copy(bias_parts[lo:lo + E, :], bias_f[lo:lo + E, :]))
                    lo += E
            pool.memset(ones96[:, :], 1.0).then_inc(bias_split, 1)
            pool.wait_ge(ln_ready, 4)
            load_gains(a["ln1_g"], a["ln1_b"])
            pool.wait_ge(rms_var, 1)
            pool.tensor_tensor(rms[:, 2, :], rms[:, 1, :], half[:, :], ALU.pow).then_inc(rms_rstd, 1)
            for n in range(2, 4):
                inverse_root(n)
            pool.wait_ge(ln_ready, 8)
            load_gains(a["ln2_g"], a["ln2_b"])
            for n in range(4, 6):
                inverse_root(n)

            for part in range(2):
                pool.wait_ge(part_ready[0], part + 1)
                take_part(pool, part, 0)
            pool.wait_ge(part_ready[0], 3)
            pool.memset(y_e[:, :], 0.0).then_inc(y_ready, 1)
            for n in range(6, 8):
                inverse_root(n)

        @block.tensor
        def _(pe):
            def turn_rows(name, src, t, q):
                b = bank_for(pe, name, t, q)
                for j in range(4):
                    c = 4 * q + j
                    last = pe.transpose(b[:, P * j:P * (j + 1)], src[:, t, P * c:P * (c + 1)], ident)
                last.then_inc(filled_by(name, t, q), 1)

            def turned_rows(name):
                def before(c):
                    if c % 4 == 0:
                        for t in range(NT):
                            wait_drained(pe, name, t, c // 4)
                return before

            def three_passes(out, stationary, moving, start, stop):
                pe.matmul(out, stationary[0], moving[0], start=start, stop=False)
                pe.matmul(out, stationary[1], moving[0], start=False, stop=False)
                return pe.matmul(out, stationary[0], moving[1], start=False, stop=stop)

            def weights(u, c, cols):
                return [w_split[:, u % SPLIT, part, c % 2, cols] for part in range(2)]

            def project_rows(blk, act_, names, before=None, by_tile=False):
                b = [bank_for(pe, *names[t]) for t in range(NT)]
                for tiles in ([[0], [1]] if by_tile else [[0, 1]]):
                    for c in range(KC):
                        u = UNITS * blk + c // 2
                        if tiles[0] == 0:
                            if c % 2 == 0:
                                pe.wait_ge(low_ready, u + 1)
                            if before:
                                before(c)
                        for t in tiles:
                            mm = three_passes(b[t][:, :], [act_[:, part, c, P * t:P * (t + 1)] for part in range(2)],
                                              weights(u, c, slice(0, 512)), c == 0, c == KC - 1)
                            if c == KC - 1:
                                mm.then_inc(filled_by(*names[t]), 1)
                        if c % 2 and c < KC - 1 and tiles[-1] == NT - 1:
                            mm.then_inc(unit_used, 1)

            def project_cols(blk, act_, name, cb, before=None):
                b = [bank_for(pe, name, cb, j) for j in range(4)]
                for c in range(KC):
                    u = UNITS * blk + c // 2
                    if c % 2 == 0:
                        pe.wait_ge(low_ready, u + 1)
                    if before:
                        before(c)
                    for j in range(4):
                        mm = three_passes(b[j][:, 0:S], weights(u, c, slice(P * j, P * (j + 1))),
                                          [act_[:, part, c, :] for part in range(2)], c == 0, c == KC - 1)
                        if c == KC - 1:
                            mm.then_inc(filled_by(name, cb, j), 1)
                    if c % 2 and c < KC - 1:
                        mm.then_inc(unit_used, 1)

            def turn_heads(kind, index):
                pe.wait_ge(roped, index + 1)
                for t in range(NT):
                    b = bank_for(pe, "T" + kind, t)
                    for j in range(4):
                        last = pe.transpose(b[:, P * j:P * (j + 1)], qk_raw[:, t, index % 2, P * j:P * (j + 1)], ident)
                    last.then_inc(filled_by("T" + kind, t), 1)

            def score(m):
                b = bank_for(pe, "S", m)
                pe.matmul(b[:, 0:P], qz[:, m % 8, 0:P], kT[:, m % 8 // 2, 0:P], start=True, stop=True)
                pe.matmul(b[:, P:SEG], qz[:, m % 8, P:S], kT[:, m % 8 // 2, :], start=True, stop=True)\
                    .then_inc(filled_by("S", m), 1)

            def probs_at(j):
                return (j // 2, 2 * (j % 2)) if j < 4 else (2 + (j - 4) // 4, (j - 4) % 4)

            def turn_probs(j):
                g, i = probs_at(j)
                if j < 4:
                    pe.wait_ge(mixed, g + 1)
                else:
                    pe.wait_ge(exp_ready, g + 1)
                b = bank_for(pe, "TA", j)
                for n in range(3):
                    last = pe.transpose(b[:, P * n:P * (n + 1)], scores[:, g % 2, i, P * n:P * (n + 1)], ident)
                last.then_inc(filled_by("TA", j), 1)

            def weigh(j):
                wait_drained(pe, "TA", j)
                b = bank_for(pe, "PV", j)
                w = P if j < 4 else HD
                col = P * j if j < 4 else 512 + HD * (j - 4)
                at = aT[:, j % GROUP, :]
                pe.matmul(b[:, 0:w], at[:, 0:P], v[:, 0, col:col + w], start=True, stop=True)
                pe.matmul(b[:, P:P + w], at[:, P:2 * P], v[:, 0, col:col + w], start=True, stop=False)
                pe.matmul(b[:, P:P + w], at[:, 2 * P:3 * P], v[:, 1, col:col + w], start=False, stop=True)\
                    .then_inc(filled_by("PV", j), 1)

            def turn_x(q):
                for t in range(NT):
                    pe.wait_ge(x_in[2 * q + t], 16)
                    turn_rows("xT", h, t, q)

            def other_half_of_x(c):
                if c == 2:
                    turn_x(1)
                turned_rows("xT")(c)

            turn_x(0)
            for i, kind in enumerate(("dq", "dk", "dv")):
                project_rows(i, left, ((kind, 0), (kind, 1)), other_half_of_x if i == 0 else None)
            turn_heads("dq", 0)
            turn_heads("dk", 1)
            pe.wait_ge(ln_ready, 4)
            for t in range(NT):
                for q in range(2):
                    turn_rows("memT", mem_o, t, q)
            for k in ("Tdq", "Tdk"):
                for t in range(NT):
                    wait_drained(pe, k, t)
            for m in range(8):
                score(m)
            project_rows(3, left, (("mq", 0), ("mq", 1)))
            project_rows(4, left, (("mk", 0), ("mk", 1)))
            project_rows(5, left, (("mv", 0), ("mv", 1)))
            for t in range(NT):
                wait_drained(pe, "dv", t)
            turn_probs(0)
            for j in range(4):
                if j < 3:
                    turn_probs(j + 1)
                weigh(j)
            turn_heads("mq", 2)
            turn_heads("mk", 3)
            project_rows(6, left_m, (("vm", 0, 0), ("vm", 0, 1)), turned_rows("memT"))
            for k in ("Tmq", "Tmk"):
                for t in range(NT):
                    wait_drained(pe, k, t)
            for m in range(8, 16):
                score(m)
            project_rows(7, left_m, (("vm", 1, 0), ("vm", 1, 1)))
            for t in range(NT):
                wait_drained(pe, "mv", t)
            turn_probs(4)
            pe.wait_ge(o_ready, 1)
            for t in range(NT):
                turn_rows("oT", mem_o, t, 0)
            for j in range(4, 12):
                if j < 11:
                    turn_probs(j + 1)
                weigh(j)
            pe.wait_ge(o_ready, 2)
            for t in range(NT):
                turn_rows("oT", mem_o, t, 1)
            project_rows(8, left, (("mix", 0, 0), ("mix", 0, 1)), turned_rows("oT"))
            project_rows(9, left, (("mix", 1, 0), ("mix", 1, 1)), by_tile=True)
            project_cols(10, left_m, "kmT", 0)
            for t in range(NT):
                for q in range(2):
                    pe.wait_ge(ln_ready, 4 + 2 * t + q + 1)
                    turn_rows("h1T", h, t, q)
            project_cols(11, left_m, "kmT", 1)

            def turn_mem_probs(hd):
                pe.wait_ge(pm_ready, hd + 1)
                b = bank_for(pe, "TP", hd)
                for mt in range(2):
                    for t in range(NT):
                        n = 2 * mt + t
                        last = pe.transpose(b[:, P * n:P * (n + 1)], pm[:, hd, t, P * mt:P * (mt + 1)], ident)
                last.then_inc(filled_by("TP", hd), 1)

            def weigh_mem(hd):
                wait_drained(pe, "TP", hd)
                b = bank_for(pe, "PM", hd)
                for i in range(2):
                    c = 2 * hd + i
                    for mt in range(2):
                        mm = pe.matmul(b[:, S * i:S * (i + 1)], vm[:, mt, P * c:P * (c + 1)], pm[:, hd, mt, :],
                                       start=(mt == 0), stop=(mt == 1))
                mm.then_inc(filled_by("PM", hd), 1)

            for cb in range(2):
                project_cols(12 + cb, left, "qmT", cb, turned_rows("h1T") if cb == 0 else None)
                if cb == 1:
                    turn_mem_probs(0)
                    turn_mem_probs(1)
                for j in range(4):
                    wait_drained(pe, "kmT", cb, j)
                    wait_drained(pe, "qmT", cb, j)
                for hd in (2 * cb, 2 * cb + 1):
                    b = bank_for(pe, "MS", hd)
                    for t in range(NT):
                        for i in range(2):
                            mm = pe.matmul(b[:, S * t:S * (t + 1)], qmT[:, 2 * hd + i, P * t:P * (t + 1)],
                                           kmT[:, 2 * hd + i, :], start=(i == 0), stop=(i == 1))
                    mm.then_inc(filled_by("MS", hd), 1)

            for cb in range(2):
                for t in range(NT):
                    wait_drained(pe, "vm", cb, t)
            weigh_mem(0)
            turn_mem_probs(2)
            weigh_mem(1)
            turn_mem_probs(3)
            weigh_mem(2)
            weigh_mem(3)
            def mem_outputs(c):
                if c % 2 == 0:
                    wait_drained(pe, "PM", c // 2)
            project_rows(14, left_o, (("mo", 0, 0), ("mo", 0, 1)), mem_outputs)
            project_rows(15, left_o, (("mo", 1, 0), ("mo", 1, 1)), by_tile=True)

            pe.wait_ge(router_in, 32)

            def route_logits(t):
                for q in range(2):
                    pe.wait_ge(ln_ready, 8 + 2 * t + q + 1)
                    turn_rows("h2T", h, t, q)
                b = bank_for(pe, "lgT", t)
                for q in range(2):
                    wait_drained(pe, "h2T", t, q)
                    for c in range(4 * q, 4 * q + 4):
                        mm = pe.matmul(b[0:E, 0:P], w_router[:, c, :], h2T[:, c, P * t:P * (t + 1)],
                                       start=(c == 0), stop=(c == KC - 1))
                mm.then_inc(filled_by("lgT", t), 1)

            def start_sum(t):
                for g in range(2):
                    b = bank_for(pe, "Y", t, g)
                    pe.matmul(b[:, :], diag[:, :], h[:, t, 512 * g:512 * (g + 1)], start=True, stop=False)

            pe.wait_ge(prepared, 1)
            for t in range(NT):
                route_logits(t)
            b = bank_for(pe, "lg")
            for t in range(NT):
                wait_drained(pe, "lgT", t)
                mm = pe.transpose(b[:, E * t:E * (t + 1)], lgT[:, P * t:P * (t + 1)], const[0:E, C_ID:C_ID + E])
            mm.then_inc(filled_by("lg"), 1)
            start_sum(0)
            pe.wait_ge(mask_ready, 1)
            b = bank_for(pe, "rank")
            pe.matmul(b[:, 0:E], tri_b[:, :], mask_b[:, 0, :], start=True, stop=True)
            pe.matmul(b[:, E:2 * E], ones_b[:, :], mask_b[:, 0, :], start=True, stop=False)
            pe.matmul(b[:, E:2 * E], tri_b[:, :], mask_b[:, 1, :], start=False, stop=True)
            pe.matmul(b[:, 2 * E:3 * E], ones_b[:, :], mask_b[:, 0, :], start=True, stop=False)
            pe.matmul(b[:, 2 * E:3 * E], ones_b[:, :], mask_b[:, 1, :], start=False, stop=True)\
                .then_inc(filled_by("rank"), 1)
            start_sum(1)

            up, ty, xg = banks[0:2], banks[2], banks[3]
            acc = [[banks[4 + 2 * t + g] for g in range(2)] for t in range(NT)]
            for i in range(4):
                pe.wait_ge(drained[i], bank_jobs[i])

            def gather():
                for c in range(KC):
                    for n in range(6):
                        t, part = n // 3, n % 3
                        mm = pe.matmul(xg[:, SLOTS * c:SLOTS * (c + 1)], h_parts[:, t, part, P * c:P * (c + 1)],
                                       pick[:, t, :], start=(n == 0), stop=(n == 5))
                mm.then_inc(gathered, 1)

            def scatter(last):
                for t in range(NT):
                    for g in range(2):
                        mm = pe.matmul(acc[t][g][:, :], back[:, g, P * t:P * (t + 1)], y_e[:, :],
                                       start=False, stop=last)
                        if last:
                            mm.then_inc(all_added, 1)
                if not last:
                    mm.then_inc(scattered, 1)


            def exchange(now):
                pe.wait_ge(pick_w_ready, now)
                pe.wait_ge(y_ready, now)
                for t in range(NT):
                    mm = pe.transpose(ty[:, P * t:P * (t + 1)], pick_w[:, t, :], ident)
                mm.then_inc(turned, 1)
                pe.wait_ge(back_ready, now)
                scatter(False)

            def gather_next(nxt):
                pe.wait_ge(pick_ready, nxt)
                gather()

            def serve(now, nxt, piece, first=False, gather_early=False):
                pe.wait_ge(hot_ready, now)
                pe.wait_ge(up_read, now)
                for n in range(2):
                    for g in range(2):
                        col = 1024 * g + 512 * n
                        pe.matmul(up[n][64 * g:64 * g + SLOTS, :], hot[:, :], bias_parts[:, col:col + 512],
                                  start=True, stop=False)
                if first:
                    for t in range(NT):
                        pe.wait_ge(part_ready[t], 3)
                    pe.wait_ge(pick_ready, 1)
                    gather()
                pe.wait_ge(x_e_ready, now)
                for k in range(KC):
                    at = piece(k)
                    for n in range(2):
                        for g in range(2):
                            col = 1024 * g + 512 * n
                            mm = pe.matmul(up[n][64 * g:64 * g + SLOTS, :], x_e[:, k, :],
                                           slot(at)[:, col:col + 512], start=False, stop=(k == KC - 1))
                    mm.then_inc(pieces_used if k < KC - 1 else up_done, 1)
                    if k == 0 and gather_early:
                        gather_next(nxt)
                exchange(now)
                if not gather_early:
                    gather_next(nxt)
                pe.wait_ge(hid_ready, now)
                pe.wait_ge(back_ready, nxt)
                for q in range(4):
                    mm = pe.transpose(ty[:, P * q:P * (q + 1)], glu[:, P * q:P * (q + 1)], ident)
                mm.then_inc(hid_turned, 1)
                pe.wait_ge(hidT_ready, now)
                for g in range(2):
                    mm = pe.matmul(ty[64 * g:64 * g + SLOTS, :], hot[:, :],
                                   bias_parts[:, 2 * FF + 512 * g:2 * FF + 512 * (g + 1)], start=True, stop=False)
                mm.then_inc(hot_used, 1)
                for u in range(4):
                    at = piece(KC + u)
                    for i in range(2):
                        c = 2 * u + i
                        for g in range(2):
                            mm = pe.matmul(ty[64 * g:64 * g + SLOTS, :],
                                           hidT[:, P * (c % 4) + 64 * (c // 4):P * (c % 4) + 64 * (c // 4) + SLOTS],
                                           slot(at)[:, D * i + 512 * g:D * i + 512 * (g + 1)],
                                           start=False, stop=(c == KC - 1))
                    mm.then_inc(pieces_used if u < 3 else down_done, 1)

            def early_piece(e):
                def piece(k):
                    n = PIECES * e + k
                    pe.wait_ge(piece_in[n % NSLOT], 16 * (n // NSLOT + 1))
                    return n % NSLOT
                return piece

            def steady_piece(loads):
                def piece(k):
                    pe.wait_ge(piece_in[STEADY + k], loads)
                    return STEADY + k
                return piece

            for e in range(PEELED):
                serve(e + 1, e + 2, early_piece(e), first=(e == 0))
            with pe.Fori(PEELED, E - 1) as e:
                serve(pe.snap(e + 1), pe.snap(e + 2), steady_piece(pe.snap((e - LAG) * 16)))
            serve(E, E + 1, steady_piece((E - 1 - LAG) * 16), gather_early=True)
            pe.wait_ge(sweeps_ready, 1)
            sweeps = pe.value_load(sweeps_i[0:1, 0:1], min_val=1, max_val=S // SLOTS)
            with pe.If(sweeps > 1):
                with pe.Fori(1, sweeps) as s:
                    with pe.Fori(0, E) as e:
                        now = pe.snap(s * E + e + 1)
                        serve(now, pe.snap(now + 1), steady_piece(pe.snap((now - 1 - LAG) * 16)))
            served = pe.snap(sweeps * E + 1)
            pe.wait_ge(y_ready, served)
            pe.wait_ge(back_ready, served)
            scatter(True)

        @block.scalar
        def _(act):
            def copy_rows(name, dst, tiles):
                for t, q in tiles:
                    b = wait_filled(act, name, t, q)
                    act.activation(dst[:, 4 * q:4 * q + 4, P * t:P * (t + 1)],
                                   b[:, :].rearrange("p (c n) -> p c n", c=4), ACT.Copy).then_inc(drained_by(name, t, q), 1)

            units = [0]

            def split(count):
                for _ in range(count):
                    u = units[0]
                    units[0] += 1
                    act.wait_ge(unit_in[u % RAW], 16 * (u // RAW + 1))
                    if u >= SPLIT:
                        wait_unit_used(act, u - SPLIT)
                    act.activation(w_split[:, u % SPLIT, 0], w_raw[:, u % RAW], ACT.Copy).then_inc(high_ready, 1)

            def split_rows(name, dst, tiles):
                for t, q in tiles:
                    b = wait_filled(act, name, t, q)
                    act.activation(dst[:, 0, 4 * q:4 * q + 4, P * t:P * (t + 1)],
                                   b[:, :].rearrange("p (c n) -> p c n", c=4), ACT.Copy).then_inc(left_high, 1)

            def copy_to(dst, *name):
                b = wait_filled(act, *name)
                act.activation(dst, b[:, 0:512], ACT.Copy).then_inc(drained_by(*name), 1)

            def copy_heads(kind):
                for t in range(NT):
                    b = wait_filled(act, "T" + kind, t)
                    src = b[:, :].rearrange("p (j n) -> p j n", j=4)
                    if kind[1] == "q":
                        to = qz[:, :, P * t:P * (t + 1)].rearrange("p (j c) n -> p j c n", c=2)
                        act.activation(to[0:HD, :, 0, :], src[0:HD], ACT.Copy)
                        act.activation(to[HD:P, :, 1, :], src[HD:P], ACT.Copy).then_inc(drained_by("T" + kind, t), 1)
                    else:
                        act.activation(kT[:, :, P * t:P * (t + 1)], src, ACT.Copy)\
                            .then_inc(drained_by("T" + kind, t), 1)

            def exps(g):
                act.wait_ge(max_ready, g + 1)
                for t in range(NT):
                    for i in range(GROUP):
                        at = scores[:, g % 2, i, 0:P] if t == 0 else scores[:, g % 2, i, P:SEG]
                        last = act.activation(at, at, ACT.Exp, bias=top_max[:, g, t, i:i + 1], scale=SCALE,
                                              accum_out=sums[:, g, t, i:i + 1])
                last.then_inc(exp_ready, 1)

            def copy_probs(j):
                b = wait_filled(act, "TA", j)
                if j >= GROUP:
                    wait_filled(act, "PV", j - GROUP)
                act.activation(aT[:, j % GROUP, :], b[:, 0:SEG], ACT.Copy).then_inc(drained_by("TA", j), 1)

            def copy_raw(index, kind):
                for t in range(NT):
                    copy_to(qk_raw[:, t, index, :], kind, t)

            def copy_cols(name, cb, dst):
                for j in range(4):
                    b = wait_filled(act, name, cb, j)
                    act.activation(dst[:, 4 * cb + j, :], b[:, 0:S], ACT.Copy).then_inc(drained_by(name, cb, j), 1)

            def split_pair(hd):
                b = wait_filled(act, "PM", hd)
                act.activation(left_o[:, 0, 2 * hd:2 * hd + 2, :], b[:, :].rearrange("p (c n) -> p c n", c=2), ACT.Copy)\
                    .then_inc(left_high, 1)

            split_rows("xT", left, BY_HALF[0:NT])
            split(2)
            split_rows("xT", left, BY_HALF[NT:])
            split(6)
            copy_raw(0, "dq")
            split(4)
            copy_raw(1, "dk")
            act.wait_ge(lam_sums, 1)
            act.activation(lam[:, 2:4], lam[:, 0:2], ACT.Exp).then_inc(lam_exp, 1)
            split(4)
            for t in range(NT):
                copy_to(v[:, t, 0:512], "dv", t)
            act.wait_ge(qz_zeroed, 1)
            copy_heads("dq")
            copy_heads("dk")
            split_rows("memT", left_m, BY_TILE)
            exps(0)
            split(4)
            exps(1)
            copy_raw(0, "mq")
            split(4)
            copy_raw(1, "mk")
            split(4)
            for t in range(NT):
                copy_to(v[:, t, 512:1024], "mv", t)
            for j in range(4):
                copy_probs(j)
            copy_heads("mq")
            copy_heads("mk")
            for j in range(4):
                wait_drained(act, "PV", j)
                for t in range(NT):
                    if j or t:
                        act.wait_ge(squared, 2 * j + t)
                    act.activation(square[:, :], mem_o[:, t, P * j:P * (j + 1)], ACT.Square,
                                   accum_out=rms[:, 0, 4 * t + j:4 * t + j + 1]).then_inc(squared, 1)
            split(4)
            act.wait_ge(bias_split, 1)

            def copy_vm(cb):
                for t in range(NT):
                    copy_to(vm[:, t, 512 * cb:512 * (cb + 1)], "vm", cb, t)

            def mem_exps(hd):
                b = wait_filled(act, "MS", hd)
                act.wait_ge(mem_max, hd + 1)
                for t in range(NT):
                    last = act.activation(pm[:, hd, t, :], b[:, S * t:S * (t + 1)], ACT.Exp,
                                          bias=mem_s[:, 1, hd, t:t + 1], scale=MEM_SCALE,
                                          accum_out=mem_s[:, 2, hd, t:t + 1])
                last.then_inc(drained_by("MS", hd), 1)

            copy_vm(0)
            exps(2)
            exps(3)
            split(2)
            copy_probs(4)
            split_rows("oT", left, BY_HALF[0:NT])
            copy_vm(1)
            for j in range(5, 12):
                copy_probs(j)
                if j < 7:
                    split(1)
            split_rows("oT", left, BY_HALF[NT:])
            split(12)
            copy_cols("kmT", 0, kmT)
            split_rows("h1T", left, BY_TILE)
            split(4)
            copy_cols("kmT", 1, kmT)
            split(4)
            copy_cols("qmT", 0, qmT)
            mem_exps(0)
            mem_exps(1)
            split(4)
            copy_cols("qmT", 1, qmT)

            def copy_mem_probs(hd):
                copy_to(pm[:, hd, :, :].rearrange("p t n -> p (t n)"), "TP", hd)

            copy_mem_probs(0)
            copy_mem_probs(1)
            mem_exps(2)
            mem_exps(3)
            split_pair(0)
            copy_mem_probs(2)
            split_pair(1)
            copy_mem_probs(3)
            split_pair(2)
            split_pair(3)
            split(4)
            assert units[0] == UNITS * len(BLOCKS)
            copy_rows("h2T", h2T, [(0, 0), (0, 1)])
            act.wait_ge(router_in, 32)

            def logits(t):
                b = wait_filled(act, "lgT", t)
                act.activation(lgT[:, P * t:P * (t + 1)], b[0:E, 0:P], ACT.Identity, bias=b_router[:, 0:1], scale=1.0)\
                    .then_inc(drained_by("lgT", t), 1)

            def h_part(part, t):
                if part:
                    act.wait_ge(rest_ready[t], part)
                else:
                    act.wait_ge(ln_ready, 8 + 2 * (t + 1))
                    wait_filled(act, "mo", 1, 1)
                act.activation(h_parts[:, t, part, :].rearrange("p (c n) -> p c n", c=KC),
                               h2_rest[t] if part else h[:, t, :].rearrange("p (c n) -> p c n", c=KC),
                               ACT.Copy).then_inc(part_ready[t], 1)

            h_part(0, 0)
            logits(0)
            copy_rows("h2T", h2T, [(1, 0), (1, 1)])
            h_part(0, 1)
            logits(1)
            h_part(1, 0)
            h_part(1, 1)
            act.wait_ge(best_ready, 1)
            for t in range(NT):
                last = act.activation(route[:, 2, t, :], lg[:, t, :], ACT.Exp, bias=small[:, t:t + 1], scale=1.0)
            last.then_inc(route_exp, 1)
            h_part(2, 0)
            h_part(2, 1)

            def take_tokens():
                act.activation(x_e[:, :, :], banks[3][:, :].rearrange("p (c n) -> p c n", c=KC), ACT.Copy)\
                    .then_inc(x_e_ready, 1)

            act.wait_ge(gathered, 1)
            take_tokens()
            act.wait_ge(sweeps_ready, 1)
            sweeps = act.value_load(sweeps_i[0:1, 0:1], min_val=1, max_val=S // SLOTS)
            with act.Fori(0, sweeps) as s:
                with act.Fori(0, E) as e:
                    now = act.snap(s * E + e + 1)
                    nxt = act.snap(now + 1)
                    act.wait_ge(glu_ready, now)
                    act.activation(sig, glu, ACT.Sigmoid, scale=SW_ALPHA).then_inc(sig_ready, 1)
                    act.wait_ge(gathered, nxt)
                    take_tokens()
                    act.wait_ge(hid_turned, now)
                    act.activation(hidT, banks[2][:, :], ACT.Copy).then_inc(hidT_ready, 1)
                    act.wait_ge(down_done, now)
                    act.activation(y_e[:, :], banks[2][:, :], ACT.Copy).then_inc(y_ready, 1)

        @block.vector
        def _(dve):
            steps = [0]

            def step(ins):
                steps[0] += 1
                ins.then_inc(dve_step, 1)
                dve.wait_ge(dve_step, steps[0])

            def copy_rows(name, dst, tiles):
                for t, q in tiles:
                    b = wait_filled(dve, name, t, q)
                    dve.tensor_copy(dst[:, 4 * q:4 * q + 4, P * t:P * (t + 1)],
                                    b[:, :].rearrange("p (c n) -> p c n", c=4)).then_inc(drained_by(name, t, q), 1)

            units, turns = [0], [0]

            def split(count):
                for _ in range(count):
                    u = units[0]
                    units[0] += 1
                    dve.wait_ge(high_ready, u + 1)
                    dve.tensor_tensor(w_split[:, u % SPLIT, 1], w_raw[:, u % RAW], w_split[:, u % SPLIT, 0].bitcast(F32),
                                      ALU.subtract).then_inc(low_ready, 1)

            def low_part(dst, src, high, *name):
                turns[0] += 1
                dve.wait_ge(left_high, turns[0])
                dve.tensor_tensor(dst, src, high.bitcast(F32), ALU.subtract).then_inc(drained_by(*name), 1)

            def split_rows(name, dst, tiles):
                for t, q in tiles:
                    b = wait_filled(dve, name, t, q)
                    at = (slice(4 * q, 4 * q + 4), slice(P * t, P * (t + 1)))
                    low_part(dst[:, 1, at[0], at[1]], b[:, :].rearrange("p (c n) -> p c n", c=4),
                             dst[:, 0, at[0], at[1]], name, t, q)

            def half_stats(n, q, src):
                return dve.bn_stats(stats[:, n, q, :], src)

            def variance(n):
                step(dve.bn_aggr(mv_ln[:, n, :], stats[:, n, :, :].rearrange("p a b -> p (a b)")))
                dve.tensor_scalar(ln_s[:, n, 0:1], mv_ln[:, n, 1:2], EPS, None, ALU.add).then_inc(var_ready, 1)

            def apply_norm(n, x, src, gb=gb):
                halves = [slice(0, 512), slice(512, D)]
                for q in range(2):
                    step(dve.scalar_tensor_tensor(out=x[:, halves[q]], in0=src[q], scalar=mv_ln[:, n, 0:1],
                                                  in1=gb[:, 0, halves[q]], op0=ALU.subtract, op1=ALU.mult))
                    if q == 0:
                        dve.wait_ge(rstd_ready, n + 1)
                    dve.scalar_tensor_tensor(out=x[:, halves[q]], in0=x[:, halves[q]], scalar=ln_s[:, n, 1:2],
                                             in1=gb[:, 1, halves[q]], op0=ALU.mult, op1=ALU.add).then_inc(ln_ready, 1)

            def residual(name, cb, t):
                b = wait_filled(dve, name, cb, t)
                x = h[:, t, 512 * cb:512 * (cb + 1)]
                dve.scalar_tensor_tensor(out=x, in0=x, scalar=ALPHA, in1=b[:, :], op0=ALU.mult, op1=ALU.add)\
                    .then_inc(drained_by(name, cb, t), 1)

            def first_halves(n, name):
                for t in range(NT):
                    residual(name, 0, t)
                for t in range(NT):
                    wait_drained(dve, name, 0, t)
                    half_stats(n + t, 0, h[:, t, 0:512])

            def finish(n, name, t, gb_count):
                residual(name, 1, t)
                wait_drained(dve, name, 1, t)
                step(half_stats(n + t, 1, h[:, t, 512:1024]))
                variance(n + t)
                dve.wait_ge(gb_in, gb_count)
                apply_norm(n + t, h[:, t, :], [h[:, t, 0:512], h[:, t, 512:1024]])

            def rope(index, kinds):
                for t in range(NT):
                    wait_drained(dve, kinds, t)
                x = qk_raw[:, :, index % 2, :].rearrange("p t (h d) -> p t h d", h=8)
                x1, x2 = x[:, :, :, 0:ROT], x[:, :, :, ROT:2 * ROT]
                cos = const[:, C_COS:C_COS + 2 * ROT].rearrange("p (t a r) -> p t a r", t=NT, a=1).broadcast_to([P, NT, 8, ROT])
                sin = const[:, C_SIN:C_SIN + 2 * ROT].rearrange("p (t a r) -> p t a r", t=NT, a=1).broadcast_to([P, NT, 8, ROT])
                dve.tensor_tensor(rope_tmp[:, 0], x1, cos, ALU.mult)
                dve.tensor_tensor(rope_tmp[:, 1], x2, sin, ALU.mult)
                dve.tensor_tensor(rope_tmp[:, 2], x2, cos, ALU.mult)
                step(dve.tensor_tensor(rope_tmp[:, 3], x1, sin, ALU.mult))
                dve.tensor_tensor(x1, rope_tmp[:, 0], rope_tmp[:, 1], ALU.subtract)
                dve.tensor_tensor(x2, rope_tmp[:, 2], rope_tmp[:, 3], ALU.add).then_inc(roped, 1)
                dve.wait_ge(roped, index + 1)

            def mask_group(g):
                if g >= 2:
                    wait_filled(dve, "TA", 2 * (g - 2) + 1)
                for i in range(GROUP):
                    m = GROUP * g + i
                    b = wait_filled(dve, "S", m)
                    dve.tensor_tensor(scores[:, g % 2, i, :], b[:, 0:SEG], mask, ALU.add).then_inc(drained_by("S", m), 1)
                wait_drained(dve, "S", GROUP * g + GROUP - 1)
                dve.tensor_reduce(top_max[:, g, 0, :], scores[:, g % 2, :, 0:P], AX.X, ALU.max)
                step(dve.tensor_reduce(top_max[:, g, 1, :], scores[:, g % 2, :, P:SEG], AX.X, ALU.max))
                dve.tensor_scalar(top_max[:, g], top_max[:, g], -SCALE, None, ALU.mult).then_inc(max_ready, 1)

            def invert(g):
                dve.wait_ge(exp_ready, g + 1)
                step(dve.reciprocal(recips[:, g], sums[:, g]))

            def mix_group(g):
                invert(g)
                r1 = recips[:, g].rearrange("p t (j c) -> p t j c", c=2)[:, :, :, 1]
                step(dve.tensor_scalar(r1, r1, lam[:, 4:5], None, ALU.mult))
                parts = [(i, t, slice(0, P) if t == 0 else slice(P, SEG)) for i in (0, 2) for t in range(NT)]
                for i, t, at in parts:
                    p1 = scores[:, g % 2, i + 1, at]
                    last = dve.tensor_scalar(p1, p1, recips[:, g, t, i + 1:i + 2], None, ALU.mult)
                step(last)
                for i, t, at in parts:
                    p0 = scores[:, g % 2, i, at]
                    last = dve.scalar_tensor_tensor(out=p0, in0=p0, scalar=recips[:, g, t, i:i + 1],
                                                    in1=scores[:, g % 2, i + 1, at], op0=ALU.mult, op1=ALU.add)
                last.then_inc(mixed, 1)

            split_rows("xT", left, BY_HALF[0:NT])
            split(2)
            split_rows("xT", left, BY_HALF[NT:])
            split(3)
            for t in range(NT):
                dve.wait_ge(mem_in[t], 16)
                for q in range(2):
                    last = half_stats(t, q, mem_o[:, t, 512 * q:512 * (q + 1)])
                step(last)
                variance(t)
            split(3)
            dve.wait_ge(small_in, 16 * 5)
            step(dve.tensor_tensor(lam_in[:, 0:2, :], lam_in[:, 0:2, :], lam_in[:, 2:4, :], ALU.mult))
            dve.tensor_reduce(lam[:, 0:2], lam_in[:, 0:2, :], AX.X, ALU.add).then_inc(lam_sums, 1)
            dve.tensor_scalar(sub_g[:, :], sub_g[:, :], 1.0 - LAMBDA_INIT, None, ALU.mult)
            dve.wait_ge(const_in, 16)
            dve.tensor_copy(tri_b[:, :], const[:, C_TRI:C_TRI + P])
            dve.memset(ones_b[:, :], 1.0)
            dve.tensor_scalar(diag[:, :], ident, ALPHA, None, ALU.mult).then_inc(prepared, 1)
            split(4)
            rope(0, "dq")
            dve.wait_ge(gb_in, 32)
            for t in range(NT):
                apply_norm(t, mem_o[:, t, :], [mem_o[:, t, 0:512], mem_o[:, t, 512:1024]])
            dve.wait_ge(lam_exp, 1)
            step(dve.tensor_scalar(lam[:, 4:5], lam[:, 3:4], lam[:, 2:3], LAMBDA_INIT, ALU.subtract, ALU.subtract))
            rope(1, "dk")
            split(4)
            dve.wait_ge(prepared, 1)
            split_rows("memT", left_m, BY_TILE)
            mask_group(0)
            split(2)
            mask_group(1)
            split(2)
            mix_group(0)
            split(2)
            mix_group(1)
            split(2)
            rope(2, "mq")
            rope(3, "mk")
            split(4)
            for j in range(4):
                b = wait_filled(dve, "PV", j)
                dve.tensor_copy(mem_o[:, :, P * j:P * (j + 1)], b[:, 0:2 * P].rearrange("p (t n) -> p t n", t=NT))\
                    .then_inc(drained_by("PV", j), 1)
            dve.wait_ge(squared, 8)
            dve.tensor_scalar(rms[:, 1, :], rms[:, 0, :], 1.0 / P, EPS, ALU.mult, ALU.add).then_inc(rms_var, 1)
            dve.wait_ge(rms_rstd, 1)
            for t in range(NT):
                for j in range(4):
                    o = mem_o[:, t, P * j:P * (j + 1)]
                    last = dve.scalar_tensor_tensor(out=o, in0=o, scalar=rms[:, 2, 4 * t + j:4 * t + j + 1], in1=sub_g[:, :],
                                                    op0=ALU.mult, op1=ALU.mult)
            last.then_inc(o_ready, 1)
            split(4)
            mask_group(2)
            mask_group(3)
            split(2)
            split_rows("oT", left, BY_HALF[0:NT])
            invert(2)
            invert(3)
            for j in range(8):
                b = wait_filled(dve, "PV", 4 + j)
                for t in range(NT):
                    last = dve.tensor_scalar(mem_o[:, t, 512 + HD * j:512 + HD * (j + 1)], b[:, P * t:P * t + HD],
                                             recips[:, 2 + j // 4, t, j % 4:j % 4 + 1], None, ALU.mult)
                last.then_inc(drained_by("PV", 4 + j), 1)
                if j in (1, 2):
                    split(1)
            wait_drained(dve, "PV", 11)
            dve.memset(small[:, 8:16], 0.0).then_inc(o_ready, 1)
            split_rows("oT", left, BY_HALF[NT:])
            split(4)
            first_halves(2, "mix")
            split(1)
            finish(2, "mix", 0, 64)
            split(3)
            finish(2, "mix", 1, 64)
            split(4)
            split_rows("h1T", left, BY_TILE)
            dve.memset(back[:, :, :], 0.0).then_inc(back_ready, 1)
            split(8)

            def mem_softmax(heads):
                for hd in heads:
                    b = wait_filled(dve, "MS", hd)
                    step(dve.tensor_reduce(mem_s[:, 0, hd, :], b[:, :].rearrange("p (t n) -> p t n", t=NT), AX.X, ALU.max))
                    dve.tensor_scalar(mem_s[:, 1, hd, :], mem_s[:, 0, hd, :], -MEM_SCALE, None, ALU.mult)\
                        .then_inc(mem_max, 1)
                for hd in heads:
                    wait_drained(dve, "MS", hd)
                    step(dve.reciprocal(mem_s[:, 3, hd, :], mem_s[:, 2, hd, :]))
                    for t in range(NT):
                        last = dve.tensor_scalar(pm[:, hd, t, :], pm[:, hd, t, :], mem_s[:, 3, hd, t:t + 1], None, ALU.mult)
                    last.then_inc(pm_ready, 1)

            mem_softmax((0, 1))
            split(4)
            mem_softmax((2, 3))
            for hd in range(MEM_HEADS):
                b = wait_filled(dve, "PM", hd)
                low_part(left_o[:, 1, 2 * hd:2 * hd + 2, :], b[:, :].rearrange("p (c n) -> p c n", c=2),
                         left_o[:, 0, 2 * hd:2 * hd + 2, :], "PM", hd)
            split(4)
            def choose(e):
                for t in range(NT):
                    last = dve.tensor_scalar(pick[:, t, :], iota[:, 0:SLOTS], pos[:, t, ds(e, 1)], None, ALU.is_equal)
                last.then_inc(pick_ready, 1)

            def choose_weighted(e):
                for t in range(NT):
                    last = dve.tensor_scalar(pick_w[:, t, :], iota, pos[:, t, ds(e, 1)], wt[:, t, ds(e, 1)],
                                             ALU.is_equal, ALU.mult)
                last.then_inc(pick_w_ready, 1)

            def mark(e):
                dve.tensor_scalar(hot[:, :], ones96[:, :], const[0:96, ds(C_HOT + e, 1)], None, ALU.mult).then_inc(hot_ready, 1)

            dve.wait_ge(bias_split, 1)
            mark(0)
            dve.memset(small[:, 12:13], 0.0).then_inc(up_read, 1)
            first_halves(4, "mo")
            for t in range(NT):
                finish(4, "mo", t, 96)

            dve.wait_ge(part_ready[1], 1)
            wait_filled(dve, "lgT", 0)
            take_part(dve, 0, 1)
            b = wait_filled(dve, "lg")
            dve.tensor_copy(lg[:, :, :], b[:, 0:2 * E].rearrange("p (t e) -> p t e", t=NT)).then_inc(drained_by("lg"), 1)
            wait_drained(dve, "lg")
            for t in range(NT):
                last = dve.max(best[:, t, :], lg[:, t, :])
            step(last)
            dve.tensor_scalar(small[:, 0:2], best[:, :, 0], -1.0, None, ALU.mult).then_inc(best_ready, 1)
            step(dve.memset(best[:, :, TOPK:8], 3e38))
            for t in range(NT):
                last = dve.match_replace(route[:, 0, t, :], best[:, t, :], lg[:, t, :], -BIG)
            step(last)
            step(dve.tensor_tensor(route[:, 1], route[:, 0], lg[:, :, :], ALU.not_equal))
            dve.tensor_copy(mask_b[:, :, :], route[:, 1]).then_inc(mask_ready, 1)
            dve.wait_ge(part_ready[1], 2)
            take_part(dve, 1, 1)
            b = wait_filled(dve, "rank")
            step(dve.scalar_tensor_tensor(out=route[:, 3], in0=b[:, 0:2 * E].rearrange("p (t e) -> p t e", t=NT), scalar=1.0,
                                          in1=route[:, 1], op0=ALU.add, op1=ALU.mult))
            step(dve.tensor_scalar(pos[:, :, 0:E], route[:, 3], -1.0, None, ALU.add))
            step(dve.tensor_scalar(pos[:, :, E:E + 1], pos[:, :, 0:1], -float(SLOTS), None, ALU.add))
            choose(0)
            dve.tensor_reduce(small[:, 6:7], b[:, 2 * E:3 * E], AX.X, ALU.max).then_inc(drained_by("rank"), 1)
            wait_drained(dve, "rank")
            step(dve.tensor_scalar(small[:, 8:9], small[:, 6:7], float(SLOTS), 1.0, ALU.is_gt, ALU.add))
            for i in (2, 3):
                step(dve.tensor_scalar(small[:, 7 + i:8 + i], small[:, 6:7], float(SLOTS * i), small[:, 6 + i:7 + i],
                                       ALU.is_gt, ALU.add))
            dve.tensor_copy(sweeps_i[:, :], small[:, 10:11]).then_inc(sweeps_ready, 1)

            dve.wait_ge(route_exp, 1)
            step(dve.tensor_tensor(route[:, 2], route[:, 2], route[:, 1], ALU.mult))
            step(dve.tensor_reduce(small[:, 2:4], route[:, 2], AX.X, ALU.add))
            step(dve.reciprocal(small[:, 4:6], small[:, 2:4]))
            for t in range(NT):
                last = dve.tensor_scalar(wt[:, t, 0:E], route[:, 2, t, :], small[:, 4 + t:5 + t], None, ALU.mult)
            step(last)
            step(dve.tensor_copy(wt[:, :, E:E + 1], wt[:, :, 0:1]))
            choose_weighted(0)
            dve.wait_ge(sweeps_ready, 1)
            sweeps = dve.value_load(sweeps_i[0:1, 0:1], min_val=1, max_val=S // SLOTS)
            with dve.Fori(0, sweeps) as s:
                with dve.Fori(0, E) as e:
                    now = dve.snap(s * E + e + 1)
                    nxt = dve.snap(now + 1)
                    dve.wait_ge(gathered, now)
                    choose(e + 1)
                    dve.wait_ge(up_done, now)
                    for n in range(2):
                        hid = banks[n][:, :].rearrange("p (j c) -> p j c", c=2)
                        last = dve.tensor_scalar(glu[:, S * n:S * (n + 1)], hid[:, :, 0], LIMIT, None, ALU.min)
                    last.then_inc(glu_ready, 1)
                    for n in range(2):
                        hid = banks[n][:, :].rearrange("p (j c) -> p j c", c=2)
                        last = dve.tensor_scalar(lin[:, S * n:S * (n + 1)], hid[:, :, 1], LIMIT, -LIMIT, ALU.min, ALU.max)
                    last.then_inc(up_read, 1)
                    dve.wait_ge(up_read, nxt)
                    dve.scalar_tensor_tensor(out=lin, in0=lin, scalar=1.0, in1=glu, op0=ALU.add, op1=ALU.mult)\
                        .then_inc(act_ready, 1)
                    dve.wait_ge(act_ready, now)
                    dve.wait_ge(sig_ready, now)
                    dve.tensor_tensor(glu, lin, sig, ALU.mult).then_inc(hid_ready, 1)
                    dve.wait_ge(turned, now)
                    dve.wait_ge(scattered, now)
                    for g in range(2):
                        last = dve.tensor_copy(back[64 * g:64 * g + SLOTS, g, :], banks[2][64 * g:64 * g + SLOTS, 0:S])
                    last.then_inc(back_ready, 1)
                    choose_weighted(e + 1)
                    dve.wait_ge(hot_used, now)
                    mark(e + 1)
                dve.wait_ge(pick_w_ready, s * E + E + 1)
                dve.tensor_scalar(pos[:, :, :], pos[:, :, :], -float(SLOTS), None, ALU.add).then_inc(pos_moved, 1)
                dve.wait_ge(pos_moved, s + 1)
            for t in range(NT):
                for q in range(2):
                    dve.wait_ge(all_added, 2 * t + q + 1)
                    last = half_stats(6 + t, q, banks[4 + 2 * t + q][:, :])
                step(last)
                variance(6 + t)
                dve.wait_ge(last_gb_in, 32)
                apply_norm(6 + t, h[:, t, :], [banks[4 + 2 * t + q][:, :] for q in range(2)], last_gb)


_INS = ["x", "mem", "w_in", "diff_lambda_q1", "diff_lambda_k1", "diff_lambda_q2", "diff_lambda_k2", "diff_subln_g",
        "w_mix_out", "ln1_g", "ln1_b", "mem_ln_g", "mem_ln_b", "w_mem_q", "w_mem_kv", "w_mem_o", "ln2_g", "ln2_b",
        "w_router", "b_router", "w_mlp1", "b_mlp1", "w_mlp2", "b_mlp2", "ln3_g", "ln3_b"]


def kernel(**inputs):
    import concourse.bacc as _bacc
    from concourse.bass_utils import run_bass_kernel_spmd as _run

    nc = _bacc.Bacc("TRN2", target_bir_lowering=False, num_devices=1)
    arrays, args = {}, {}
    for name in _INS:
        x = np.ascontiguousarray(inputs[name])
        arrays[f"in_{name}"] = x
        args[name] = nc.dram_tensor(f"in_{name}", x.shape, mybir.dt.from_np(x.dtype), kind="ExternalInput").ap()
    c = shape_constants()
    arrays["in_const"] = c
    args["const"] = nc.dram_tensor("in_const", c.shape, F32, kind="ExternalInput").ap()
    args["out"] = nc.dram_tensor("out", (1, S, D), F32, kind="ExternalOutput").ap()
    decoder_layer(nc, args)
    return _run(nc, [arrays], core_ids=[0]).results[0]["out"]
```
